# Optimizing a Trainium2 kernel written in Bass

```python
import math
import jax, jax.numpy as jnp
from jax import lax
import numpy as np

D_MODEL = 1024
BATCH = 1
SEQ = 256
DEPTH = 2

ROPE_THETA = 10000.0
EPS = 1e-6
LN_EPS = 1e-5
MLA_H = 8
MLA_NOPE = 64
MLA_ROPE = 32
MLA_V = 64
Q_LORA = 256
KV_LORA = 128
ATTN_BLOCK = 128
GDN_H = 4
GDN_DK = 128
GDN_DV = 128
CONV_W = 4
GDN_CHUNK = 64
ML_H = 4
ML_DK = 64
ML_DV = 128
ML_CHUNK = 64
SWA_H = 8
SWA_KV = 2
SWA_D = 64
WINDOW = 128
N_EXPERTS = 64
N_GROUPS = 8
TOPK_GROUPS = 4
TOP_K = 8
D_EXPERT = 256
D_SHARED = 256
ROUTED_SCALE = 2.5
DISPATCH_BLOCK = 128
DN_ALPHA = (2 * DEPTH) ** 0.25
DN_BETA = (8 * DEPTH) ** -0.25

EV_SIZES = (Q_LORA, KV_LORA + MLA_ROPE, GDN_H * GDN_DK, GDN_H * GDN_DK, GDN_H * GDN_DV, GDN_H, GDN_H, GDN_H * GDN_DV)
OD_SIZES = (ML_H * ML_DK, ML_H * ML_DK, ML_H * ML_DV, ML_H, ML_H, ML_H * ML_DV, SWA_H * SWA_D, SWA_KV * SWA_D, SWA_KV * SWA_D)
EV_IN = sum(EV_SIZES)
OD_IN = sum(OD_SIZES)
EV_MIX = MLA_H * MLA_V + GDN_H * GDN_DV
OD_MIX = ML_H * ML_DV + SWA_H * SWA_D

kernel_name = "hybrid_mla_gdn_mlstm_swa_moe_deepnorm"

def split_cols(t, sizes):
    return jnp.split(t, np.cumsum(sizes)[:-1].tolist(), axis=-1)

def rms_norm(t, g):
    tf = t.astype(jnp.float32)
    y = tf * lax.rsqrt(jnp.mean(tf * tf, -1, keepdims=True) + EPS)
    return (y * g.astype(jnp.float32)).astype(t.dtype)

def layer_norm(t, g, b):
    tf = t.astype(jnp.float32)
    mu = jnp.mean(tf, -1, keepdims=True)
    var = jnp.mean(jnp.square(tf - mu), -1, keepdims=True)
    y = (tf - mu) * lax.rsqrt(var + LN_EPS) * g.astype(jnp.float32) + b.astype(jnp.float32)
    return y.astype(t.dtype)

def l2_normalize(t):
    tf = t.astype(jnp.float32)
    return tf * lax.rsqrt(jnp.sum(tf * tf, -1, keepdims=True) + EPS)

def rope_tables(positions, dim):
    inv_freq = ROPE_THETA ** (-(jnp.arange(0, dim, 2, dtype=jnp.float32) / dim))
    ang = positions.astype(jnp.float32)[..., None] * inv_freq
    return jnp.cos(ang), jnp.sin(ang)

def apply_rope(t, cos, sin):
    shape = cos.shape[:2] + (1,) * (t.ndim - 3) + cos.shape[2:]
    c, s = cos.reshape(shape), sin.reshape(shape)
    tf = t.astype(jnp.float32)
    half = t.shape[-1] // 2
    t1, t2 = tf[..., :half], tf[..., half:]
    return jnp.concatenate([t1 * c - t2 * s, t2 * c + t1 * s], -1).astype(t.dtype)

def causal_dwconv(t, w):
    width, ch = w.shape
    return lax.conv_general_dilated(t, w[:, None, :].astype(t.dtype), window_strides=(1,),
                                    padding=[(width - 1, 0)], dimension_numbers=('NWC', 'WIO', 'NWC'),
                                    feature_group_count=ch)

def to_chunks(t, c):
    b, s, h = t.shape[:3]
    t = t.astype(jnp.float32).reshape((b, s // c, c, h) + t.shape[3:])
    return jnp.moveaxis(t, (1, 3), (0, 2))

def from_chunks(o):
    n, b, h, c, d = o.shape
    return jnp.moveaxis(o, (0, 2), (1, 3)).reshape(b, n * c, h, d)

def mla_attention(q_nope, q_rope, k_nope, k_rope, v):
    b, s, h, _ = q_nope.shape
    nb = s // ATTN_BLOCK
    scale = (MLA_NOPE + MLA_ROPE) ** -0.5
    kpos = jnp.arange(s)

    def blocks(t):
        return jnp.moveaxis(t.reshape((b, nb, ATTN_BLOCK) + t.shape[2:]), 1, 0)

    def one_block(args):
        qn, qr, n = args
        sc = jnp.einsum('bqhd,bkhd->bhqk', qn, k_nope) + jnp.einsum('bqhd,bkd->bhqk', qr, k_rope)
        sc = sc.astype(jnp.float32) * scale
        qpos = n * ATTN_BLOCK + jnp.arange(ATTN_BLOCK)
        sc = jnp.where(qpos[:, None] >= kpos[None, :], sc, -jnp.inf)
        p = jax.nn.softmax(sc, -1).astype(v.dtype)
        return jnp.einsum('bhqk,bkhd->bqhd', p, v)

    o = lax.map(one_block, (blocks(q_nope), blocks(q_rope), jnp.arange(nb)))
    return jnp.moveaxis(o, 0, 1).reshape(b, s, h * MLA_V)

def gated_delta_rule(q, k, v, beta, g):
    b, s, h, dk = q.shape
    dv = v.shape[-1]
    c = GDN_CHUNK
    q = to_chunks(q, c) * dk ** -0.5
    k, v, beta = to_chunks(k, c), to_chunks(v, c), to_chunks(beta, c)
    g = jnp.cumsum(to_chunks(g, c), -1)
    incl = jnp.tril(jnp.ones((c, c), bool))
    strict = jnp.tril(jnp.ones((c, c), bool), -1)
    decay = jnp.exp(jnp.where(incl, g[..., :, None] - g[..., None, :], -jnp.inf))
    kb = k * beta[..., None]
    lower = jnp.where(strict, jnp.einsum('nbhcd,nbhsd->nbhcs', kb, k) * decay, 0.0)
    eye = jnp.eye(c, dtype=jnp.float32)
    a = eye + lower
    t_inv = lax.linalg.triangular_solve(a, jnp.broadcast_to(eye, a.shape), left_side=True,
                                        lower=True, unit_diagonal=True)
    u = t_inv @ (v * beta[..., None])
    w = t_inv @ (kb * jnp.exp(g)[..., None])
    attn = jnp.einsum('nbhcd,nbhsd->nbhcs', q, k) * decay
    qg = q * jnp.exp(g)[..., None]
    kg = k * jnp.exp(g[..., -1:] - g)[..., None]
    glast = jnp.exp(g[..., -1])

    def step(state, inp):
        qg_c, kg_c, u_c, w_c, a_c, gl = inp
        v_new = u_c - w_c @ state
        o = qg_c @ state + a_c @ v_new
        state = state * gl[..., None, None] + jnp.einsum('bhcd,bhce->bhde', kg_c, v_new)
        return state, o

    _, o = lax.scan(step, jnp.zeros((b, h, dk, dv), jnp.float32), (qg, kg, u, w, attn, glast))
    return from_chunks(o)

def mlstm_chunked(q, k, v, i_pre, logf):
    b, s, h, dk = q.shape
    dv = v.shape[-1]
    c = ML_CHUNK
    incl = jnp.tril(jnp.ones((c, c), bool))
    xs = (to_chunks(q, c), to_chunks(k, c), to_chunks(v, c), to_chunks(i_pre, c), to_chunks(logf, c))

    def step(carry, inp):
        c_st, n_st, m_st = carry
        q_c, k_c, v_c, i_c, lf_c = inp
        bcum = jnp.cumsum(lf_c, -1)
        d = jnp.where(incl, bcum[..., :, None] - bcum[..., None, :] + i_c[..., None, :], -jnp.inf)
        inter = bcum + m_st[..., None]
        m_t = jnp.maximum(inter, jnp.max(d, -1))
        w_inter = jnp.exp(inter - m_t)
        p = jnp.exp(d - m_t[..., None]) * jnp.einsum('bhtd,bhsd->bhts', q_c, k_c)
        num = w_inter[..., None] * jnp.einsum('bhtd,bhde->bhte', q_c, c_st) + p @ v_c
        den = w_inter * jnp.einsum('bhtd,bhd->bht', q_c, n_st) + jnp.sum(p, -1)
        h_c = num / jnp.maximum(jnp.abs(den), jnp.exp(-m_t))[..., None]
        b_end = bcum[..., -1]
        a = b_end[..., None] - bcum + i_c
        m_new = jnp.maximum(b_end + m_st, jnp.max(a, -1))
        s_a = jnp.exp(a - m_new[..., None])
        keep = jnp.exp(b_end + m_st - m_new)
        c_st = keep[..., None, None] * c_st + jnp.einsum('bhsd,bhse->bhde', k_c * s_a[..., None], v_c)
        n_st = keep[..., None] * n_st + jnp.einsum('bhsd,bhs->bhd', k_c, s_a)
        return (c_st, n_st, m_new), h_c

    init = (jnp.zeros((b, h, dk, dv), jnp.float32), jnp.zeros((b, h, dk), jnp.float32),
            jnp.zeros((b, h), jnp.float32))
    _, o = lax.scan(step, init, xs)
    return from_chunks(o)

def swa_with_sinks(q, k, v, sinks):
    b, s, hq, d = q.shape
    grp = hq // SWA_KV
    nb = s // WINDOW
    qb = q.reshape(b, nb, WINDOW, SWA_KV, grp, d)

    def band(t):
        tb = t.reshape(b, nb, WINDOW, SWA_KV, d)
        prev = jnp.pad(tb, ((0, 0), (1, 0), (0, 0), (0, 0), (0, 0)))[:, :-1]
        return jnp.concatenate([prev, tb], axis=2)

    kb, vb = band(k), band(v)
    sc = jnp.einsum('bnqhgd,bnkhd->bnhgqk', qb, kb).astype(jnp.float32) * d ** -0.5
    qi = jnp.arange(WINDOW)[:, None]
    kj = jnp.arange(2 * WINDOW)[None, :]
    rel = qi + WINDOW - kj
    in_band = (rel >= 0) & (rel < WINDOW)
    exists = (jnp.arange(nb)[:, None, None] > 0) | (kj >= WINDOW)[None]
    mask = in_band[None] & exists
    sc = jnp.where(mask[None, :, None, None], sc, -jnp.inf)
    sink = jnp.broadcast_to(sinks.astype(jnp.float32).reshape(1, 1, SWA_KV, grp, 1, 1), sc.shape[:-1] + (1,))
    p = jax.nn.softmax(jnp.concatenate([sc, sink], -1), -1)[..., :-1].astype(v.dtype)
    o = jnp.einsum('bnhgqk,bnkhd->bnqhgd', p, vb)
    return o.reshape(b, s, hq * d)

def even_mixer(x, cos_m, sin_m, w_in, q_norm, w_qb, kv_norm, w_kvb, conv_w, a_log, dt_bias, o_norm, w_out):
    b, s, _ = x.shape
    c_q, kv_a, gq, gk, gv, g_beta, g_decay, z = split_cols(x @ w_in, EV_SIZES)
    q = (rms_norm(c_q, q_norm) @ w_qb).reshape(b, s, MLA_H, MLA_NOPE + MLA_ROPE)
    q_nope, q_rope = q[..., :MLA_NOPE], apply_rope(q[..., MLA_NOPE:], cos_m, sin_m)
    c_kv, k_rope = kv_a[..., :KV_LORA], apply_rope(kv_a[..., KV_LORA:], cos_m, sin_m)
    kv = (rms_norm(c_kv, kv_norm) @ w_kvb).reshape(b, s, MLA_H, MLA_NOPE + MLA_V)
    o_a = mla_attention(q_nope, q_rope, kv[..., :MLA_NOPE], k_rope, kv[..., MLA_NOPE:])
    qkv = jax.nn.silu(causal_dwconv(jnp.concatenate([gq, gk, gv], -1), conv_w))
    gq, gk, gv = split_cols(qkv, (GDN_H * GDN_DK, GDN_H * GDN_DK, GDN_H * GDN_DV))
    gq = l2_normalize(gq.reshape(b, s, GDN_H, GDN_DK))
    gk = l2_normalize(gk.reshape(b, s, GDN_H, GDN_DK))
    gv = gv.reshape(b, s, GDN_H, GDN_DV)
    beta = jax.nn.sigmoid(g_beta.astype(jnp.float32))
    g = -jnp.exp(a_log.astype(jnp.float32)) * jax.nn.softplus(g_decay.astype(jnp.float32) + dt_bias.astype(jnp.float32))
    o_b = gated_delta_rule(gq, gk, gv, beta, g)
    o_b = rms_norm(o_b, o_norm) * jax.nn.silu(z.reshape(b, s, GDN_H, GDN_DV).astype(jnp.float32))
    o_b = o_b.reshape(b, s, GDN_H * GDN_DV).astype(x.dtype)
    return jnp.concatenate([o_a, o_b], -1) @ w_out

def odd_mixer(x, cos_s, sin_s, w_in, b_i, b_f, ml_norm, sinks, w_out):
    b, s, _ = x.shape
    mq, mk, mv, mi, mf, mo, sq, sk, sv = split_cols(x @ w_in, OD_SIZES)
    i_pre = mi.astype(jnp.float32) + b_i.astype(jnp.float32)
    logf = jax.nn.log_sigmoid(mf.astype(jnp.float32) + b_f.astype(jnp.float32))
    h = mlstm_chunked(mq.reshape(b, s, ML_H, ML_DK), mk.reshape(b, s, ML_H, ML_DK) * ML_DK ** -0.5,
                      mv.reshape(b, s, ML_H, ML_DV), i_pre, logf)
    h = rms_norm(h, ml_norm.reshape(ML_H, ML_DV)) * jax.nn.sigmoid(mo.reshape(b, s, ML_H, ML_DV).astype(jnp.float32))
    o_c = h.reshape(b, s, ML_H * ML_DV).astype(x.dtype)
    q = apply_rope(sq.reshape(b, s, SWA_H, SWA_D), cos_s, sin_s)
    k = apply_rope(sk.reshape(b, s, SWA_KV, SWA_D), cos_s, sin_s)
    o_d = swa_with_sinks(q, k, sv.reshape(b, s, SWA_KV, SWA_D), sinks)
    return jnp.concatenate([o_c, o_d], -1) @ w_out

def moe_ffn(x, router_w, router_b, w_gate, w_up, w_down, s_gate, s_up, s_down):
    t, d = x.shape
    scores = jax.nn.sigmoid((x @ router_w).astype(jnp.float32))
    grouped = (scores + router_b.astype(jnp.float32)).reshape(t, N_GROUPS, N_EXPERTS // N_GROUPS)
    group_score = jnp.sum(lax.top_k(grouped, 2)[0], -1)
    _, top_groups = lax.top_k(group_score, TOPK_GROUPS)
    group_mask = jnp.any(top_groups[..., None] == jnp.arange(N_GROUPS), axis=1)
    masked = jnp.where(group_mask[..., None], grouped, -jnp.inf).reshape(t, N_EXPERTS)
    _, idx = lax.top_k(masked, TOP_K)
    gate = jnp.take_along_axis(scores, idx, -1)
    gate = gate / jnp.sum(gate, -1, keepdims=True) * ROUTED_SCALE
    n_assign = t * TOP_K
    flat_e = idx.reshape(-1)
    order = jnp.argsort(flat_e)
    e_sorted = flat_e[order]
    tok_sorted = (order // TOP_K).astype(jnp.int32)
    w_sorted = gate.reshape(-1)[order].astype(x.dtype)
    counts = jnp.bincount(flat_e, length=N_EXPERTS)
    padded = (counts + DISPATCH_BLOCK - 1) // DISPATCH_BLOCK * DISPATCH_BLOCK
    pad_end = jnp.cumsum(padded)
    pad_start = pad_end - padded
    start = jnp.cumsum(counts) - counts
    dest = pad_start[e_sorted] + jnp.arange(n_assign) - start[e_sorted]
    n_blocks = -(-n_assign // DISPATCH_BLOCK) + N_EXPERTS
    rows = n_blocks * DISPATCH_BLOCK
    row_tok = jnp.zeros((rows,), jnp.int32).at[dest].set(tok_sorted)
    row_w = jnp.zeros((rows,), x.dtype).at[dest].set(w_sorted)
    block_e = jnp.minimum(jnp.searchsorted(pad_end, jnp.arange(n_blocks) * DISPATCH_BLOCK, side='right'), N_EXPERTS - 1)

    def body(y, blk):
        tok, wt, e = blk
        xb = x[tok]
        hb = jax.nn.silu(xb @ w_gate[e]) * (xb @ w_up[e])
        return y.at[tok].add((hb @ w_down[e]) * wt[:, None]), None

    y, _ = lax.scan(body, jnp.zeros_like(x), (row_tok.reshape(n_blocks, DISPATCH_BLOCK),
                                              row_w.reshape(n_blocks, DISPATCH_BLOCK), block_e))
    shared = (jax.nn.silu(x @ s_gate) * (x @ s_up)) @ s_down
    return y + shared

def setup_inputs(seed: int = 0) -> dict:
    key = jax.random.key(seed)
    keys = iter(jax.random.split(key, 40))
    ne, no = (DEPTH + 1) // 2, DEPTH // 2

    def nrm(shape, scale):
        return jax.random.normal(next(keys), shape, jnp.float32) * scale

    def gain(shape):
        return 1.0 + nrm(shape, 0.02)

    x = nrm((BATCH, SEQ, D_MODEL), 1.0)
    positions = jax.random.randint(next(keys), (BATCH, 1), 0, 4096, dtype=jnp.int32) + jnp.arange(SEQ, dtype=jnp.int32)[None, :]
    u = jax.random.uniform(next(keys), (ne, GDN_H), jnp.float32)
    dt = jnp.exp(u * (math.log(0.1) - math.log(0.001)) + math.log(0.001))
    return {
        'x': x,
        'positions': positions,
        'ev_w_in': nrm((ne, D_MODEL, EV_IN), D_MODEL ** -0.5),
        'mla_q_norm': gain((ne, Q_LORA)),
        'mla_w_qb': nrm((ne, Q_LORA, MLA_H * (MLA_NOPE + MLA_ROPE)), Q_LORA ** -0.5),
        'mla_kv_norm': gain((ne, KV_LORA)),
        'mla_w_kvb': nrm((ne, KV_LORA, MLA_H * (MLA_NOPE + MLA_V)), KV_LORA ** -0.5),
        'gdn_conv': nrm((ne, CONV_W, GDN_H * (2 * GDN_DK + GDN_DV)), CONV_W ** -0.5),
        'gdn_a_log': jnp.log(jax.random.uniform(next(keys), (ne, GDN_H), jnp.float32, 1.0, 16.0)),
        'gdn_dt_bias': dt + jnp.log(-jnp.expm1(-dt)),
        'gdn_norm': gain((ne, GDN_DV)),
        'ev_w_out': nrm((ne, EV_MIX, D_MODEL), EV_MIX ** -0.5 * DN_BETA),
        'od_w_in': nrm((no, D_MODEL, OD_IN), D_MODEL ** -0.5),
        'mlstm_b_i': nrm((no, ML_H), 0.1) - 1.0,
        'mlstm_b_f': jnp.linspace(3.0, 6.0, ML_H, dtype=jnp.float32)[None, :] + nrm((no, ML_H), 0.1),
        'mlstm_norm': gain((no, ML_H * ML_DV)),
        'swa_sinks': nrm((no, SWA_H), 0.5),
        'od_w_out': nrm((no, OD_MIX, D_MODEL), OD_MIX ** -0.5 * DN_BETA),
        'ln1_g': gain((DEPTH, D_MODEL)),
        'ln1_b': nrm((DEPTH, D_MODEL), 0.02),
        'router_w': nrm((DEPTH, D_MODEL, N_EXPERTS), D_MODEL ** -0.5),
        'router_b': nrm((DEPTH, N_EXPERTS), 0.01),
        'moe_w_gate': nrm((DEPTH, N_EXPERTS, D_MODEL, D_EXPERT), D_MODEL ** -0.5),
        'moe_w_up': nrm((DEPTH, N_EXPERTS, D_MODEL, D_EXPERT), D_MODEL ** -0.5),
        'moe_w_down': nrm((DEPTH, N_EXPERTS, D_EXPERT, D_MODEL), D_EXPERT ** -0.5 * DN_BETA),
        'shared_w_gate': nrm((DEPTH, D_MODEL, D_SHARED), D_MODEL ** -0.5),
        'shared_w_up': nrm((DEPTH, D_MODEL, D_SHARED), D_MODEL ** -0.5),
        'shared_w_down': nrm((DEPTH, D_SHARED, D_MODEL), D_SHARED ** -0.5 * DN_BETA),
        'ln2_g': gain((DEPTH, D_MODEL)),
        'ln2_b': nrm((DEPTH, D_MODEL), 0.02),
    }

def reference(x, positions, ev_w_in, mla_q_norm, mla_w_qb, mla_kv_norm, mla_w_kvb, gdn_conv, gdn_a_log,
              gdn_dt_bias, gdn_norm, ev_w_out, od_w_in, mlstm_b_i, mlstm_b_f, mlstm_norm, swa_sinks, od_w_out,
              ln1_g, ln1_b, router_w, router_b, moe_w_gate, moe_w_up, moe_w_down, shared_w_gate, shared_w_up,
              shared_w_down, ln2_g, ln2_b):
    b, s, d = x.shape
    cos_m, sin_m = rope_tables(positions, MLA_ROPE)
    cos_s, sin_s = rope_tables(positions, SWA_D)
    for layer in range(DEPTH):
        j = layer // 2
        if layer % 2 == 0:
            mix = even_mixer(x, cos_m, sin_m, ev_w_in[j], mla_q_norm[j], mla_w_qb[j], mla_kv_norm[j], mla_w_kvb[j],
                             gdn_conv[j], gdn_a_log[j], gdn_dt_bias[j], gdn_norm[j], ev_w_out[j])
        else:
            mix = odd_mixer(x, cos_s, sin_s, od_w_in[j], mlstm_b_i[j], mlstm_b_f[j], mlstm_norm[j], swa_sinks[j], od_w_out[j])
        x = layer_norm(DN_ALPHA * x + mix, ln1_g[layer], ln1_b[layer])
        ff = moe_ffn(x.reshape(b * s, d), router_w[layer], router_b[layer], moe_w_gate[layer], moe_w_up[layer],
                     moe_w_down[layer], shared_w_gate[layer], shared_w_up[layer], shared_w_down[layer])
        x = layer_norm(DN_ALPHA * x + ff.reshape(b, s, d), ln2_g[layer], ln2_b[layer])
    return x


_drawn_inputs = setup_inputs


def setup_inputs(seed=0):
    import zlib

    import numpy as np

    out = dict(_drawn_inputs(seed))
    spreads = {}
    factors = {'mla_q_norm': 5.285,
     'mla_kv_norm': 4.018,
     'gdn_norm': 3.241,
     'mlstm_b_i': 8.0,
     'mlstm_norm': 4.78,
     'swa_sinks': 8.0}
    for name, (base, spread) in spreads.items():
        noise = np.random.default_rng([zlib.crc32(name.encode()), seed]).standard_normal(out[name].shape)
        drawn = base * np.exp(spread * noise) if base else spread * noise
        out[name] = __import__('jax').numpy.asarray(drawn.astype(out[name].dtype))
    for name, factor in factors.items():
        out[name] = (out[name] * factor).astype(out[name].dtype)
    return out
```

```python
from contextlib import ExitStack

import numpy as np
import concourse.bass as bass
from concourse import mybir

F32 = mybir.dt.float32
BF16 = mybir.dt.bfloat16
I32 = mybir.dt.int32
ALU = mybir.AluOpType
ACT = mybir.ActivationFunctionType
AX = mybir.AxisListType

P = 128
D = 1024
S = 256
NT = S // P
KD = D // P
BANK = 512

N_EXP = 64
GROUPS = 8
GROUP = N_EXP // GROUPS
TOP_GROUPS = 4
TOP_K = 8
FE = 256
KF = FE // P
SLOTS = 64
PAIRS = N_EXP // 2
MAX_OVER = 32
ROUTED_SCALE = 2.5
ALPHA = float(4 ** 0.25)
LN_EPS = 1e-5
RMS_EPS = 1e-6
NEG = -1e30
OFF_GROUP = -3.0e38
TAKEN = -3.3e38

MLA_H, MLA_N, MLA_R, MLA_V = 8, 64, 32, 64
MLA_QK = MLA_N + MLA_R
Q_LORA, KV_LORA = 256, 128
GH, GD = 4, 128
CONV_W = 4
LH, LK, LV = 4, 64, 128
WH, WKV, WD = 8, 2, 64
ROPE_THETA = 10000.0


def named(**parts):
    return type("Parts", (), parts)


def semaphores(ctx, nc, prefix, names):
    made = {n: nc.alloc_semaphore(f"{prefix}_{n}") for n in names.split()}

    def clear():
        nc.clear_and_free_semaphores(list(made.values()))
        nc.all_engine_barrier()

    ctx.callback(clear)
    return named(**made)


class Chain:

    def __init__(self, eng, sem):
        self.eng, self.sem, self.n = eng, sem, 0

    def __call__(self, instruction):
        self.n += 1
        instruction.then_inc(self.sem, 1)
        self.eng.wait_ge(self.sem, self.n)


def over(ap, axis, n):
    v = ap.unsqueeze(axis)
    shape = list(v.shape)
    shape[axis] = n
    return v.to_broadcast(shape)


def persistent(ctx, nc):
    def sb(name, shape, dt=F32):
        return ctx.enter_context(nc.sbuf_tensor(name, shape, dt))

    k = named()
    k.x = sb("x_tokens", [P, NT, D])
    k.xT = sb("x_transposed", [P, KD, S])
    k.w_up = [sb(f"w_up_ring{i}", [P, 2, KD, FE]) for i in range(4)]
    k.w_down = [sb(f"w_down_ring{i}", [P, KF, D]) for i in range(4)]
    k.ln = sb("ln_gain_bias", [P, 2, D])
    k.mixT = sb("mixed_transposed", [P, KD, S])
    k.cos = sb("rope_cos", [P, NT, MLA_R // 2 + WD // 2])
    k.sin = sb("rope_sin", [P, NT, MLA_R // 2 + WD // 2])
    k.upto = sb("upto", [P, P])
    k.no_later = sb("no_later", [P, 2 * P])
    k.no_later_T = sb("no_later_T", [P, P])
    k.off_strict = sb("off_strict", [P, P])
    k.block8 = sb("block8", [P, P])
    k.eps = sb("epsilons", [P, 2])
    k.router_w = sb("router_w_sb", [P, KD, N_EXP])
    k.router_b = sb("router_b_sb", [P, N_EXP])
    k.ident = sb("identity", [P, P])
    k.ones = sb("ones", [P, P])
    k.ones_bf = sb("ones_bf", [P, P], BF16)
    k.before_bf = sb("before_bf", [P, P], BF16)
    k.slot_no = sb("slot_no", [P, SLOTS])
    k.earlier8 = sb("earlier8", [P, GROUPS, GROUPS])
    k.pass_no = sb("pass_no", [MAX_OVER, 1])
    k.psum = ctx.enter_context(nc.psum_tensor("psum", [P, 8, BANK], F32))
    k.over_dram = nc.dram_tensor("overflow_table", [MAX_OVER, 4], I32, kind="Internal").ap()
    return k


def constants(nc, k):
    ctx = ExitStack()
    s = semaphores(ctx, nc, "const", "pool zeros")
    with nc.Block(no_gpsimd_drain=True) as block:
        @block.vector
        def _(dve):
            nc.vector.memset(k.ident[:], 0.0)
            nc.vector.memset(k.ones[:], 1.0)
            nc.vector.memset(k.ones_bf[:], 1.0)
            nc.vector.memset(k.no_later[:], 0.0)
            nc.vector.memset(k.no_later_T[:], 0.0)
            nc.vector.memset(k.off_strict[:], 0.0)
            nc.vector.memset(k.block8[:], 1.0)
            nc.vector.memset(k.eps[:, 0:1], RMS_EPS)
            nc.vector.memset(k.eps[:, 1:2], float(np.pi / 2))
            nc.vector.memset(k.earlier8[:], 1.0).then_inc(s.zeros, 1)

        @block.gpsimd
        def _(pool):
            step = Chain(pool, s.pool)
            step(nc.gpsimd.iota(k.slot_no[:], [[1, SLOTS]], base=1, channel_multiplier=0,
                                allow_small_or_imprecise_dtypes=True))
            step(nc.gpsimd.iota(k.pass_no[:], [[1, 1]], base=0, channel_multiplier=1,
                                allow_small_or_imprecise_dtypes=True))
            pool.wait_ge(s.zeros, 1)
            step(nc.gpsimd.affine_select(out=k.ident[:], in_=k.ident[:], pattern=[[-1, P]],
                                         compare_op=ALU.not_equal, fill=1.0, base=0, channel_multiplier=1))
            step(nc.gpsimd.affine_select(out=k.before_bf[:], in_=k.ones_bf[:], pattern=[[1, P]],
                                         compare_op=ALU.is_gt, fill=0.0, base=0, channel_multiplier=-1))
            step(nc.gpsimd.affine_select(out=k.earlier8[:], in_=k.earlier8[:], pattern=[[1, GROUPS], [-1, GROUPS]],
                                         compare_op=ALU.is_gt, fill=0.0, base=0, channel_multiplier=0))
            step(nc.gpsimd.affine_select(out=k.upto[:], in_=k.ones[:], pattern=[[1, P]],
                                         compare_op=ALU.is_ge, fill=0.0, base=0, channel_multiplier=-1))
            step(nc.gpsimd.affine_select(out=k.no_later[:, P:2 * P], in_=k.no_later[:, P:2 * P], pattern=[[-1, P]],
                                         compare_op=ALU.is_ge, fill=NEG, base=0, channel_multiplier=1))
            step(nc.gpsimd.affine_select(out=k.no_later_T[:], in_=k.no_later_T[:], pattern=[[1, P]],
                                         compare_op=ALU.is_ge, fill=NEG, base=0, channel_multiplier=-1))
            step(nc.gpsimd.affine_select(out=k.off_strict[:], in_=k.off_strict[:], pattern=[[-1, P]],
                                         compare_op=ALU.is_gt, fill=-NEG, base=0, channel_multiplier=1))
            step(nc.gpsimd.affine_select(out=k.block8[:], in_=k.block8[:], pattern=[[-8, P // 8], [0, 8]],
                                         compare_op=ALU.is_ge, fill=0.0, base=0, channel_multiplier=1))
            step(nc.gpsimd.affine_select(out=k.block8[:], in_=k.block8[:], pattern=[[8, P // 8], [0, 8]],
                                         compare_op=ALU.is_ge, fill=0.0, base=7, channel_multiplier=-1))
    ctx.close()



def layer_norm_vector(nc, dve, step, s, k, w, mix_ready):
    for t in range(NT):
        dve.wait_ge(mix_ready, t + 1)
        for half in range(2):
            cols = slice(half * BANK, (half + 1) * BANK)
            step(nc.vector.scalar_tensor_tensor(w.resid[:, t, cols], k.x[:, t, cols], ALPHA,
                                                k.psum[:, 2 * t + half, :], ALU.mult, ALU.add))
            step(nc.vector.bn_stats(w.bn[:, t, half, :], w.resid[:, t, cols]))
        nc.vector.bn_aggr(w.meanvar[:, t, :], w.bn[:, t, :, :]).then_inc(s.variance, 1)
    for t in range(NT):
        dve.wait_ge(s.root, t + 1)
        step(nc.vector.reciprocal(w.rstd[:, t:t + 1], w.root[:, t:t + 1]))
        step(nc.vector.tensor_scalar(w.resid[:, t, :], w.resid[:, t, :], w.meanvar[:, t, 0:1],
                                     w.rstd[:, t:t + 1], ALU.subtract, ALU.mult))
        step(nc.vector.tensor_tensor(w.resid[:, t, :], w.resid[:, t, :], k.ln[:, 0, :], ALU.mult))
        step(nc.vector.tensor_tensor(k.x[:, t, :], w.resid[:, t, :], k.ln[:, 1, :], ALU.add))
        nc.vector.engine_nop().then_inc(s.normed, 1)


def layer_norm_scalar(nc, act, s, w):
    for t in range(NT):
        act.wait_ge(s.variance, t + 1)
        nc.scalar.activation(w.root[:, t:t + 1], w.meanvar[:, t, 1:2], ACT.Sqrt,
                             bias=w.ln_eps[:, 0:1]).then_inc(s.root, 1)


def layer_norm_tiles(sb):
    return dict(resid=sb("resid", [P, NT, D]), bn=sb("bn", [P, NT, 2, 6]), meanvar=sb("meanvar", [P, NT, 2]),
                root=sb("root", [P, NT]), rstd=sb("rstd", [P, NT]), ln_eps=sb("ln_eps", [P, 1]))



def transpose_x_tensor(nc, pe, s, k):
    for b in range(KD // 2):
        for c in range(2):
            for t in range(NT):
                last = nc.tensor.transpose(k.psum[:, b, c * S + t * P:c * S + (t + 1) * P],
                                           k.x[:, t, 2 * b + c:D:KD], k.ident[:])
        last.then_inc(s.xT_psum, 1)


def transpose_x_scalar(nc, act, s, k):
    for b in range(KD // 2):
        act.wait_ge(s.xT_psum, b + 1)
        nc.scalar.copy(k.xT[:, 2 * b:2 * b + 2, :].rearrange("p c t -> p (c t)"),
                       k.psum[:, b, :]).then_inc(s.xT, 1)



def moe_layer(nc, k, d, layer, out=None, fetch_next=None):
    ctx = ExitStack()
    names = ("tables shared_w xT_psum xT dve pool parts logits scores selected places routed table_sb table_dram "
             "table_back shared_up shared_h shared_silu shared_hT_psum shared_hT shared_down "
             "gu0 gu1 dn0 dn1 match gated silu h up gather_a gather_b xsel_a xsel_b turned turned_sb "
             "down_a down_b o_a o_b combined "
             "v_back v_load v_shifted v_match v_silu v_h v_up v_gather v_xsel_a v_xsel_b v_turned v_turned_sb v_down v_o_a v_o_b "
             "v_combined y_ready variance root normed stored eps")
    s = semaphores(ctx, nc, f"moe{layer}", names)

    def sb(name, shape, dt=F32):
        return ctx.enter_context(nc.sbuf_tensor(f"moe{layer}_{name}", shape, dt))

    w = named(**layer_norm_tiles(sb))
    part = [sb(f"x_part{i}", [P, NT, D], BF16) for i in range(3)]
    rest = w.resid
    match = [sb(f"match{i}", [P, NT, 2, SLOTS], BF16) for i in range(2)]
    gated = [sb(f"gated{i}", [P, NT, 2, SLOTS]) for i in range(2)]
    xsel = sb("x_selected", [P, KD, P])
    silu = sb("silu", [P, FE])
    h = sb("h", [P, FE])
    turned = [sb(f"turned{i}", [P, KF * P + S]) for i in range(2)]
    o = sb("expert_out", [P, D])
    score = sb("score", [P, NT, N_EXP])
    biased = sb("biased", [P, NT, N_EXP])
    top8 = sb("top8", [P, NT * GROUPS, 8])
    gscore = sb("group_score", [P, NT, GROUPS])
    cmp_a = sb("cmp_a", [P, NT, GROUPS, GROUPS])
    cmp_b = sb("cmp_b", [P, NT, GROUPS, GROUPS])
    rank = sb("rank", [P, NT, GROUPS])
    gmask = sb("gmask", [P, NT, GROUPS])
    goff = sb("goff", [P, NT, GROUPS])
    best8 = sb("best8", [P, NT, 8])
    taken = sb("taken", [P, NT, N_EXP])
    sel = sb("sel", [P, NT, N_EXP])
    sel_bf = sb("sel_bf", [P, NT, N_EXP], BF16)
    gsum = sb("gsum", [P, NT])
    ginv = sb("ginv", [P, NT])
    gate = sb("gate", [P, NT, N_EXP])
    place = sb("place", [P, NT, N_EXP])
    sh = sb("shared_h", [P, NT, FE])
    ssilu = sb("shared_silu", [P, NT, FE])
    shT = sb("shared_hT", [P, NT, KF, P])
    c1 = sb("over_64", [MAX_OVER, N_EXP])
    c2 = sb("over_128", [MAX_OVER, N_EXP])
    c3 = sb("extra_before", [MAX_OVER, N_EXP])
    table = sb("table", [MAX_OVER, 4])
    table_i = sb("table_i", [MAX_OVER, 4], I32)
    back_i = sb("back_i", [P, MAX_OVER, 4], I32)
    back = sb("back", [P, MAX_OVER, 4])
    shifted = sb("shifted", [P, NT, 2])

    up_ps, turn_ps = k.psum[:, 6, :], k.psum[:, 7, :]

    def up_view(slot, kk):
        return k.w_up[slot][:, :, kk, :]

    def pe_up(slots):
        for kk in range(KD):
            for e in range(2):
                last = nc.tensor.matmul(k.psum[e * SLOTS:(e + 1) * SLOTS, 6, :], xsel[:, kk, e * SLOTS:(e + 1) * SLOTS],
                                        up_view(slots[e], kk), start=kk == 0, stop=kk == KD - 1)
        return last

    def pe_gather(bank, m):
        for c in range(4):
            kk = 4 * (bank - 4) + c
            for i in range(3):
                for t in range(NT):
                    last = nc.tensor.matmul(k.psum[:, bank, c * P:(c + 1) * P], part[i][:, t, kk:D:KD],
                                            m[:, t, :, :].rearrange("p e s -> p (e s)"),
                                            start=i == 0 and t == 0, stop=i == 2 and t == NT - 1)
        return last

    def pe_turn(g):
        for j in range(KF):
            nc.tensor.transpose(turn_ps[:, j * P:(j + 1) * P], h[:, j * P:(j + 1) * P], k.ident[:])
        for t in range(NT):
            last = nc.tensor.transpose(turn_ps[:, FE + t * P:FE + (t + 1) * P],
                                       g[:, t, :, :].rearrange("p e s -> p (e s)"), k.ident[:])
        return last

    def pe_combine(par):
        for t in range(NT):
            for half in range(2):
                last = nc.tensor.matmul(k.psum[:, 2 * t + half, :], turned[par][:, FE + t * P:FE + (t + 1) * P],
                                        o[:, half * BANK:(half + 1) * BANK], start=False, stop=True,
                                        skip_group_check=True)
        return last

    def pe_down(par, slots, half, bank):
        for j in range(KF):
            for e in range(2):
                last = nc.tensor.matmul(k.psum[e * SLOTS:(e + 1) * SLOTS, bank, :], turned[par][:, j * P + e * SLOTS:j * P + (e + 1) * SLOTS],
                                        k.w_down[slots[e]][:, j, half * BANK:(half + 1) * BANK],
                                        start=j == 0, stop=j == KF - 1)
        return last

    def flat(ap):
        return ap.rearrange("p a b -> p (a b)")

    def load_up(sp, slot, e, sem):
        sp.dma_start(k.w_up[slot][:, 0:1].rearrange("p a k f -> p a (k f)"),
                     d.w_gate[layer, bass.ds(e, 1)].rearrange("e (p k) f -> p e (k f)", k=KD)).then_inc(sem, 16)
        sp.dma_start(k.w_up[slot][:, 1:2].rearrange("p a k f -> p a (k f)"),
                     d.w_up[layer, bass.ds(e, 1)].rearrange("e (p k) f -> p e (k f)", k=KD)).then_inc(sem, 16)

    def load_down(sp, slot, e, sem):
        sp.dma_start(k.w_down[slot][:], d.w_down[layer, bass.ds(e, 1)].rearrange("e (j p) n -> p (e j) n", p=P)).then_inc(sem, 16)

    gu, dn = [s.gu0, s.gu1], [s.dn0, s.dn1]

    with nc.Block(no_gpsimd_drain=True) as block:
        @block.sync
        def _(sp):
            sp.dma_start(k.router_w[:], d.router_w[layer].rearrange("(p k) e -> p k e", k=KD)).then_inc(s.tables, 16)
            sp.dma_start(k.router_b[:], d.router_b[layer:layer + 1].to_broadcast([P, N_EXP])).then_inc(s.tables, 16)
            for i, src in enumerate((d.ln2_g, d.ln2_b)):
                sp.dma_start(k.ln[:, i, :], src[layer:layer + 1].to_broadcast([P, D])).then_inc(s.tables, 16)
            sp.dma_start(k.w_up[3][:, 0], d.s_gate[layer].rearrange("(p k) f -> p k f", k=KD)).then_inc(s.shared_w, 16)
            sp.dma_start(k.w_up[3][:, 1], d.s_up[layer].rearrange("(p k) f -> p k f", k=KD)).then_inc(s.shared_w, 16)
            sp.dma_start(k.w_down[3][:], d.s_down[layer].rearrange("(j p) n -> p j n", p=P)).then_inc(s.shared_w, 16)
            for e in range(3):
                load_up(sp, e, e, gu[e // 2])
            for e in range(3):
                load_down(sp, e, e, dn[e // 2])
            sp.wait_ge(s.shared_up, NT)
            load_up(sp, 3, 3, gu[1])
            sp.wait_ge(s.shared_down, NT)
            load_down(sp, 3, 3, dn[1])
            with sp.Fori(1, PAIRS // 2) as i:
                for par in range(2):
                    sp.wait_ge(s.up, 2 * i + par - 1)
                    for j in range(2):
                        load_up(sp, 2 * par + j, 4 * i + 2 * par + j, gu[par])
                    sp.wait_ge(s.down_b, 2 * i + par - 1)
                    for j in range(2):
                        load_down(sp, 2 * par + j, 4 * i + 2 * par + j, dn[par])
            sp.wait_ge(s.table_sb, 1)
            sp.dma_start(k.over_dram, table_i[:]).then_inc(s.table_dram, 16)
            sp.wait_ge(s.table_dram, 16)
            sp.dma_start(back_i[:].rearrange("p b c -> p (b c)"),
                         k.over_dram.rearrange("b c -> (b c)").unsqueeze(0).to_broadcast([P, MAX_OVER * 4])
                         ).then_inc(s.table_back, 16)
            sp.wait_ge(s.table_back, 16)
            n_over = sp.value_load(k.over_dram[0:1, 2:3], min_val=0, max_val=MAX_OVER)
            with sp.If(n_over > 0):
                sp.wait_ge(s.combined, PAIRS)
                with sp.Fori(0, (n_over + 1) // 2) as i:
                    experts = [sp.value_load(k.over_dram[bass.ds(2 * i + j, 1), 0:1], min_val=0,
                                             max_val=N_EXP - 1) for j in range(2)]
                    sp.wait_ge(s.v_combined, i + 1)
                    for j, e in enumerate(experts):
                        load_up(sp, j, e, s.v_load)
                        load_down(sp, j, e, s.v_load)
            if out is not None:
                for t in range(NT):
                    sp.wait_ge(s.normed, t + 1)
                    sp.dma_start(out[t * P:(t + 1) * P, :], k.x[:, t, :]).then_inc(s.stored, 16)
                sp.wait_ge(s.stored, 16 * NT)

        @block.tensor
        def _(pe):
            transpose_x_tensor(nc, pe, s, k)
            pe.wait_ge(s.tables, 16 * 4)
            pe.wait_ge(s.xT, KD // 2)
            for t in range(NT):
                for kk in range(KD):
                    last = nc.tensor.matmul(k.psum[:, 4, t * N_EXP:(t + 1) * N_EXP], k.xT[:, kk, t * P:(t + 1) * P],
                                            k.router_w[:, kk, :], start=kk == 0, stop=kk == KD - 1)
            last.then_inc(s.logits, 1)
            pe.wait_ge(s.shared_w, 16 * 3)
            for t in range(NT):
                for kk in range(KD):
                    last = nc.tensor.matmul(k.psum[:, 5 + t, :], k.xT[:, kk, t * P:(t + 1) * P], up_view(3, kk),
                                            start=kk == 0, stop=kk == KD - 1)
                last.then_inc(s.shared_up, 1)
            pe.wait_ge(s.selected, 1)
            for t in range(NT):
                nc.tensor.matmul(k.psum[:, 4, t * N_EXP:(t + 1) * N_EXP], k.before_bf[:], sel_bf[:, t, :],
                                 start=True, stop=t == 0)
                if t:
                    nc.tensor.matmul(k.psum[:, 4, t * N_EXP:(t + 1) * N_EXP], k.ones_bf[:], sel_bf[:, 0, :],
                                     start=False, stop=True)
            for t in range(NT):
                last = nc.tensor.matmul(k.psum[0:MAX_OVER, 4, 2 * N_EXP:3 * N_EXP], k.ones_bf[:, 0:MAX_OVER],
                                        sel_bf[:, t, :], start=t == 0, stop=t == NT - 1)
            last.then_inc(s.places, 1)
            for t in range(NT):
                pe.wait_ge(s.shared_h, t + 1)
                for j in range(KF):
                    last = nc.tensor.transpose(turn_ps[:, (t * KF + j) * P:(t * KF + j + 1) * P],
                                               sh[:, t, j * P:(j + 1) * P], k.ident[:])
            last.then_inc(s.shared_hT_psum, 1)
            pe.wait_ge(s.parts, 1)
            pe.wait_ge(s.routed, 1)
            pe.wait_ge(s.match, 1)
            pe_gather(4, match[0]).then_inc(s.gather_a, 1)
            pe_gather(5, match[0]).then_inc(s.gather_b, 1)
            pe.wait_ge(s.shared_hT, 1)
            for t in range(NT):
                for half in range(2):
                    for j in range(KF):
                        last = nc.tensor.matmul(k.psum[:, 2 * t + half, :], shT[:, t, j, :],
                                                k.w_down[3][:, j, half * BANK:(half + 1) * BANK],
                                                start=j == 0, stop=j == KF - 1)
                last.then_inc(s.shared_down, 1)

            def pair(p, turn, par, first=False, final=False):
                slots = (2 * par, 2 * par + 1)
                pe.wait_ge(s.xsel_a, p + 1)
                pe.wait_ge(s.xsel_b, p + 1)
                pe.wait_ge(gu[par], 64 * (turn + 1))
                if not first:
                    pe.wait_ge(s.h, p)
                pe_up(slots).then_inc(s.up, 1)
                if not final:
                    pe.wait_ge(s.match, p + 2)
                    if not first:
                        pe.wait_ge(s.o_a, p)
                    pe_gather(4, match[1 - par]).then_inc(s.gather_a, 1)
                    pe_gather(5, match[1 - par]).then_inc(s.gather_b, 1)
                pe.wait_ge(s.h, p + 1)
                pe.wait_ge(s.gated, p + 1)
                if not first:
                    pe.wait_ge(s.o_b, p)
                pe_turn(gated[par]).then_inc(s.turned, 1)
                if not first:
                    pe.wait_ge(s.o_a, p)
                    pe_combine(1 - par).then_inc(s.combined, 1)
                pe.wait_ge(s.turned_sb, p + 1)
                pe.wait_ge(dn[par], 32 * (turn + 1))
                if not final:
                    pe.wait_ge(s.xsel_a, p + 2)
                pe_down(par, slots, 0, 4).then_inc(s.down_a, 1)
                pe_down(par, slots, 1, 7).then_inc(s.down_b, 1)

            pair(0, 0, 0, first=True)
            pair(1, 0, 1)
            with pe.Fori(1, PAIRS // 2 - 1) as i:
                pair(2 * i, i, 0)
                pair(2 * i + 1, i, 1)
            pair(PAIRS - 2, PAIRS // 2 - 1, 0)
            pair(PAIRS - 1, PAIRS // 2 - 1, 1, final=True)
            pe.wait_ge(s.o_a, PAIRS)
            pe.wait_ge(s.o_b, PAIRS)
            pe_combine(1).then_inc(s.combined, 1)

            pe.wait_ge(s.table_back, 16)
            n_over = pe.value_load(k.over_dram[0:1, 2:3], min_val=0, max_val=MAX_OVER)
            with pe.If(n_over > 0):
                nc.tensor.transpose(k.psum[:, 6, 0:P], k.ident[:], k.ident[:]).then_inc(s.v_combined, 1)
                with pe.Fori(0, (n_over + 1) // 2) as i:
                    pe.wait_ge(s.v_match, 2 * i + 2)
                    pe_gather(4, match[0])
                    pe_gather(5, match[0]).then_inc(s.v_gather, 1)
                    pe.wait_ge(s.v_xsel_a, i + 1)
                    pe.wait_ge(s.v_xsel_b, i + 1)
                    pe.wait_ge(s.v_load, 96 * i + 96)
                    pe_up((0, 1)).then_inc(s.v_up, 1)
                    pe.wait_ge(s.v_h, i + 1)
                    pe_turn(gated[0]).then_inc(s.v_turned, 1)
                    pe.wait_ge(s.v_turned_sb, i + 1)
                    pe_down(0, (0, 1), 0, 4)
                    pe_down(0, (0, 1), 1, 7).then_inc(s.v_down, 1)
                    pe.wait_ge(s.v_o_a, i + 1)
                    pe.wait_ge(s.v_o_b, i + 1)
                    pe_combine(0).then_inc(s.v_combined, 1)
            nc.tensor.transpose(k.psum[:, 6, 0:P], k.ident[:], k.ident[:]).then_inc(s.y_ready, NT)

        @block.scalar
        def _(act):
            transpose_x_scalar(nc, act, s, k)
            act.wait_ge(s.logits, 1)
            nc.scalar.activation(flat(score[:]), k.psum[:, 4, 0:NT * N_EXP], ACT.Sigmoid).then_inc(s.scores, 1)
            for t in range(NT):
                act.wait_ge(s.shared_up, t + 1)
                nc.scalar.activation(ssilu[:, t, :], k.psum[:, 5 + t, 0:FE], ACT.Silu).then_inc(s.shared_silu, 1)
            act.wait_ge(s.gather_a, 1)
            nc.scalar.copy(flat(xsel[:, 0:4, :]), k.psum[:, 4, :]).then_inc(s.xsel_a, 1)

            def pair(p, par, final=False):
                act.wait_ge(s.up, p + 1)
                nc.scalar.activation(silu[:], up_ps[:, 0:FE], ACT.Silu).then_inc(s.silu, 1)
                if not final:
                    act.wait_ge(s.gather_a, p + 2)
                    nc.scalar.copy(flat(xsel[:, 0:4, :]), k.psum[:, 4, :]).then_inc(s.xsel_a, 1)
                act.wait_ge(s.turned, p + 1)
                nc.scalar.copy(turned[par][:], turn_ps).then_inc(s.turned_sb, 1)
                act.wait_ge(s.down_a, p + 1)
                nc.scalar.copy(o[:, 0:BANK], k.psum[:, 4, :]).then_inc(s.o_a, 1)

            with act.Fori(0, PAIRS // 2 - 1) as i:
                pair(2 * i, 0)
                pair(2 * i + 1, 1)
            pair(PAIRS - 2, 0)
            pair(PAIRS - 1, 1, final=True)

            act.wait_ge(s.table_back, 16)
            n_over = act.value_load(k.over_dram[0:1, 2:3], min_val=0, max_val=MAX_OVER)
            with act.If(n_over > 0):
                with act.Fori(0, (n_over + 1) // 2) as i:
                    act.wait_ge(s.v_gather, i + 1)
                    nc.scalar.copy(flat(xsel[:, 0:4, :]), k.psum[:, 4, :]).then_inc(s.v_xsel_a, 1)
                    act.wait_ge(s.v_up, i + 1)
                    nc.scalar.activation(silu[:], up_ps[:, 0:FE], ACT.Silu).then_inc(s.v_silu, 1)
                    act.wait_ge(s.v_turned, i + 1)
                    nc.scalar.copy(turned[0][:], turn_ps).then_inc(s.v_turned_sb, 1)
                    act.wait_ge(s.v_down, i + 1)
                    nc.scalar.copy(o[:, 0:BANK], k.psum[:, 4, :]).then_inc(s.v_o_a, 1)
            act.wait_ge(s.eps, 1)
            layer_norm_scalar(nc, act, s, w)

        @block.gpsimd
        def _(pool):
            def gated_matrix(p, par):
                pool.wait_ge(s.match, p + 1)
                nc.gpsimd.tensor_tensor(gated[par][:], match[par][:],
                                        over(gate[:, :, bass.ds(2 * p, 2)], 3, SLOTS), ALU.mult).then_inc(s.gated, 1)

            gated_matrix(0, 0)
            gated_matrix(1, 1)
            with pool.Fori(1, PAIRS // 2) as i:
                for par in range(2):
                    pool.wait_ge(s.turned, 2 * i + par - 1)
                    gated_matrix(2 * i + par, par)

        @block.vector
        def _(dve):
            step = Chain(dve, s.dve)
            nc.vector.memset(w.ln_eps[:], LN_EPS).then_inc(s.eps, 1)
            step(nc.vector.tensor_copy(part[0][:], k.x[:]))
            step(nc.vector.tensor_tensor(rest[:], k.x[:], part[0][:], ALU.subtract))
            step(nc.vector.tensor_copy(part[1][:], rest[:]))
            step(nc.vector.tensor_tensor(rest[:], rest[:], part[1][:], ALU.subtract))
            nc.vector.tensor_copy(part[2][:], rest[:]).then_inc(s.parts, 1)

            dve.wait_ge(s.scores, 1)
            dve.wait_ge(s.tables, 16 * 4)
            step(nc.vector.tensor_tensor(biased[:], score[:], over(k.router_b[:], 1, NT), ALU.add))
            for t in range(NT):
                for g in range(GROUPS):
                    last = nc.vector.max(top8[:, t * GROUPS + g, :], biased[:, t, g * GROUP:(g + 1) * GROUP])
            step(last)
            step(nc.vector.tensor_tensor(flat(gscore[:]), top8[:, :, 0], top8[:, :, 1], ALU.add))
            other, own = over(gscore[:], 2, GROUPS), over(gscore[:], 3, GROUPS)
            step(nc.vector.tensor_tensor(cmp_a[:], other, own, ALU.is_gt))
            step(nc.vector.tensor_tensor(cmp_b[:], other, own, ALU.is_equal))
            step(nc.vector.tensor_tensor(cmp_b[:], cmp_b[:], over(k.earlier8[:], 1, NT), ALU.mult))
            step(nc.vector.tensor_tensor(cmp_a[:], cmp_a[:], cmp_b[:], ALU.add))
            step(nc.vector.tensor_reduce(rank[:], cmp_a[:], AX.X, ALU.add))
            step(nc.vector.tensor_scalar(gmask[:], rank[:], TOP_GROUPS - 0.5, None, ALU.is_lt))
            step(nc.vector.tensor_scalar(goff[:], gmask[:], 1.0, -OFF_GROUP, ALU.subtract, ALU.mult))
            grouped = biased[:].rearrange("p t (g e) -> p t g e", g=GROUPS)
            step(nc.vector.tensor_tensor(grouped, grouped, over(gmask[:], 3, GROUP), ALU.mult))
            step(nc.vector.tensor_tensor(grouped, grouped, over(goff[:], 3, GROUP), ALU.add))
            for t in range(NT):
                step(nc.vector.max(best8[:, t, :], biased[:, t, :]))
                step(nc.vector.match_replace(taken[:, t, :], best8[:, t, :], biased[:, t, :], TAKEN))
            step(nc.vector.tensor_tensor(sel[:], biased[:], taken[:], ALU.not_equal))
            nc.vector.tensor_copy(sel_bf[:], sel[:]).then_inc(s.selected, 1)
            step(nc.vector.tensor_tensor(gate[:], score[:], sel[:], ALU.mult))
            step(nc.vector.tensor_reduce(gsum[:], gate[:], AX.X, ALU.add))
            step(nc.vector.reciprocal(ginv[:], gsum[:]))
            for t in range(NT):
                step(nc.vector.tensor_scalar(gate[:, t, :], gate[:, t, :], ginv[:, t:t + 1], ROUTED_SCALE, ALU.mult, ALU.mult))
            dve.wait_ge(s.places, 1)
            for t in range(NT):
                step(nc.vector.scalar_tensor_tensor(place[:, t, :], k.psum[:, 4, t * N_EXP:(t + 1) * N_EXP], 1.0,
                                                    sel[:, t, :], ALU.add, ALU.mult))
            count = k.psum[0:MAX_OVER, 4, 2 * N_EXP:3 * N_EXP]
            step(nc.vector.tensor_scalar(c1[:], count, SLOTS + 0.5, None, ALU.is_gt))
            step(nc.vector.tensor_scalar(c2[:], count, 2 * SLOTS + 0.5, None, ALU.is_gt))
            step(nc.vector.tensor_scalar(c3[:], count, 3 * SLOTS + 0.5, None, ALU.is_gt))
            nc.vector.engine_nop().then_inc(s.routed, 1)

            def match_matrix(p, par):
                slot = over(over(k.slot_no[:], 1, 2), 1, NT)
                nc.vector.tensor_tensor(match[par][:], slot, over(place[:, :, bass.ds(2 * p, 2)], 3, SLOTS),
                                        ALU.is_equal).then_inc(s.match, 1)

            match_matrix(0, 0)
            match_matrix(1, 1)
            step(nc.vector.tensor_tensor(c1[:], c1[:], c2[:], ALU.add))
            step(nc.vector.tensor_tensor(c1[:], c1[:], c3[:], ALU.add))
            step(nc.vector.memset(c2[:], 0.0))
            step(nc.vector.tensor_tensor_scan(c3[:], c1[:], c2[:], 0.0, ALU.add, ALU.add))
            step(nc.vector.tensor_copy(table[:, 2:3], c3[:, N_EXP - 1:N_EXP]))
            step(nc.vector.tensor_scalar(c2[:], c3[:], k.pass_no[:, 0:1], None, ALU.is_le))
            step(nc.vector.tensor_reduce(table[:, 0:1], c2[:], AX.X, ALU.add))
            step(nc.vector.tensor_tensor(c1[:], c1[:], c2[:], ALU.mult))
            step(nc.vector.tensor_reduce(table[:, 1:2], c1[:], AX.X, ALU.add))
            step(nc.vector.tensor_tensor(table[:, 1:2], k.pass_no[:, 0:1], table[:, 1:2], ALU.subtract))
            step(nc.vector.tensor_scalar(table[:, 1:2], table[:, 1:2], 1.0, float(SLOTS), ALU.add, ALU.mult))
            step(nc.vector.tensor_scalar(table[:, 3:4], table[:, 0:1], N_EXP - 0.5, 4.0 * S, ALU.is_gt, ALU.mult))
            step(nc.vector.tensor_tensor(table[:, 1:2], table[:, 1:2], table[:, 3:4], ALU.add))
            step(nc.vector.tensor_scalar(table[:, 0:1], table[:, 0:1], N_EXP - 1.0, None, ALU.min))
            nc.vector.tensor_copy(table_i[:], table[:]).then_inc(s.table_sb, 1)

            for t in range(NT):
                dve.wait_ge(s.shared_silu, t + 1)
                nc.vector.tensor_tensor(sh[:, t, :], ssilu[:, t, :], k.psum[:, 5 + t, FE:2 * FE],
                                        ALU.mult).then_inc(s.shared_h, 1)
            dve.wait_ge(s.shared_hT_psum, 1)
            nc.vector.tensor_copy(shT[:].rearrange("p t j c -> p (t j c)"), turn_ps).then_inc(s.shared_hT, 1)
            dve.wait_ge(s.gather_b, 1)
            nc.vector.tensor_copy(flat(xsel[:, 4:8, :]), k.psum[:, 5, :]).then_inc(s.xsel_b, 1)

            def pair(p, par, final=False, last_match=False):
                dve.wait_ge(s.silu, p + 1)
                nc.vector.tensor_tensor(h[:], silu[:], up_ps[:, FE:2 * FE], ALU.mult).then_inc(s.h, 1)
                if not final:
                    dve.wait_ge(s.gather_b, p + 2)
                    nc.vector.tensor_copy(flat(xsel[:, 4:8, :]), k.psum[:, 5, :]).then_inc(s.xsel_b, 1)
                if not last_match:
                    dve.wait_ge(s.gated, p + 1)
                    match_matrix(p + 2, par)
                dve.wait_ge(s.down_b, p + 1)
                nc.vector.tensor_copy(o[:, BANK:D], turn_ps).then_inc(s.o_b, 1)

            with dve.Fori(0, PAIRS // 2 - 1) as i:
                pair(2 * i, 0)
                pair(2 * i + 1, 1)
            pair(PAIRS - 2, 0, last_match=True)
            pair(PAIRS - 1, 1, final=True, last_match=True)

            dve.wait_ge(s.table_back, 16)
            n_over = dve.value_load(k.over_dram[0:1, 2:3], min_val=0, max_val=MAX_OVER)
            with dve.If(n_over > 0):
                nc.vector.tensor_copy(back[:], back_i[:]).then_inc(s.v_back, 1)
                dve.wait_ge(s.v_back, 1)
                dve.wait_ge(s.combined, PAIRS)
                slot = over(k.slot_no[:], 1, NT)
                with dve.Fori(0, (n_over + 1) // 2) as i:
                    experts = [dve.value_load(k.over_dram[bass.ds(2 * i + j, 1), 0:1], min_val=0,
                                              max_val=N_EXP - 1) for j in range(2)]
                    dve.wait_ge(s.v_combined, i + 1)
                    for j, e in enumerate(experts):
                        nc.vector.tensor_scalar(shifted[:, :, j], place[:, :, bass.ds(e, 1)].rearrange("p t o -> p (t o)"),
                                                back[:, bass.ds(2 * i + j, 1), 1], None, ALU.subtract
                                                ).then_inc(s.v_shifted, 1)
                        dve.wait_ge(s.v_shifted, 4 * i + 2 * j + 1)
                        nc.vector.tensor_tensor(match[0][:, :, j, :], slot, over(shifted[:, :, j], 2, SLOTS),
                                                ALU.is_equal).then_inc(s.v_shifted, 1)
                        dve.wait_ge(s.v_shifted, 4 * i + 2 * j + 2)
                        nc.vector.tensor_tensor(gated[0][:, :, j, :], match[0][:, :, j, :],
                                                over(gate[:, :, bass.ds(e, 1)].rearrange("p t o -> p (t o)"), 2, SLOTS),
                                                ALU.mult).then_inc(s.v_match, 1)
                    dve.wait_ge(s.v_gather, i + 1)
                    nc.vector.tensor_copy(flat(xsel[:, 4:8, :]), k.psum[:, 5, :]).then_inc(s.v_xsel_b, 1)
                    dve.wait_ge(s.v_silu, i + 1)
                    nc.vector.tensor_tensor(h[:], silu[:], up_ps[:, FE:2 * FE], ALU.mult).then_inc(s.v_h, 1)
                    dve.wait_ge(s.v_down, i + 1)
                    nc.vector.tensor_copy(o[:, BANK:D], turn_ps).then_inc(s.v_o_b, 1)
            layer_norm_vector(nc, dve, step, s, k, w, s.y_ready)
    ctx.close()



def flat(ap):
    return ap.rearrange("p a b -> p (a b)")


EV_LAT = Q_LORA + KV_LORA + MLA_R
EV_G = EV_LAT
EV_GATES = EV_G + 3 * GH * GD
EV_Z = EV_GATES + 2 * GH
G_CHUNKS = 3 * GH
PAD = CONV_W - 1
TWO_PI_HIGH, TWO_PI_MID = 6.28125, 0.0019350051879882812
TWO_PI_LOW = float(2 * np.pi - TWO_PI_HIGH - TWO_PI_MID)
ROUND = 1.5 * 2.0 ** 23


def columns_of(k, slot):
    return k.w_up[slot][:].rearrange("p a k f -> p (a k f)").rearrange("p (k n) -> p k n", k=KD)


def even_project(nc, k, d, e):
    ctx = ExitStack()
    s = semaphores(ctx, nc, "evp", "x small w0 w1 w2 w3 wz xT_psum xT vec rows_T rows lat_psum lat g_psum tap conv "
                                   "conv_done g z_psum z pool freq angle sines zero_pad")

    def sb(name, shape, dt=F32):
        return ctx.enter_context(nc.sbuf_tensor(f"evp_{name}", shape, dt))

    rows = sb("row_vectors", [CONV_W * G_CHUNKS + 3, P])
    raw = sb("raw", [P, G_CHUNKS, PAD + S])
    acc = sb("acc", [P, 2, S])
    pos_i = sb("pos_i", [P, NT], I32)
    pos = sb("pos", [P, NT])
    freq = sb("freq", [P, (MLA_R + WD) // 2])
    ang = sb("ang", [P, NT, (MLA_R + WD) // 2])
    turns = sb("turns", [P, NT, (MLA_R + WD) // 2])
    n_conv = CONV_W * G_CHUNKS
    win = d.ev_w_in[0].rearrange("(p k) n -> p k n", k=KD)

    with nc.Block(no_gpsimd_drain=True) as block:
        @block.sync
        def _(sp):
            sp.dma_start(k.x[:], d.x.rearrange("b (t p) n -> p (b t) n", p=P)).then_inc(s.x, 16)
            w0 = columns_of(k, 0)
            sp.dma_start(w0[:, :, 0:EV_LAT], win[:, :, 0:EV_LAT]).then_inc(s.w0, 16)
            sp.dma_start(w0[:, :, EV_LAT:EV_LAT + 2 * GH], win[:, :, EV_GATES:EV_Z]).then_inc(s.w0, 16)
            sp.dma_start(rows[0:n_conv, :], d.gdn_conv[0].rearrange("w (c p) -> (w c) p", p=P)).then_inc(s.small, 16)
            sp.dma_start(rows[n_conv:n_conv + 2, :], d.mla_q_norm[0].rearrange("(c p) -> c p", p=P)).then_inc(s.small, 16)
            sp.dma_start(rows[n_conv + 2:n_conv + 3, :], d.mla_kv_norm).then_inc(s.small, 16)
            with nc.allow_non_contiguous_dma(reason="256 positions"):
                sp.dma_start(pos_i[:], d.positions.rearrange("b (t p) -> p (b t)", p=P)).then_inc(s.small, 16)
            for i, sem in enumerate((s.w1, s.w2, s.w3)):
                sp.dma_start(columns_of(k, 1 + i), win[:, :, EV_G + i * GH * GD:EV_G + (i + 1) * GH * GD]).then_inc(sem, 16)
            sp.wait_ge(s.lat_psum, NT)
            sp.dma_start(columns_of(k, 0), win[:, :, EV_Z:EV_Z + GH * GD]).then_inc(s.wz, 16)
            sp.dma_start(k.w_down[0][:].rearrange("p j n -> p (j n)")[:, 0:2 * MLA_H * MLA_QK].rearrange("p (c n) -> p c n", c=2),
                         d.mla_w_qb[0].rearrange("(c p) n -> p c n", p=P)).then_inc(k.s_mla_w, 16)
            sp.dma_start(k.w_down[1][:, 0, :], d.mla_w_kvb[0]).then_inc(k.s_mla_w, 16)

        @block.gpsimd
        def _(pool):
            half_m, half_s = MLA_R // 2, WD // 2
            for i in range(half_m):
                nc.gpsimd.memset(freq[:, i:i + 1], float(np.float32(ROPE_THETA) ** -np.float32(2 * i / MLA_R)))
            for i in range(half_s):
                last = nc.gpsimd.memset(freq[:, half_m + i:half_m + i + 1],
                                        float(np.float32(ROPE_THETA) ** -np.float32(2 * i / WD)))
            last.then_inc(s.freq, 1)

        @block.tensor
        def _(pe):
            pe.wait_ge(s.x, 16)
            transpose_x_tensor(nc, pe, s, k)
            pe.wait_ge(s.small, 64)
            nr = n_conv + 3
            nc.tensor.transpose(k.psum[:, 4, 0:nr], rows[:, :], k.ident[0:nr, 0:nr]).then_inc(s.rows_T, 1)
            pe.wait_ge(s.w0, 32)
            pe.wait_ge(s.xT, KD // 2)
            w = columns_of(k, 0)
            for t in range(NT):
                for kk in range(KD):
                    last = nc.tensor.matmul(k.psum[:, 5 + t, 0:EV_LAT + 2 * GH], k.xT[:, kk, t * P:(t + 1) * P],
                                            w[:, kk, 0:EV_LAT + 2 * GH], start=kk == 0, stop=kk == KD - 1)
                last.then_inc(s.lat_psum, 1)
            for c in range(G_CHUNKS):
                pe.wait_ge((s.w1, s.w2, s.w3)[c // GH], 16)
                if c >= 4:
                    pe.wait_ge(s.tap, c - 3)
                w = columns_of(k, 1 + c // GH)
                for kk in range(KD):
                    last = nc.tensor.matmul(k.psum[:, c % 4, 0:S], w[:, kk, (c % GH) * P:(c % GH + 1) * P], k.xT[:, kk, :],
                                            start=kk == 0, stop=kk == KD - 1)
                last.then_inc(s.g_psum, 1)
            pe.wait_ge(s.wz, 16)
            pe.wait_ge(s.lat, NT)
            w = columns_of(k, 0)
            for t in range(NT):
                for kk in range(KD):
                    last = nc.tensor.matmul(k.psum[:, 5 + t, :], k.xT[:, kk, t * P:(t + 1) * P], w[:, kk, :],
                                            start=kk == 0, stop=kk == KD - 1)
                last.then_inc(s.z_psum, 1)

        @block.scalar
        def _(act):
            transpose_x_scalar(nc, act, s, k)
            act.wait_ge(s.rows_T, 1)
            nc.scalar.copy(e.cols[:], k.psum[:, 4, 0:n_conv + 3]).then_inc(s.rows, 1)
            for t in range(NT):
                act.wait_ge(s.lat_psum, t + 1)
                nc.scalar.copy(e.lat[:, t, :], k.psum[:, 5 + t, 0:EV_LAT + 2 * GH]).then_inc(s.lat, 1)
            act.wait_ge(s.angle, 2)
            nc.scalar.activation(flat(k.sin[:]), flat(ang[:]), ACT.Sin).then_inc(s.sines, 1)
            nc.scalar.activation(flat(k.cos[:]), flat(turns[:]), ACT.Sin, bias=k.eps[:, 1:2], scale=-1.0).then_inc(s.sines, 1)
            for c in range(G_CHUNKS):
                act.wait_ge(s.g_psum, c + 1)
                nc.scalar.copy(raw[:, c, PAD:], k.psum[:, c % 4, 0:S]).then_inc(s.tap, 1)
                if c >= 1:
                    act.wait_ge(s.conv, c)
                    nc.scalar.activation(e.gT[:, c - 1, :], acc[:, (c - 1) % 2, :], ACT.Silu).then_inc(s.g, 1)
            act.wait_ge(s.conv, G_CHUNKS)
            nc.scalar.activation(e.gT[:, G_CHUNKS - 1, :], acc[:, (G_CHUNKS - 1) % 2, :], ACT.Silu).then_inc(s.g, 1)
            for t in range(NT):
                act.wait_ge(s.z_psum, t + 1)
                nc.scalar.activation(e.z[:, t, :], k.psum[:, 5 + t, :], ACT.Silu).then_inc(s.z, 1)

        @block.vector
        def _(dve):
            step = Chain(dve, s.vec)
            step(nc.vector.memset(raw[:, :, 0:PAD], 0.0))
            dve.wait_ge(s.small, 64)
            dve.wait_ge(s.freq, 1)
            step(nc.vector.tensor_copy(pos[:], pos_i[:]))
            for t in range(NT):
                step(nc.vector.tensor_scalar(ang[:, t, :], freq[:], pos[:, t:t + 1], None, ALU.mult))
            a, n = flat(ang[:]), flat(turns[:])
            step(nc.vector.tensor_scalar(n, a, float(1 / (2 * np.pi)), None, ALU.mult))
            step(nc.vector.tensor_scalar(n, n, ROUND, None, ALU.add))
            step(nc.vector.tensor_scalar(n, n, ROUND, None, ALU.subtract))
            for part in (TWO_PI_HIGH, TWO_PI_MID, TWO_PI_LOW):
                step(nc.vector.scalar_tensor_tensor(a, n, -part, a, ALU.mult, ALU.add))
            step(nc.vector.tensor_scalar(a, a, 3.1415925, -3.1415925, ALU.min, ALU.max))
            nc.vector.engine_nop().then_inc(s.angle, 1)
            nc.vector.scalar_tensor_tensor(n, a, -1.0, a, ALU.mult, ALU.max).then_inc(s.angle, 1)
            dve.wait_ge(s.rows, 1)
            for c in range(G_CHUNKS):
                dve.wait_ge(s.tap, c + 1)
                if c >= 2:
                    dve.wait_ge(s.g, c - 1)
                y = acc[:, c % 2, :]
                step(nc.vector.tensor_scalar(y, raw[:, c, 0:S], e.cols[:, c:c + 1], None, ALU.mult))
                for i in range(1, CONV_W):
                    last = nc.vector.scalar_tensor_tensor(y, raw[:, c, i:i + S], e.cols[:, i * G_CHUNKS + c:i * G_CHUNKS + c + 1],
                                                          y, ALU.mult, ALU.add)
                    if i < CONV_W - 1:
                        step(last)
                    else:
                        last.then_inc(s.conv, 1)
    ctx.close()



HEADS, HV = 8, 64


def attention_tensor(nc, pe, s, k, a):
    for t in range(NT):
        keys = (t + 1) * P
        for b in range(4):
            pe.wait_ge(s.qT, b + 1)
            pe.wait_ge(s.kT, b + 1)
            if t:
                pe.wait_ge(s.masked, b + 1)
            for i in range(2):
                last = nc.tensor.matmul(k.psum[:, 4 + b, i * S:i * S + keys], a.qT(2 * b + i, t),
                                        a.kT(2 * b + i, keys), start=True, stop=True)
            last.then_inc(s.scores, 1)
        for half in range(2):
            pe.wait_ge(s.scaled, 8 * t + 4 * half + 4)
            if t:
                pe.wait_ge(s.mixed, half + 1)
            for kt in range(t + 1):
                for i in range(4):
                    last = nc.tensor.transpose(k.psum[:, 2 * half + kt, i * P:(i + 1) * P],
                                               a.pr[:, 4 * half + i, kt * P:(kt + 1) * P], k.ident[:])
            last.then_inc(s.turned, 1)
        for half in range(2):
            pe.wait_ge(s.pT, half + 1 if t == 0 else 4 + 2 * half)
            for b in range(2):
                for i in range(2):
                    for kt in range(t + 1):
                        last = nc.tensor.matmul(k.psum[i * HV:(i + 1) * HV, 2 * half, b * P:(b + 1) * P],
                                                a.v(4 * half + 2 * b + i, kt),
                                                a.pT[:, half, kt, (2 * b + i) * P:(2 * b + i + 1) * P],
                                                start=kt == 0, stop=kt == t)
            last.then_inc(s.done, 1)


def attention_scalar(nc, act, s, k, a):
    for t in range(NT):
        keys = (t + 1) * P
        act.wait_ge(s.max, t + 1)
        for h in range(HEADS):
            nc.scalar.activation(a.pr[:, h, 0:keys], a.pr[:, h, 0:keys], ACT.Exp, bias=a.nb[:, h:h + 1], scale=a.scale,
                                 accum_out=a.den[:, h:h + 1]).then_inc(s.probs, 1)
        if a.sinks is not None:
            act.wait_ge(s.sunk, t + 1)
            nc.scalar.activation(a.sunk[:], a.sunk[:], ACT.Exp).then_inc(s.sink_exp, 1)
        for half in range(2):
            act.wait_ge(s.turned, 2 * t + half + 1)
            if t:
                act.wait_ge(s.done, half + 1)
            for kt in range(t + 1):
                nc.scalar.copy(a.pT[:, half, kt, :], k.psum[:, 2 * half + kt, :]).then_inc(s.pT, 1)


def attention_vector(nc, dve, step, s, k, a):
    for t in range(NT):
        keys = (t + 1) * P
        for b in range(4):
            dve.wait_ge(s.scores, 4 * t + b + 1)
            if t:
                dve.wait_ge(s.turned, 2)
            nc.vector.tensor_tensor(a.pr[:, 2 * b:2 * b + 2, 0:keys],
                                    k.psum[:, 4 + b, :].rearrange("p (h c) -> p h c", h=2)[:, :, 0:keys],
                                    over(a.mask[:, 2 * P - keys:], 1, 2), ALU.add).then_inc(s.masked, 1)
        dve.wait_ge(s.masked, 4 * t + 4)
        step(nc.vector.tensor_reduce(a.mx[:], a.pr[:, :, 0:keys], AX.X, ALU.max))
        if a.sinks is None:
            nc.vector.tensor_scalar(a.nb[:], a.mx[:], -a.scale, None, ALU.mult).then_inc(s.max, 1)
        else:
            step(nc.vector.scalar_tensor_tensor(a.mx[:], a.mx[:], a.scale, a.sinks[:], ALU.mult, ALU.max))
            nc.vector.tensor_scalar(a.nb[:], a.mx[:], -1.0, None, ALU.mult).then_inc(s.max, 1)
            nc.vector.tensor_tensor(a.sunk[:], a.sinks[:], a.mx[:], ALU.subtract).then_inc(s.sunk, 1)
        for half in range(2):
            hs = slice(4 * half, 4 * half + 4)
            dve.wait_ge(s.probs, 8 * t + 4 * half + 4)
            if a.sinks is not None:
                dve.wait_ge(s.sink_exp, t + 1)
                step(nc.vector.tensor_tensor(a.den[:, hs], a.den[:, hs], a.sunk[:, hs], ALU.add))
            step(nc.vector.reciprocal(a.dinv[:, hs], a.den[:, hs]))
            for h in range(4 * half, 4 * half + 4):
                nc.vector.tensor_scalar(a.pr[:, h, 0:keys], a.pr[:, h, 0:keys], a.dinv[:, h:h + 1], None,
                                        ALU.mult).then_inc(s.scaled, 1)
        for half in range(2):
            dve.wait_ge(s.done, 2 * t + half + 1)
            nc.vector.tensor_copy(k.mixT[:, a.chunk + 2 * half:a.chunk + 2 * half + 2, t * P:(t + 1) * P],
                                  k.psum[:, 2 * half, 0:2 * P].rearrange("p (b c) -> p b c", b=2)).then_inc(s.mixed, 1)


def rope(nc, step, tmp, first, second, out1, out2, c, sn):
    n = first.shape[1]
    t1, t2, t3, t4 = (x[:, 0:n, :] for x in tmp)
    cc, ss = over(c, 1, n), over(sn, 1, n)
    step(nc.vector.tensor_tensor(t1, first, cc, ALU.mult))
    step(nc.vector.tensor_tensor(t2, second, ss, ALU.mult))
    step(nc.vector.tensor_tensor(t3, second, cc, ALU.mult))
    step(nc.vector.tensor_tensor(t4, first, ss, ALU.mult))
    step(nc.vector.tensor_tensor(out1, t1, t2, ALU.subtract))
    step(nc.vector.tensor_tensor(out2, t3, t4, ALU.add))



def even_latent_attention(nc, k, d, e):
    ctx = ExitStack()
    s = semaphores(ctx, nc, "mla", "vec act sumsq root normed latT_psum latT_q latT_kv q_psum kv_psum q_sb kv_sb kv_freed q_ready k_ready "
                                   "qT_psum kT_psum qT kT scores masked max probs scaled turned pT mixed done act_ssq")

    def sb(name, shape, dt=F32):
        return ctx.enter_context(nc.sbuf_tensor(f"mla_{name}", shape, dt))

    H, QK, HR = MLA_H, MLA_QK, MLA_R // 2
    junk = sb("junk", [P, Q_LORA])
    ssq = sb("ssq", [P, NT, 2])
    root = sb("root", [P, NT, 2])
    rinv = sb("rinv", [P, NT, 2])
    latT = sb("latT", [P, 3, S])
    qk = sb("qk", [P, 2 * NT * H * QK])
    q = qk[:, 0:NT * H * QK].rearrange("p (t h c) -> p t h c", t=NT, h=H)
    kc = qk[:, NT * H * QK:].rearrange("p (t h c) -> p t h c", t=NT, h=H)
    v = sb("v", [P, NT, H, MLA_V])
    tmp = [sb(f"tmp{i}", [P, H, HR]) for i in range(4)]
    krot = sb("krot", [P, NT, MLA_R])
    qT = sb("qT", [QK, H, S])
    kT = sb("kT", [QK, H, S])
    pr = qk[:, 0:H * S].rearrange("p (h c) -> p h c", h=H)
    pT = sb("pT", [P, 2, 2, H // 2 * P])
    mx = sb("max", [P, H])
    nb = sb("negmax", [P, H])
    den = sb("den", [P, H])
    dinv = sb("dinv", [P, H])
    scale = float(QK ** -0.5)
    a = named(pr=pr, pT=pT, mx=mx, nb=nb, den=den, dinv=dinv, scale=scale, mask=k.no_later, sinks=None, chunk=0,
                        qT=lambda h, t: qT[:, h, t * P:(t + 1) * P], kT=lambda h, keys: kT[:, h, 0:keys],
                        v=lambda h, kt: v[:, kt, h, :])
    wq = k.w_down[0][:].rearrange("p j n -> p (j n)")[:, 0:2 * H * QK].rearrange("p (c n) -> p c n", c=2)
    wkv = k.w_down[1][:, 0, :]
    n_conv = CONV_W * G_CHUNKS

    with nc.Block(no_gpsimd_drain=True) as block:
        @block.sync
        def _(sp):
            for half in range(2):
                sp.dma_start(columns_of(k, 1 + half),
                             d.ev_w_out[0][:, half * BANK:(half + 1) * BANK].rearrange("(c p) n -> p c n", p=P)).then_inc(k.s_out_w, 16)
            for i, src in enumerate((d.ln1_g, d.ln1_b)):
                sp.dma_start(k.ln[:, i, :], src[0:1].to_broadcast([P, D])).then_inc(k.s_out_w, 16)
            sp.dma_start(e.o_gain[:], d.gdn_norm.to_broadcast([P, GD])).then_inc(k.s_gdn_w, 16)
            sp.dma_start(e.a_log[:], d.gdn_a_log.to_broadcast([P, GH])).then_inc(k.s_gdn_w, 16)
            sp.dma_start(e.dt_bias[:], d.gdn_dt_bias.to_broadcast([P, GH])).then_inc(k.s_gdn_w, 16)

        @block.scalar
        def _(act):
            for t in range(NT):
                nc.scalar.activation(junk[:], e.lat[:, t, 0:Q_LORA], ACT.Square, accum_out=ssq[:, t, 0:1]).then_inc(s.act_ssq, 1)
                act.wait_ge(s.act_ssq, 2 * t + 1)
                nc.scalar.activation(junk[:, 0:KV_LORA], e.lat[:, t, Q_LORA:Q_LORA + KV_LORA], ACT.Square,
                                     accum_out=ssq[:, t, 1:2]).then_inc(s.act_ssq, 1)
                act.wait_ge(s.act_ssq, 2 * t + 2)
            nc.scalar.activation(root[:, :, 0], ssq[:, :, 0], ACT.Sqrt, bias=k.eps[:, 0:1], scale=1.0 / Q_LORA).then_inc(s.root, 1)
            nc.scalar.activation(root[:, :, 1], ssq[:, :, 1], ACT.Sqrt, bias=k.eps[:, 0:1], scale=1.0 / KV_LORA).then_inc(s.root, 1)
            act.wait_ge(s.latT_psum, 1)
            for c in range(2):
                nc.scalar.activation(latT[:, c, :], k.psum[:, 0, c * S:(c + 1) * S], ACT.Copy,
                                     scale=e.cols[:, n_conv + c:n_conv + c + 1]).then_inc(s.latT_q, 1)
            nc.scalar.activation(latT[:, 2, :], k.psum[:, 1, 0:S], ACT.Copy,
                                 scale=e.cols[:, n_conv + 2:n_conv + 3]).then_inc(s.latT_kv, 1)
            for t in range(NT):
                act.wait_ge(s.q_psum, t + 1)
                for half in range(2):
                    nc.scalar.copy(q[:, t, 4 * half:4 * half + 4, :].rearrange("p h c -> p (h c)"),
                                   k.psum[:, 2 + 2 * t + half, 0:H * QK // 2]).then_inc(s.q_sb, 1)
                act.wait_ge(s.kv_psum, t + 1)
                for half in range(2):
                    bank = (6 if t == 0 else 0) + half
                    both = k.psum[:, bank, :].rearrange("p (h c) -> p h c", c=MLA_N + MLA_V)
                    nc.scalar.copy(kc[:, t, 4 * half:4 * half + 4, 0:MLA_N], both[:, :, 0:MLA_N]).then_inc(s.kv_sb, 1)
                    nc.scalar.copy(v[:, t, 4 * half:4 * half + 4, :], both[:, :, MLA_N:]).then_inc(s.kv_sb, 1)
            for b in range(4):
                act.wait_ge(s.qT_psum, b + 1)
                nc.scalar.copy(qT[:, 2 * b:2 * b + 2, :].rearrange("p h c -> p (h c)"), k.psum[0:QK, b, :]).then_inc(s.qT, 1)
            attention_scalar(nc, act, s, k, a)

        @block.tensor
        def _(pe):
            pe.wait_ge(s.normed, 1)
            for c in range(3):
                for t in range(NT):
                    last = nc.tensor.transpose(k.psum[:, c // 2, (c % 2) * S + t * P:(c % 2) * S + (t + 1) * P],
                                               e.lat[:, t, c * P:(c + 1) * P], k.ident[:])
            last.then_inc(s.latT_psum, 1)
            pe.wait_ge(k.s_mla_w, 32)
            pe.wait_ge(s.latT_q, 2)
            pe.wait_ge(s.latT_kv, 1)
            for t in range(NT):
                for half in range(2):
                    for c in range(2):
                        last = nc.tensor.matmul(k.psum[:, 2 + 2 * t + half, 0:H * QK // 2], latT[:, c, t * P:(t + 1) * P],
                                                wq[:, c, half * H * QK // 2:(half + 1) * H * QK // 2], start=c == 0, stop=c == 1)
                last.then_inc(s.q_psum, 1)
                for half in range(2):
                    last = nc.tensor.matmul(k.psum[:, (6 if t == 0 else 0) + half, :], latT[:, 2, t * P:(t + 1) * P],
                                            wkv[:, half * BANK:(half + 1) * BANK], start=True, stop=True)
                last.then_inc(s.kv_psum, 1)
            pe.wait_ge(s.kv_sb, 8)
            pe.wait_ge(s.q_ready, 1)
            for b in range(4):
                for i in range(2):
                    for t in range(NT):
                        last = nc.tensor.transpose(k.psum[0:QK, b, i * S + t * P:i * S + (t + 1) * P], q[:, t, 2 * b + i, :], k.ident[:])
                last.then_inc(s.qT_psum, 1)
            pe.wait_ge(s.k_ready, 1)
            for b in range(4):
                for i in range(2):
                    for t in range(NT):
                        last = nc.tensor.transpose(k.psum[0:QK, 4 + b, i * S + t * P:i * S + (t + 1) * P], kc[:, t, 2 * b + i, :], k.ident[:])
                last.then_inc(s.kT_psum, 1)
            attention_tensor(nc, pe, s, k, a)

        @block.vector
        def _(dve):
            step = Chain(dve, s.vec)
            dve.wait_ge(s.root, 2)
            step(nc.vector.reciprocal(flat(rinv[:]), flat(root[:])))
            for t in range(NT):
                step(nc.vector.tensor_scalar(e.lat[:, t, 0:Q_LORA], e.lat[:, t, 0:Q_LORA], rinv[:, t, 0:1], None, ALU.mult))
                step(nc.vector.tensor_scalar(e.lat[:, t, Q_LORA:Q_LORA + KV_LORA], e.lat[:, t, Q_LORA:Q_LORA + KV_LORA],
                                             rinv[:, t, 1:2], None, ALU.mult))
            nc.vector.engine_nop().then_inc(s.normed, 1)
            k0 = Q_LORA + KV_LORA
            for t in range(NT):
                rope(nc, step, tmp, e.lat[:, t:t + 1, k0:k0 + HR], e.lat[:, t:t + 1, k0 + HR:k0 + MLA_R],
                     krot[:, t:t + 1, 0:HR], krot[:, t:t + 1, HR:], k.cos[:, t, 0:HR], k.sin[:, t, 0:HR])
            for t in range(NT):
                step(nc.vector.tensor_copy(kc[:, t, :, MLA_N:], over(krot[:, t, :], 1, H)))
            nc.vector.engine_nop().then_inc(s.k_ready, 1)
            for t in range(NT):
                dve.wait_ge(s.q_sb, 2 * t + 2)
                r1, r2 = q[:, t, :, MLA_N:MLA_N + HR], q[:, t, :, MLA_N + HR:]
                rope(nc, step, tmp, r1, r2, r1, r2, k.cos[:, t, 0:HR], k.sin[:, t, 0:HR])
            nc.vector.engine_nop().then_inc(s.q_ready, 1)
            for b in range(4):
                dve.wait_ge(s.kT_psum, b + 1)
                nc.vector.tensor_copy(kT[:, 2 * b:2 * b + 2, :].rearrange("p h c -> p (h c)"), k.psum[0:QK, 4 + b, :]).then_inc(s.kT, 1)
            attention_vector(nc, dve, step, s, k, a)
    ctx.close()



def log1p_exp_vector(nc, dve, step, s, x, out, w):
    step(nc.vector.scalar_tensor_tensor(w.mag, x, -1.0, x, ALU.mult, ALU.max))
    nc.vector.engine_nop().then_inc(s.mag, 1)
    dve.wait_ge(s.exp_mag, 1)
    step(nc.vector.tensor_scalar(w.u, w.t, 1.0, None, ALU.add))
    nc.vector.engine_nop().then_inc(s.one_more, 1)
    step(nc.vector.tensor_scalar(w.d, w.u, 1.0, None, ALU.subtract))
    step(nc.vector.tensor_scalar(w.tiny, w.d, 0.0, None, ALU.is_equal))
    step(nc.vector.tensor_tensor(w.d, w.d, w.tiny, ALU.add))
    step(nc.vector.reciprocal(w.d, w.d))
    step(nc.vector.tensor_tensor(w.tiny, w.tiny, w.t, ALU.mult))
    dve.wait_ge(s.log_u, 1)
    step(nc.vector.tensor_tensor(out, w.log, w.t, ALU.mult))
    step(nc.vector.tensor_tensor(out, out, w.d, ALU.mult))
    step(nc.vector.tensor_tensor(out, out, w.tiny, ALU.add))


def log1p_exp_scalar(nc, act, s, w):
    act.wait_ge(s.mag, 1)
    nc.scalar.activation(w.t, w.mag, ACT.Exp, scale=-1.0).then_inc(s.exp_mag, 1)
    act.wait_ge(s.one_more, 1)
    nc.scalar.activation(w.log, w.u, ACT.Ln).then_inc(s.log_u, 1)


def even_delta_net(nc, k, e):
    ctx = ExitStack()
    s = semaphores(ctx, nc, "gdn", "vec mag exp_mag one_more log_u beta_exp gates wide cum_psum cum exps cumrow decay_in decay "
                                   "nat_psum nat ssq root scaled extra T_psum T_a T_v pair_psum lower prod sub_v sub_a "
                                   "v0 w1 vn0 nw1 st_psum st o0 vn1_psum vn1 o1 o_sb ssq_o root_o on onT onT_sb mixed "
                                   "variance root_ln normed eps alog")

    def sb(name, shape, dt=F32):
        return ctx.enter_context(nc.sbuf_tensor(f"gdn_{name}", shape, dt))

    H, C = GH, GH * GD
    beta, decay = e.lat[:, :, EV_LAT:EV_LAT + H], e.lat[:, :, EV_LAT + H:EV_LAT + 2 * H]
    small = {n: sb(n, [P, NT, H]) for n in ("x", "lp", "beta", "g", "cum", "last", "e_cum", "e_left", "mag", "t", "u", "d", "tiny", "log", "tb")}
    w = named(**{n: small[n][:] for n in small})
    ea = sb("ea", [P, H])
    D_t = sb("decay_t", [P, NT, C])
    Dn = sb("decay_n", [P, NT, C])
    q, kk_, v = (sb(n, [P, NT, C]) for n in ("q", "k", "v"))
    kb = sb("kb", [P, NT, C])
    qg1, kg0, kbg1 = (sb(n, [P, C]) for n in ("qg1", "kg0", "kbg1"))
    qgT1 = sb("qgT1", [P, H, GD])
    ssq = sb("ssq", [P, 2, NT, H])
    rs = sb("rs", [P, 2, NT, H])
    A, B, Cm, Z = (sb(n, [P, NT, C]) for n in ("ma", "mb", "mc", "mz"))
    Lo, AT = (k.xT[:, 4 * i:4 * i + 4, :].rearrange("p c t -> p (c t)").rearrange("p (t c) -> p t c", t=NT)
              for i in range(2))
    wide = Cm
    blk = sb("block8_before", [P, P])
    vn, o = D_t, Dn
    nw1 = qg1
    st = sb("state", [P, C])
    qT, kT, kbT = e.gT[:, 0:H, :], e.gT[:, H:2 * H, :], e.gT[:, 2 * H:3 * H, :]
    heads = lambda ap: ap.rearrange("p (h c) -> p h c", h=H)
    bank = lambda b: k.psum[:, b, :]
    per_head = lambda ap: over(ap, 2, GD)
    V_STAGES, A_STAGES = (1, 2, 3, 4, 5, 6, 7, 8), (1, 2, 4, 5, 6, 7, 9)

    def reached(stages, m, t):
        return NT * sum(1 for x in stages if x < m) + t + 1

    with nc.Block(no_gpsimd_drain=True) as block:
        @block.tensor
        def _(pe):
            for i in range(3):
                for t in range(NT):
                    for h in range(H):
                        last = nc.tensor.transpose(k.psum[:, 2 + 2 * i + t, h * P:(h + 1) * P],
                                                   e.gT[:, i * H + h, t * P:(t + 1) * P], k.ident[:])
                    last.then_inc(s.nat_psum, 1)
            pe.wait_ge(s.gates, 1)
            for t in range(NT):
                nc.tensor.matmul(k.psum[:, 0, t * H:(t + 1) * H], k.upto[:], w.g[:, t, :], start=True, stop=True)
                last = nc.tensor.matmul(k.psum[:, 0, (NT + t) * H:(NT + t + 1) * H], k.ones[:], w.g[:, t, :],
                                        start=True, stop=True)
            last.then_inc(s.cum_psum, 1)
            pe.wait_ge(s.wide, 1)
            pe.wait_ge(s.cum, 1)
            for t in range(NT):
                for h in range(H):
                    last = nc.tensor.matmul(k.psum[:, 1 - t, h * P:(h + 1) * P], wide[:, t, h * P:(h + 1) * P], k.upto[:],
                                            start=True, stop=True)
                last.then_inc(s.cumrow, 1)
            pe.wait_ge(s.nat, 6)
            for i, src in enumerate((q, kk_, kb)):
                pe.wait_ge(s.scaled, i + 1)
                for t in range(NT):
                    for h in range(H):
                        last = nc.tensor.transpose(k.psum[:, 2 + 2 * i + t, h * P:(h + 1) * P],
                                                   src[:, t, h * P:(h + 1) * P], k.ident[:])
                    last.then_inc(s.T_psum, 1)
            pe.wait_ge(s.extra, 1)
            pe.wait_ge(s.decay_in, NT)
            for h in range(H):
                last = nc.tensor.transpose(k.psum[:, 0, h * P:(h + 1) * P], qg1[:, h * P:(h + 1) * P], k.ident[:])
            last.then_inc(s.T_psum, 1)
            pe.wait_ge(s.T_a, 4)
            pe.wait_ge(s.T_v, 3)
            for t in range(NT):
                tok = slice(t * P, (t + 1) * P)
                for i, (lhs, rhs) in enumerate(((kT, qT), (kT, kbT), (kbT, kT))):
                    for h in range(H):
                        last = nc.tensor.matmul(k.psum[:, 4 * t + 1 + i, h * P:(h + 1) * P], lhs[:, h, tok], rhs[:, h, tok],
                                                start=True, stop=True)
                last.then_inc(s.pair_psum, 1)

            def mm(t, b, left_t, right):
                for h in range(H):
                    cols = slice(h * P, (h + 1) * P)
                    last = nc.tensor.matmul(k.psum[:, 4 * t + b, cols], left_t[:, t, cols], right[:, t, cols], start=True, stop=True)
                return last

            def turn(t, b, m):
                for h in range(H):
                    cols = slice(h * P, (h + 1) * P)
                    nc.tensor.transpose(k.psum[:, 4 * t + b, cols], m[:, t, cols], k.ident[:])

            def product(m, t):
                if m == 1:
                    mm(t, 0, B, A)
                    return mm(t, 1, A, B)
                if m == 2:
                    mm(t, 2, B, A)
                    return mm(t, 3, A, Z)
                if m == 3:
                    return mm(t, 0, B, Z)
                if m == 4:
                    turn(t, 1, Z)
                    mm(t, 2, Lo, Z)
                    return mm(t, 3, Z, Lo)
                if m == 5:
                    mm(t, 0, Cm, B)
                    return mm(t, 1, B, Cm)
                if m == 6:
                    mm(t, 2, Cm, B)
                    mm(t, 3, B, Cm)
                    return mm(t, 0, B, Z)
                if m == 7:
                    mm(t, 1, Cm, B)
                    return mm(t, 2, B, Z)
                if m == 8:
                    return mm(t, 3, B, Z)
                return mm(t, 0, A, Z)

            for m in range(1, 10):
                for t in range(NT):
                    if m == 1:
                        pe.wait_ge(s.lower, t + 1)
                    else:
                        pe.wait_ge(s.sub_v, reached(V_STAGES, m - 1, t))
                        pe.wait_ge(s.sub_a, reached(A_STAGES, m - 1, t) if m - 1 in A_STAGES else reached(A_STAGES, m - 2, t))
                    product(m, t).then_inc(s.prod, 1)

            pe.wait_ge(s.sub_a, reached(A_STAGES, 9, 1))
            for h in range(H):
                cols = slice(h * P, (h + 1) * P)
                last = nc.tensor.matmul(k.psum[:, 1, cols], B[:, 0, cols], v[:, 0, cols], start=True, stop=True)
            last.then_inc(s.v0, 1)
            pe.wait_ge(s.extra, 2)
            for h in range(H):
                cols = slice(h * P, (h + 1) * P)
                last = nc.tensor.matmul(k.psum[:, 5, cols], kbg1[:, cols], B[:, 1, cols], start=True, stop=True)
            last.then_inc(s.w1, 1)
            pe.wait_ge(s.vn0, 1)
            for h in range(H):
                cols = slice(h * P, (h + 1) * P)
                last = nc.tensor.matmul(k.psum[:, 2, cols], kg0[:, cols], vn[:, 0, cols], start=True, stop=True)
            last.then_inc(s.st_psum, 1)
            for h in range(H):
                cols = slice(h * P, (h + 1) * P)
                last = nc.tensor.matmul(k.psum[:, 3, cols], AT[:, 0, cols], vn[:, 0, cols], start=True, stop=True)
            last.then_inc(s.o0, 1)
            pe.wait_ge(s.st, 1)
            pe.wait_ge(s.nw1, 1)
            for h in range(H):
                cols = slice(h * P, (h + 1) * P)
                nc.tensor.matmul(k.psum[:, 6, cols], B[:, 1, cols], v[:, 1, cols], start=True, stop=False)
                last = nc.tensor.matmul(k.psum[:, 6, cols], nw1[:, cols], st[:, cols], start=False, stop=True)
            last.then_inc(s.vn1_psum, 1)
            pe.wait_ge(s.vn1, 1)
            for h in range(H):
                cols = slice(h * P, (h + 1) * P)
                nc.tensor.matmul(k.psum[:, 7, cols], qgT1[:, h, :], st[:, cols], start=True, stop=False)
                last = nc.tensor.matmul(k.psum[:, 7, cols], AT[:, 1, cols], vn[:, 1, cols], start=False, stop=True)
            last.then_inc(s.o1, 1)
            for t in range(NT):
                pe.wait_ge(s.on, t + 1)
                for h in range(H):
                    last = nc.tensor.transpose(k.psum[:, 4 + t, h * P:(h + 1) * P], o[:, t, h * P:(h + 1) * P], k.ident[:])
                last.then_inc(s.onT, 1)

        @block.scalar
        def _(act):
            act.wait_ge(k.s_gdn_w, 48)
            nc.scalar.activation(ea[:], e.a_log[:], ACT.Exp).then_inc(s.alog, 1)
            nc.scalar.activation(w.tb, beta, ACT.Exp, scale=-1.0).then_inc(s.beta_exp, 1)
            log1p_exp_scalar(nc, act, s, w)
            for i in range(6):
                act.wait_ge(s.nat_psum, i + 1)
                nc.scalar.copy((q, kk_, v)[i // 2][:, i % 2, :], bank(2 + i)).then_inc(s.nat, 1)
            act.wait_ge(s.cum, 1)
            nc.scalar.activation(w.e_cum, w.cum, ACT.Exp).then_inc(s.exps, 1)
            nc.scalar.activation(w.e_left, w.last, ACT.Exp).then_inc(s.exps, 1)
            for t in range(NT):
                act.wait_ge(s.decay_in, t + 1)
                nc.scalar.activation(D_t[:, t, :], D_t[:, t, :], ACT.Exp).then_inc(s.decay, 1)
                nc.scalar.activation(Dn[:, t, :], Dn[:, t, :], ACT.Exp, scale=-1.0).then_inc(s.decay, 1)
            act.wait_ge(s.ssq, 1)
            nc.scalar.activation(rs[:].rearrange("p a t h -> p (a t h)"), ssq[:].rearrange("p a t h -> p (a t h)"),
                                 ACT.Sqrt, bias=k.eps[:, 0:1]).then_inc(s.root, 1)
            for i in (0, 2):
                for t in range(NT):
                    act.wait_ge(s.T_psum, 2 * i + t + 1)
                    nc.scalar.copy((qT, kT, kbT)[i][:, :, t * P:(t + 1) * P], heads(bank(2 + 2 * i + t))).then_inc(s.T_a, 1)
            for m in A_STAGES:
                for t in range(NT):
                    act.wait_ge(s.prod, NT * (m - 1) + t + 1)
                    moves = {1: [(A, 0)], 2: [(B, 2)], 4: [(A, 1), (B, 3)], 5: [(B, 0)], 6: [(B, 2), (Cm, 3)], 7: [(B, 1)],
                             9: [(B, 0)]}[m]
                    for to, b in moves:
                        last = nc.scalar.copy(to[:, t, :], bank(4 * t + b))
                    last.then_inc(s.sub_a, 1)
            act.wait_ge(s.w1, 1)
            nc.scalar.mul(nw1[:], bank(5), -1.0).then_inc(s.nw1, 1)
            act.wait_ge(s.st_psum, 1)
            nc.scalar.copy(st[:], bank(2)).then_inc(s.st, 1)
            for t in range(NT):
                act.wait_ge((s.o0, s.o1)[t], 1)
                nc.scalar.copy(o[:, t, :], bank(3 + 4 * t)).then_inc(s.o_sb, 1)
                act.wait_ge(s.ssq_o, t + 1)
                nc.scalar.activation(rs[:, 0, t, :], ssq[:, 0, t, :], ACT.Sqrt, bias=k.eps[:, 0:1], scale=1.0 / GD).then_inc(s.root_o, 1)
            for t in range(NT):
                act.wait_ge(s.onT, t + 1)
                nc.scalar.copy(k.mixT[:, 4:8, t * P:(t + 1) * P], heads(bank(4 + t))).then_inc(s.mixed, 1)

        @block.gpsimd
        def _(pool):
            pool.wait_ge(s.gates, 1)
            nc.gpsimd.tensor_copy(wide[:].rearrange("p t (h c) -> p (t h) c", h=H),
                                  over(w.g.rearrange("p t h -> p (t h)"), 2, GD)).then_inc(s.wide, 1)
            pool.wait_ge(s.nat, 6)
            pool.wait_ge(s.gates, 1)
            for t in range(NT):
                last = nc.gpsimd.tensor_tensor(heads(v[:, t, :]), heads(v[:, t, :]), per_head(w.beta[:, t, :]), ALU.mult)
            pool.wait_ge(s.scaled, 3)
            pool.wait_ge(s.exps, 2)
            nc.gpsimd.tensor_tensor(heads(qg1[:]), heads(q[:, 1, :]), per_head(w.e_cum[:, 1, :]), ALU.mult).then_inc(s.extra, 1)
            nc.gpsimd.tensor_tensor(heads(kg0[:]), heads(kk_[:, 0, :]), per_head(w.e_left[:, 0, :]), ALU.mult)
            nc.gpsimd.tensor_tensor(heads(kbg1[:]), heads(kb[:, 1, :]), per_head(w.e_cum[:, 1, :]), ALU.mult).then_inc(s.extra, 1)

        @block.vector
        def _(dve):
            step = Chain(dve, s.vec)
            step(nc.vector.tensor_tensor(blk[:], k.block8[:], k.upto[:], ALU.mult))
            step(nc.vector.tensor_tensor(blk[:], blk[:], k.ident[:], ALU.subtract))
            dve.wait_ge(s.beta_exp, 1)
            step(nc.vector.tensor_scalar(w.tb, w.tb, 1.0, None, ALU.add))
            step(nc.vector.reciprocal(w.beta, w.tb))
            dve.wait_ge(k.s_gdn_w, 48)
            step(nc.vector.tensor_tensor(w.x, decay, over(e.dt_bias[:], 1, NT), ALU.add))
            log1p_exp_vector(nc, dve, step, s, w.x, w.lp, w)
            step(nc.vector.scalar_tensor_tensor(w.g, w.x, 0.0, w.lp, ALU.max, ALU.add))
            dve.wait_ge(s.alog, 1)
            for t in range(NT):
                step(nc.vector.scalar_tensor_tensor(w.g[:, t, :], w.g[:, t, :], -1.0, ea[:], ALU.mult, ALU.mult))
            nc.vector.engine_nop().then_inc(s.gates, 1)
            dve.wait_ge(s.cum_psum, 1)
            step(nc.vector.tensor_copy(w.cum.rearrange("p t h -> p (t h)"), k.psum[:, 0, 0:NT * H]))
            step(nc.vector.tensor_tensor(w.last.rearrange("p t h -> p (t h)"), k.psum[:, 0, NT * H:2 * NT * H],
                                         w.cum.rearrange("p t h -> p (t h)"), ALU.subtract))
            nc.vector.engine_nop().then_inc(s.cum, 1)
            for t in range(NT):
                dve.wait_ge(s.cumrow, t + 1)
                for h in range(H):
                    cols = slice(h * P, (h + 1) * P)
                    nc.vector.scalar_tensor_tensor(D_t[:, t, cols], k.psum[:, 1 - t, cols], w.cum[:, t, h:h + 1],
                                                   k.no_later_T[:], ALU.subtract, ALU.add)
                    last = nc.vector.scalar_tensor_tensor(Dn[:, t, cols], k.psum[:, 1 - t, cols], w.cum[:, t, h:h + 1],
                                                          k.off_strict[:], ALU.subtract, ALU.add)
                last.then_inc(s.decay_in, 1)
            dve.wait_ge(s.nat, 4)
            dve.wait_ge(s.cumrow, NT)
            for i, m in enumerate((q, kk_)):
                for t in range(NT):
                    step(nc.vector.tensor_tensor(A[:, t, :], m[:, t, :], m[:, t, :], ALU.mult))
                    step(nc.vector.tensor_reduce(ssq[:, i, t, :], heads(A[:, t, :]), AX.X, ALU.add))
            nc.vector.engine_nop().then_inc(s.ssq, 1)
            dve.wait_ge(s.root, 1)
            step(nc.vector.reciprocal(rs[:].rearrange("p a t h -> p (a t h)"), rs[:].rearrange("p a t h -> p (a t h)")))
            for t in range(NT):
                step(nc.vector.scalar_tensor_tensor(heads(q[:, t, :]), heads(q[:, t, :]), float(GD ** -0.5),
                                                    per_head(rs[:, 0, t, :]), ALU.mult, ALU.mult))
            nc.vector.engine_nop().then_inc(s.scaled, 1)
            for t in range(NT):
                step(nc.vector.tensor_tensor(heads(kk_[:, t, :]), heads(kk_[:, t, :]), per_head(rs[:, 1, t, :]), ALU.mult))
            nc.vector.engine_nop().then_inc(s.scaled, 1)
            for t in range(NT):
                step(nc.vector.tensor_tensor(heads(kb[:, t, :]), heads(kk_[:, t, :]), per_head(w.beta[:, t, :]), ALU.mult))
            nc.vector.engine_nop().then_inc(s.scaled, 1)
            for t in range(NT):
                dve.wait_ge(s.T_psum, 2 + t + 1)
                nc.vector.tensor_copy(kT[:, :, t * P:(t + 1) * P], heads(bank(4 + t))).then_inc(s.T_v, 1)
            dve.wait_ge(s.T_psum, 7)
            nc.vector.tensor_copy(qgT1[:], heads(bank(0))).then_inc(s.T_v, 1)
            dve.wait_ge(s.decay, 2 * NT)
            blocks, blocks_t = over(k.block8[:], 1, H), over(blk[:], 1, H)
            one = over(k.ident[:], 1, H)
            for t in range(NT):
                dve.wait_ge(s.pair_psum, t + 1)
                step(nc.vector.tensor_tensor(AT[:, t, :], bank(4 * t + 1), D_t[:, t, :], ALU.mult))
                step(nc.vector.tensor_tensor(B[:, t, :], bank(4 * t + 2), D_t[:, t, :], ALU.mult))
                step(nc.vector.tensor_tensor(heads(B[:, t, :]), heads(B[:, t, :]), blocks_t, ALU.mult))
                step(nc.vector.tensor_tensor(Lo[:, t, :], bank(4 * t + 3), Dn[:, t, :], ALU.mult))
                step(nc.vector.tensor_tensor(heads(A[:, t, :]), heads(Lo[:, t, :]), blocks, ALU.mult))
                step(nc.vector.tensor_tensor(Lo[:, t, :], Lo[:, t, :], A[:, t, :], ALU.subtract))
                step(nc.vector.tensor_tensor(heads(Z[:, t, :]), one, heads(B[:, t, :]), ALU.subtract))
                nc.vector.engine_nop().then_inc(s.lower, 1)
            for m in V_STAGES:
                for t in range(NT):
                    dve.wait_ge(s.prod, NT * (m - 1) + t + 1)
                    if m == 4:
                        step(nc.vector.tensor_copy(Cm[:, t, :], bank(4 * t + 2)))
                        last = nc.vector.tensor_tensor(heads(Z[:, t, :]), one, heads(Cm[:, t, :]), ALU.subtract)
                    elif m in (1, 5):
                        last = nc.vector.tensor_copy((B if m == 1 else Cm)[:, t, :], bank(4 * t + 1))
                    else:
                        b = {2: 3, 3: 0, 6: 0, 7: 2, 8: 3}[m]
                        last = nc.vector.tensor_tensor(Z[:, t, :], Z[:, t, :], bank(4 * t + b), ALU.add)
                    last.then_inc(s.sub_v, 1)
            dve.wait_ge(s.v0, 1)
            nc.vector.tensor_copy(vn[:, 0, :], bank(1)).then_inc(s.vn0, 1)
            dve.wait_ge(s.vn1_psum, 1)
            nc.vector.tensor_copy(vn[:, 1, :], bank(6)).then_inc(s.vn1, 1)
            for t in range(NT):
                dve.wait_ge(s.o_sb, t + 1)
                step(nc.vector.tensor_tensor(wide[:, t, :], o[:, t, :], o[:, t, :], ALU.mult))
                step(nc.vector.tensor_reduce(ssq[:, 0, t, :], heads(wide[:, t, :]), AX.X, ALU.add))
                nc.vector.engine_nop().then_inc(s.ssq_o, 1)
                dve.wait_ge(s.root_o, t + 1)
                step(nc.vector.reciprocal(rs[:, 0, t, :], rs[:, 0, t, :]))
                step(nc.vector.tensor_tensor(heads(o[:, t, :]), heads(o[:, t, :]), per_head(rs[:, 0, t, :]), ALU.mult))
                step(nc.vector.tensor_tensor(heads(o[:, t, :]), heads(o[:, t, :]), over(e.o_gain[:], 1, H), ALU.mult))
                step(nc.vector.tensor_tensor(o[:, t, :], o[:, t, :], e.z[:, t, :], ALU.mult))
                nc.vector.engine_nop().then_inc(s.on, 1)
    ctx.close()


def mixer_output(nc, k, layer, weights_ready, n_ready):
    ctx = ExitStack()
    s = semaphores(ctx, nc, f"out{layer}", "vec mixed variance root normed eps")
    ln = named(**layer_norm_tiles(lambda n, sh, dt=F32: ctx.enter_context(nc.sbuf_tensor(f"out{layer}_{n}", sh, dt))))
    with nc.Block(no_gpsimd_drain=True) as block:
        @block.tensor
        def _(pe):
            pe.wait_ge(weights_ready, n_ready)
            for t in range(NT):
                for half in range(2):
                    w = columns_of(k, 1 + half)
                    for c in range(KD):
                        last = nc.tensor.matmul(k.psum[:, 2 * t + half, :], k.mixT[:, c, t * P:(t + 1) * P], w[:, c, :],
                                                start=c == 0, stop=c == KD - 1)
                last.then_inc(s.mixed, 1)

        @block.scalar
        def _(act):
            act.wait_ge(s.eps, 1)
            layer_norm_scalar(nc, act, s, ln)

        @block.vector
        def _(dve):
            step = Chain(dve, s.vec)
            nc.vector.memset(ln.ln_eps[:], LN_EPS).then_inc(s.eps, 1)
            dve.wait_ge(weights_ready, n_ready)
            layer_norm_vector(nc, dve, step, s, k, ln, s.mixed)
    ctx.close()


def even_shared(ctx, nc, k):
    def sb(name, shape, dt=F32):
        return ctx.enter_context(nc.sbuf_tensor(f"ev_{name}", shape, dt))

    e = named()
    e.lat = sb("lat", [P, NT, EV_LAT + 2 * GH])
    e.cols = sb("cols", [P, CONV_W * G_CHUNKS + 3])
    e.gT = sb("gT", [P, G_CHUNKS, S])
    e.z = sb("z", [P, NT, GH * GD])
    e.o_gain = sb("o_gain", [P, GD])
    e.a_log = sb("a_log", [P, GH])
    e.dt_bias = sb("dt_bias", [P, GH])
    w = semaphores(ctx, nc, "even", "mla_weights out_weights gdn_small_weights")
    k.s_mla_w, k.s_out_w, k.s_gdn_w = w.mla_weights, w.out_weights, w.gdn_small_weights
    return e



OD_K = LH * LK
OD_V = 2 * OD_K
OD_GATES = OD_V + LH * LV
OD_O = OD_GATES + 2 * LH
OD_SQ = OD_O + LH * LV
OD_SK = OD_SQ + WH * WD
OD_END = OD_SK + 2 * WKV * WD


def odd_shared(ctx, nc, k):
    def sb(name, shape, dt=F32):
        return ctx.enter_context(nc.sbuf_tensor(f"od_{name}", shape, dt))

    e = named()
    e.mqT = sb("mqT", [P, 2, S])
    e.mkT = sb("mkT", [P, LH, S])
    e.v1 = sb("v1", [P, NT, LH, LV + 1])
    e.gate_o = sb("gate_o", [P, NT, LH * LV])
    e.m_gain = sb("m_gain", [P, LH * LV])
    e.rows = {n: sb(n, [LH, S]) for n in ("decay", "rest", "stab")}
    e.sq = sb("sq", [P, NT, WH, WD])
    e.sk = sb("sk", [P, NT, WKV, 2, 2, WD])
    e.sv = sb("sv", [P, NT, WKV, WD])
    e.sinks = sb("sinks", [P, WH])
    e.window = sb("window", [P, 2 * P])
    w = semaphores(ctx, nc, "odd", "out_weights small_weights")
    k.s_odd_out_w, k.s_odd_small = w.out_weights, w.small_weights
    return e


def odd_project(nc, k, d, e):
    ctx = ExitStack()
    s = semaphores(ctx, nc, "odp", "gates_w qk_w kv_w sq_w v_w o_w xT_psum xT vec gates_psum gates_read mq_psum mk_psum mqT mkT "
                                   "skv_psum skv sq_psum sq v_psum v o_psum o zeros pool mag exp_mag one_more log_u")

    def sb(name, shape, dt=F32):
        return ctx.enter_context(nc.sbuf_tensor(f"odp_{name}", shape, dt))

    wg = sb("w_gates", [P, KD, 2 * LH])
    bias = sb("gate_bias", [LH, 2])
    raw_i, raw_f, lp, run, off = (sb(n, [LH, S]) for n in ("raw_i", "raw_f", "lp", "run", "none"))
    w = named(**{n: sb(n, [LH, S])[:] for n in ("mag", "t", "u", "d", "tiny", "log")})
    sk_raw = sb("sk_raw", [P, NT, WKV, WD])
    tmp = [sb(f"tmp{i}", [P, WH, WD // 2]) for i in range(4)]
    win = d.od_w_in[0].rearrange("(p k) n -> p k n", k=KD)
    skv_w = k.w_down[0][:].rearrange("p j n -> p (j n)").rearrange("p (k n) -> p k n", k=KD)

    with nc.Block(no_gpsimd_drain=True) as block:
        @block.sync
        def _(sp):
            sp.dma_start(columns_of(k, 0), win[:, :, 0:OD_V]).then_inc(s.qk_w, 16)
            sp.dma_start(wg[:], win[:, :, OD_GATES:OD_O]).then_inc(s.gates_w, 16)
            with nc.allow_non_contiguous_dma(reason="four biases"):
                for i, src in enumerate((d.mlstm_b_i, d.mlstm_b_f)):
                    sp.dma_start(bias[:, i:i + 1], src.rearrange("o h -> h o")).then_inc(s.gates_w, 16)
            sp.dma_start(skv_w, win[:, :, OD_SK:OD_END]).then_inc(s.kv_w, 16)
            sp.dma_start(columns_of(k, 3), win[:, :, OD_SQ:OD_SK]).then_inc(s.sq_w, 16)
            sp.dma_start(columns_of(k, 1), win[:, :, OD_V:OD_GATES]).then_inc(s.v_w, 16)
            sp.dma_start(columns_of(k, 2), win[:, :, OD_O:OD_SQ]).then_inc(s.o_w, 16)
            sp.dma_start(e.m_gain[:], d.mlstm_norm.to_broadcast([P, LH * LV])).then_inc(k.s_odd_small, 16)
            sp.dma_start(e.sinks[:], d.swa_sinks.to_broadcast([P, WH])).then_inc(k.s_odd_small, 16)
            for i, src in enumerate((d.ln1_g, d.ln1_b)):
                sp.dma_start(k.ln[:, i, :], src[1:2].to_broadcast([P, D])).then_inc(k.s_odd_out_w, 16)
            for half, used in enumerate((s.v_psum, s.o_psum)):
                sp.wait_ge(used, NT)
                sp.dma_start(columns_of(k, 1 + half),
                             d.od_w_out[0][:, half * BANK:(half + 1) * BANK].rearrange("(c p) n -> p c n", p=P)
                             ).then_inc(k.s_odd_out_w, 16)

        @block.gpsimd
        def _(pool):
            nc.gpsimd.memset(e.mkT[:], 0.0).then_inc(s.zeros, 1)
            nc.gpsimd.memset(e.sk[:], 0.0).then_inc(s.zeros, 1)
            nc.gpsimd.memset(e.v1[:, :, :, LV:], 1.0).then_inc(s.zeros, 1)
            nc.gpsimd.memset(e.window[:], 0.0).then_inc(s.zeros, 1)
            pool.wait_ge(s.zeros, 4)
            nc.gpsimd.affine_select(out=e.window[:, 0:P], in_=e.window[:, 0:P], pattern=[[1, P]],
                                    compare_op=ALU.is_gt, fill=NEG, base=0, channel_multiplier=-1).then_inc(s.pool, 1)
            nc.gpsimd.affine_select(out=e.window[:, P:], in_=e.window[:, P:], pattern=[[-1, P]],
                                    compare_op=ALU.is_ge, fill=NEG, base=0, channel_multiplier=1).then_inc(s.pool, 1)
            pool.wait_ge(s.pool, 2)

        @block.tensor
        def _(pe):
            transpose_x_tensor(nc, pe, s, k)
            pe.wait_ge(s.xT, KD // 2)
            pe.wait_ge(s.gates_w, 48)
            for i in range(2):
                for kk in range(KD):
                    last = nc.tensor.matmul(k.psum[0:LH, 4, i * S:(i + 1) * S], wg[:, kk, i * LH:(i + 1) * LH], k.xT[:, kk, :],
                                            start=kk == 0, stop=kk == KD - 1)
            last.then_inc(s.gates_psum, 1)
            pe.wait_ge(s.qk_w, 16)
            for i, sem in enumerate((s.mq_psum, s.mk_psum)):
                w0 = columns_of(k, 0)
                for c in range(2):
                    for kk in range(KD):
                        last = nc.tensor.matmul(k.psum[:, 5 + i, c * S:(c + 1) * S],
                                                w0[:, kk, i * OD_K + c * P:i * OD_K + (c + 1) * P], k.xT[:, kk, :],
                                                start=kk == 0, stop=kk == KD - 1)
                last.then_inc(sem, 1)

            def natural(weights, bank, cols, sem):
                for t in range(NT):
                    place = k.psum[:, bank + t, :] if cols == BANK else k.psum[:, bank, t * cols:(t + 1) * cols]
                    for kk in range(KD):
                        last = nc.tensor.matmul(place, k.xT[:, kk, t * P:(t + 1) * P], weights[:, kk, :],
                                                start=kk == 0, stop=kk == KD - 1)
                    last.then_inc(sem, 1)

            pe.wait_ge(s.kv_w, 16)
            natural(skv_w, 7, S, s.skv_psum)
            pe.wait_ge(s.sq_w, 16)
            natural(columns_of(k, 3), 0, BANK, s.sq_psum)
            pe.wait_ge(s.v_w, 16)
            natural(columns_of(k, 1), 2, BANK, s.v_psum)
            pe.wait_ge(s.o_w, 16)
            pe.wait_ge(s.gates_read, 1)
            pe.wait_ge(s.mqT, 1)
            natural(columns_of(k, 2), 4, BANK, s.o_psum)

        @block.scalar
        def _(act):
            transpose_x_scalar(nc, act, s, k)
            log1p_exp_scalar(nc, act, s, w)
            act.wait_ge(s.mq_psum, 1)
            nc.scalar.copy(flat(e.mqT[:]), k.psum[:, 5, :]).then_inc(s.mqT, 1)
            act.wait_ge(s.zeros, 4)
            act.wait_ge(s.mk_psum, 1)
            for h in range(LH):
                part = slice((h % 2) * LK, (h % 2 + 1) * LK)
                nc.scalar.mul(e.mkT[part, h, :], k.psum[part, 6, (h // 2) * S:(h // 2 + 1) * S], float(LK ** -0.5)).then_inc(s.mkT, 1)
            act.wait_ge(s.skv_psum, NT)
            both = k.psum[:, 7, :].rearrange("p (t c) -> p t c", t=NT)
            nc.scalar.copy(sk_raw[:].rearrange("p t g c -> p t (g c)"), both[:, :, 0:WKV * WD]).then_inc(s.skv, 1)
            nc.scalar.copy(e.sv[:].rearrange("p t g c -> p t (g c)"), both[:, :, WKV * WD:]).then_inc(s.skv, 1)
            for t in range(NT):
                act.wait_ge(s.sq_psum, t + 1)
                nc.scalar.copy(e.sq[:, t, :, :].rearrange("p h c -> p (h c)"), k.psum[:, t, :]).then_inc(s.sq, 1)
            for t in range(NT):
                act.wait_ge(s.v_psum, t + 1)
                nc.scalar.copy(e.v1[:, t, :, 0:LV], k.psum[:, 2 + t, :].rearrange("p (h c) -> p h c", h=LH)).then_inc(s.v, 1)
            for t in range(NT):
                act.wait_ge(s.o_psum, t + 1)
                nc.scalar.activation(e.gate_o[:, t, :], k.psum[:, 4 + t, :], ACT.Sigmoid).then_inc(s.o, 1)

        @block.vector
        def _(dve):
            step = Chain(dve, s.vec)
            step(nc.vector.memset(off[:], 0.0))
            dve.wait_ge(s.gates_psum, 1)
            dve.wait_ge(s.gates_w, 48)
            step(nc.vector.tensor_scalar(raw_i[:], k.psum[0:LH, 4, 0:S], bias[:, 0:1], None, ALU.add))
            step(nc.vector.tensor_scalar(raw_f[:], k.psum[0:LH, 4, S:2 * S], bias[:, 1:2], None, ALU.add))
            nc.vector.engine_nop().then_inc(s.gates_read, 1)
            log1p_exp_vector(nc, dve, step, s, raw_f[:], lp[:], w)
            step(nc.vector.scalar_tensor_tensor(raw_f[:], raw_f[:], 0.0, lp[:], ALU.min, ALU.subtract))
            step(nc.vector.tensor_tensor_scan(run[:], raw_f[:], off[:], 0.0, ALU.add, ALU.add))
            step(nc.vector.tensor_tensor_scan(e.rows["stab"][:], raw_f[:], raw_i[:], 0.0, ALU.add, ALU.max))
            step(nc.vector.tensor_tensor(e.rows["decay"][:], run[:], e.rows["stab"][:], ALU.subtract))
            step(nc.vector.tensor_tensor(e.rows["rest"][:], raw_i[:], run[:], ALU.subtract))
            half = WD // 2
            own = slice(MLA_R // 2, None)
            dve.wait_ge(s.zeros, 4)
            dve.wait_ge(s.skv, 1)
            for t in range(NT):
                rope(nc, step, tmp, sk_raw[:, t, :, 0:half], sk_raw[:, t, :, half:], e.sk[:, t, :, 0, 0, 0:half],
                     e.sk[:, t, :, 0, 0, half:], k.cos[:, t, own], k.sin[:, t, own])
                step(nc.vector.tensor_copy(e.sk[:, t, :, 1, 1, :], e.sk[:, t, :, 0, 0, :]))
            for t in range(NT):
                dve.wait_ge(s.sq, t + 1)
                q1, q2 = e.sq[:, t, :, 0:half], e.sq[:, t, :, half:]
                rope(nc, step, tmp, q1, q2, q1, q2, k.cos[:, t, own], k.sin[:, t, own])
    ctx.close()


def odd_memory(nc, k, e):
    ctx = ExitStack()
    s = semaphores(ctx, nc, "mem", "vec sel wide_psum cols_psum cols neg_m qk_psum exps_in far exps pairs out_psum num "
                                   "ssq root normed turned mixed")

    def sb(name, shape, dt=F32):
        return ctx.enter_context(nc.sbuf_tensor(f"mem_{name}", shape, dt))

    H, C = LH, LH * LV
    sel = sb("head_rows", [H, H, P])
    cols = sb("cols", [P, 2 * NT, H])
    floor = sb("floor", [P, NT, H])
    ex = sb("exps", [P, H, S + P])
    w = sb("weights", [P, H, S + P])
    num = sb("num", [P, NT, H, LV + 1])
    den = sb("den", [P, NT, H])
    rden = sb("rden", [P, NT, H])
    o = sb("out", [P, NT, C])
    sq = sb("squares", [P, NT, C])
    ssq = sb("ssq", [P, NT, H])
    root = sb("root", [P, NT, H])
    heads = lambda ap: ap.rearrange("p (h c) -> p h c", h=H)
    wide = lambda h: k.psum[:, 4 + h // 2, (h % 2) * S:(h % 2 + 1) * S]

    with nc.Block(no_gpsimd_drain=True) as block:
        @block.tensor
        def _(pe):
            for i, r in enumerate(("rest", "stab")):
                for t in range(NT):
                    last = nc.tensor.transpose(k.psum[:, 6, (NT * i + t) * H:(NT * i + t + 1) * H],
                                               e.rows[r][:, t * P:(t + 1) * P], k.ident[0:H, 0:H])
            last.then_inc(s.cols_psum, 1)
            pe.wait_ge(s.sel, 1)
            for h in range(H):
                last = nc.tensor.matmul(wide(h), sel[:, h, :], e.rows["decay"][:], start=True, stop=True)
            last.then_inc(s.wide_psum, 1)
            for h in range(H):
                nc.tensor.matmul(k.psum[:, h, 0:S], e.mkT[:, h, 0:P], e.mqT[:, h // 2, :], start=True, stop=True)
                nc.tensor.matmul(k.psum[:, h, S:S + P], e.mkT[:, h, P:], e.mqT[:, h // 2, P:], start=True,
                                 stop=True).then_inc(s.qk_psum, 1)
            pe.wait_ge(s.pairs, H)
            for t in range(NT):
                for h in range(H):
                    place = k.psum[:, 4 + 2 * t + h // 2, (h % 2) * (LV + 1):(h % 2 + 1) * (LV + 1)]
                    for kt in range(t + 1):
                        first = S if kt else t * P
                        last = nc.tensor.matmul(place, w[:, h, first:first + P], e.v1[:, kt, h, :], start=kt == 0, stop=kt == t)
                last.then_inc(s.out_psum, 1)
            for t in range(NT):
                pe.wait_ge(s.normed, t + 1)
                for h in range(H):
                    last = nc.tensor.transpose(k.psum[:, t, h * P:(h + 1) * P], o[:, t, h * P:(h + 1) * P], k.ident[:])
                last.then_inc(s.turned, 1)

        @block.scalar
        def _(act):
            act.wait_ge(s.cols, 1)
            nc.scalar.activation(flat(floor[:]), flat(cols[:, NT:, :]), ACT.Exp, scale=-1.0).then_inc(s.neg_m, 1)
            act.wait_ge(s.exps_in, 1)
            for h in range(H):
                nc.scalar.activation(ex[:, h, P:S], wide(h)[:, P:], ACT.Exp, bias=cols[:, 0, h:h + 1]).then_inc(s.exps, 1)
                nc.scalar.activation(ex[:, h, 0:P], ex[:, h, 0:P], ACT.Exp).then_inc(s.exps, 1)
                nc.scalar.activation(ex[:, h, S:], ex[:, h, S:], ACT.Exp).then_inc(s.exps, 1)
            for t in range(NT):
                act.wait_ge(s.out_psum, t + 1)
                for half in range(2):
                    nc.scalar.copy(num[:, t, 2 * half:2 * half + 2, :].rearrange("p h c -> p (h c)"),
                                   k.psum[:, 4 + 2 * t + half, 0:2 * (LV + 1)]).then_inc(s.num, 1)
            act.wait_ge(s.ssq, 1)
            nc.scalar.activation(flat(root[:]), flat(ssq[:]), ACT.Sqrt, bias=k.eps[:, 0:1], scale=1.0 / LV).then_inc(s.root, 1)
            for t in range(NT):
                act.wait_ge(s.turned, t + 1)
                nc.scalar.copy(k.mixT[:, 0:H, t * P:(t + 1) * P], heads(k.psum[:, t, :])).then_inc(s.mixed, 1)

        @block.vector
        def _(dve):
            step = Chain(dve, s.vec)
            nc.vector.tensor_copy(sel[:], over(k.ident[0:H, 0:H], 2, P)).then_inc(s.sel, 1)
            dve.wait_ge(s.cols_psum, 1)
            nc.vector.tensor_copy(cols[:].rearrange("p i h -> p (i h)"), k.psum[:, 6, 0:2 * NT * H]).then_inc(s.cols, 1)
            dve.wait_ge(s.cols, 1)
            dve.wait_ge(s.wide_psum, 1)
            for h in range(H):
                for t in range(NT):
                    place = slice(S, S + P) if t else slice(0, P)
                    last = nc.vector.scalar_tensor_tensor(ex[:, h, place], wide(h)[:, t * P:(t + 1) * P], cols[:, t, h:h + 1],
                                                          k.no_later_T[:], ALU.add, ALU.add)
            last.then_inc(s.exps_in, 1)
            for h in range(H):
                dve.wait_ge(s.exps, 3 * h + 3)
                dve.wait_ge(s.qk_psum, h + 1)
                nc.vector.tensor_tensor(w[:, h, :], ex[:, h, :], k.psum[:, h, 0:S + P], ALU.mult).then_inc(s.pairs, 1)
            dve.wait_ge(s.neg_m, 1)
            dve.wait_ge(k.s_odd_small, 32)
            for t in range(NT):
                dve.wait_ge(s.num, 2 * t + 2)
                step(nc.vector.scalar_tensor_tensor(den[:, t, :], num[:, t, :, LV], -1.0, num[:, t, :, LV], ALU.mult, ALU.max))
                step(nc.vector.tensor_tensor(den[:, t, :], den[:, t, :], floor[:, t, :], ALU.max))
                step(nc.vector.reciprocal(rden[:, t, :], den[:, t, :]))
                step(nc.vector.tensor_tensor(heads(o[:, t, :]), num[:, t, :, 0:LV], over(rden[:, t, :], 2, LV), ALU.mult))
                step(nc.vector.tensor_tensor(sq[:, t, :], o[:, t, :], o[:, t, :], ALU.mult))
                step(nc.vector.tensor_reduce(ssq[:, t, :], heads(sq[:, t, :]), AX.X, ALU.add))
            nc.vector.engine_nop().then_inc(s.ssq, 1)
            for t in range(NT):
                step(nc.vector.tensor_tensor(e.gate_o[:, t, :], e.gate_o[:, t, :], e.m_gain[:], ALU.mult))
            dve.wait_ge(s.root, 1)
            step(nc.vector.reciprocal(flat(root[:]), flat(root[:])))
            for t in range(NT):
                step(nc.vector.tensor_tensor(heads(o[:, t, :]), heads(o[:, t, :]), over(root[:, t, :], 2, LV), ALU.mult))
                nc.vector.tensor_tensor(o[:, t, :], o[:, t, :], e.gate_o[:, t, :], ALU.mult).then_inc(s.normed, 1)
    ctx.close()


def odd_window(nc, k, e):
    ctx = ExitStack()
    s = semaphores(ctx, nc, "win", "vec qT_psum kT_psum qT kT scores masked max sunk sink_exp probs scaled turned pT mixed done")

    def sb(name, shape, dt=F32):
        return ctx.enter_context(nc.sbuf_tensor(f"win_{name}", shape, dt))

    qT = sb("qT", [P, WH // 2, S])
    kT = sb("kT", [P, WKV, 2, S])
    group = WH // WKV
    a = named(pr=sb("pr", [P, WH, S]), pT=sb("pT", [P, 2, 2, WH // 2 * P]), mx=sb("max", [P, WH]),
                        nb=sb("negmax", [P, WH]), den=sb("den", [P, WH]), dinv=sb("dinv", [P, WH]),
                        sunk=sb("sunk", [P, WH]), scale=float(WD ** -0.5), mask=e.window, sinks=e.sinks, chunk=4,
                        qT=lambda h, t: qT[:, h // 2, t * P:(t + 1) * P],
                        kT=lambda h, keys: kT[:, h // group, h % 2, 0:keys],
                        v=lambda h, kt: e.sv[:, kt, h // group, :])

    with nc.Block(no_gpsimd_drain=True) as block:
        @block.tensor
        def _(pe):
            for b in range(2):
                for i in range(2):
                    for t in range(NT):
                        last = nc.tensor.transpose(k.psum[:, b, i * S + t * P:i * S + (t + 1) * P],
                                                   e.sq[:, t, 4 * b + 2 * i:4 * b + 2 * i + 2, :].rearrange("p h c -> p (h c)"), k.ident[:])
                last.then_inc(s.qT_psum, 1)
            for g in range(WKV):
                for i in range(2):
                    for t in range(NT):
                        last = nc.tensor.transpose(k.psum[:, 2 + g, i * S + t * P:i * S + (t + 1) * P],
                                                   e.sk[:, t, g, i, :, :].rearrange("p u c -> p (u c)"), k.ident[:])
                last.then_inc(s.kT_psum, 1)
            attention_tensor(nc, pe, s, k, a)

        @block.scalar
        def _(act):
            for b in range(2):
                act.wait_ge(s.qT_psum, b + 1)
                nc.scalar.copy(flat(qT[:, 2 * b:2 * b + 2, :]), k.psum[:, b, :]).then_inc(s.qT, 2)
            attention_scalar(nc, act, s, k, a)

        @block.vector
        def _(dve):
            step = Chain(dve, s.vec)
            for g in range(WKV):
                dve.wait_ge(s.kT_psum, g + 1)
                nc.vector.tensor_copy(flat(kT[:, g, :, :]), k.psum[:, 2 + g, :]).then_inc(s.kT, 2)
            attention_vector(nc, dve, step, s, k, a)
    ctx.close()



def decoder_trunk(nc, d):
    experts = named(w_gate=d.moe_w_gate, w_up=d.moe_w_up, w_down=d.moe_w_down, s_gate=d.shared_w_gate,
                              s_up=d.shared_w_up, s_down=d.shared_w_down, router_w=d.router_w, router_b=d.router_b,
                              ln2_g=d.ln2_g, ln2_b=d.ln2_b)
    with ExitStack() as ctx:
        k = persistent(ctx, nc)
        constants(nc, k)
        with ExitStack() as layer:
            e = even_shared(layer, nc, k)
            even_project(nc, k, d, e)
            even_latent_attention(nc, k, d, e)
            even_delta_net(nc, k, e)
            mixer_output(nc, k, 0, k.s_out_w, 64)
        moe_layer(nc, k, experts, 0)
        with ExitStack() as layer:
            e = odd_shared(layer, nc, k)
            odd_project(nc, k, d, e)
            odd_memory(nc, k, e)
            odd_window(nc, k, e)
            mixer_output(nc, k, 1, k.s_odd_out_w, 64)
        moe_layer(nc, k, experts, 1, out=d.out[0])


INPUTS = ("x", "positions", "ev_w_in", "mla_q_norm", "mla_w_qb", "mla_kv_norm", "mla_w_kvb", "gdn_conv", "gdn_a_log",
          "gdn_dt_bias", "gdn_norm", "ev_w_out", "od_w_in", "mlstm_b_i", "mlstm_b_f", "mlstm_norm", "swa_sinks", "od_w_out",
          "ln1_g", "ln1_b", "router_w", "router_b", "moe_w_gate", "moe_w_up", "moe_w_down", "shared_w_gate", "shared_w_up",
          "shared_w_down", "ln2_g", "ln2_b")


def kernel(**inputs):
    import concourse.bacc as bacc
    from concourse.bass_utils import run_bass_kernel_spmd

    nc = bacc.Bacc("TRN2", target_bir_lowering=False, num_devices=1)
    arrays = {f"in_{name}": np.ascontiguousarray(inputs[name]) for name in INPUTS}
    d = named(**{name: nc.dram_tensor(f"in_{name}", list(arrays[f"in_{name}"].shape),
                                                mybir.dt.from_np(arrays[f"in_{name}"].dtype), kind="ExternalInput").ap()
                           for name in INPUTS})
    d.out = nc.dram_tensor("out_x", [1, S, D], F32, kind="ExternalOutput").ap()
    decoder_trunk(nc, d)
    result = run_bass_kernel_spmd(nc, [arrays], core_ids=[0])
    return result.results[0]["out_x"]
```

```python
from contextlib import ExitStack

import numpy as np
import concourse.bass as bass
from concourse import mybir

F32 = mybir.dt.float32
BF16 = mybir.dt.bfloat16
I32 = mybir.dt.int32
ALU = mybir.AluOpType
ACT = mybir.ActivationFunctionType
AX = mybir.AxisListType

P = 128
D = 1024
S = 256
NT = S // P
KD = D // P
BANK = 512

N_EXP = 64
GROUPS = 8
GROUP = N_EXP // GROUPS
TOP_GROUPS = 4
TOP_K = 8
FE = 256
KF = FE // P
SLOTS = 64
PAIRS = N_EXP // 2
MAX_OVER = 32
ROUTED_SCALE = 2.5
ALPHA = float(4 ** 0.25)
LN_EPS = 1e-5
RMS_EPS = 1e-6
NEG = -1e30
OFF_GROUP = -3.0e38
TAKEN = -3.3e38

MLA_H, MLA_N, MLA_R, MLA_V = 8, 64, 32, 64
MLA_QK = MLA_N + MLA_R
Q_LORA, KV_LORA = 256, 128
GH, GD = 4, 128
CONV_W = 4
LH, LK, LV = 4, 64, 128
WH, WKV, WD = 8, 2, 64
ROPE_THETA = 10000.0


def named(**parts):
    return type("Parts", (), parts)


def semaphores(ctx, nc, prefix, names):
    made = {n: nc.alloc_semaphore(f"{prefix}_{n}") for n in names.split()}

    def clear():
        nc.clear_and_free_semaphores(list(made.values()))
        nc.all_engine_barrier()

    ctx.callback(clear)
    return named(**made)


class Chain:

    def __init__(self, eng, sem):
        self.eng, self.sem, self.n = eng, sem, 0

    def __call__(self, instruction):
        self.n += 1
        instruction.then_inc(self.sem, 1)
        self.eng.wait_ge(self.sem, self.n)


def over(ap, axis, n):
    v = ap.unsqueeze(axis)
    shape = list(v.shape)
    shape[axis] = n
    return v.to_broadcast(shape)


def persistent(ctx, nc):
    def sb(name, shape, dt=F32):
        return ctx.enter_context(nc.sbuf_tensor(name, shape, dt))

    k = named()
    k.x = sb("x_tokens", [P, NT, D])
    k.xT = sb("x_transposed", [P, KD, S])
    k.w_up = [sb(f"w_up_ring{i}", [P, 2, KD, FE]) for i in range(4)]
    k.w_down = [sb(f"w_down_ring{i}", [P, KF, D]) for i in range(4)]
    k.ln = sb("ln_gain_bias", [P, 2, D])
    k.mixT = sb("mixed_transposed", [P, KD, S])
    k.cos = sb("rope_cos", [P, NT, MLA_R // 2 + WD // 2])
    k.sin = sb("rope_sin", [P, NT, MLA_R // 2 + WD // 2])
    k.upto = sb("upto", [P, P])
    k.no_later = sb("no_later", [P, 2 * P])
    k.no_later_T = sb("no_later_T", [P, P])
    k.off_strict = sb("off_strict", [P, P])
    k.block8 = sb("block8", [P, P])
    k.eps = sb("epsilons", [P, 2])
    k.router_w = sb("router_w_sb", [P, KD, N_EXP])
    k.router_b = sb("router_b_sb", [P, N_EXP])
    k.ident = sb("identity", [P, P])
    k.ident_bf = sb("identity_bf", [P, P], BF16)
    k.ones = sb("ones", [P, P])
    k.ones_bf = sb("ones_bf", [P, P], BF16)
    k.before_bf = sb("before_bf", [P, P], BF16)
    k.slot_no = sb("slot_no", [P, SLOTS])
    k.earlier8 = sb("earlier8", [P, GROUPS, GROUPS])
    k.pass_no = sb("pass_no", [MAX_OVER, 1])
    k.psum = ctx.enter_context(nc.psum_tensor("psum", [P, 8, BANK], F32))
    k.over_dram = nc.dram_tensor("overflow_table", [MAX_OVER, 4], I32, kind="Internal").ap()
    return k


def constants(nc, k):
    ctx = ExitStack()
    s = semaphores(ctx, nc, "const", "pool zeros")
    with nc.Block(no_gpsimd_drain=True) as block:
        @block.vector
        def _(dve):
            nc.vector.memset(k.ident[:], 0.0)
            nc.vector.memset(k.ones[:], 1.0)
            nc.vector.memset(k.ones_bf[:], 1.0)
            nc.vector.memset(k.no_later[:], 0.0)
            nc.vector.memset(k.no_later_T[:], 0.0)
            nc.vector.memset(k.off_strict[:], 0.0)
            nc.vector.memset(k.block8[:], 1.0)
            nc.vector.memset(k.eps[:, 0:1], RMS_EPS)
            nc.vector.memset(k.eps[:, 1:2], float(np.pi / 2))
            nc.vector.memset(k.earlier8[:], 1.0).then_inc(s.zeros, 1)

        @block.gpsimd
        def _(pool):
            step = Chain(pool, s.pool)
            step(nc.gpsimd.iota(k.slot_no[:], [[1, SLOTS]], base=1, channel_multiplier=0,
                                allow_small_or_imprecise_dtypes=True))
            step(nc.gpsimd.iota(k.pass_no[:], [[1, 1]], base=0, channel_multiplier=1,
                                allow_small_or_imprecise_dtypes=True))
            pool.wait_ge(s.zeros, 1)
            step(nc.gpsimd.affine_select(out=k.ident[:], in_=k.ident[:], pattern=[[-1, P]],
                                         compare_op=ALU.not_equal, fill=1.0, base=0, channel_multiplier=1))
            step(nc.gpsimd.tensor_copy(k.ident_bf[:], k.ident[:]))
            step(nc.gpsimd.affine_select(out=k.before_bf[:], in_=k.ones_bf[:], pattern=[[1, P]],
                                         compare_op=ALU.is_gt, fill=0.0, base=0, channel_multiplier=-1))
            step(nc.gpsimd.affine_select(out=k.earlier8[:], in_=k.earlier8[:], pattern=[[1, GROUPS], [-1, GROUPS]],
                                         compare_op=ALU.is_gt, fill=0.0, base=0, channel_multiplier=0))
            step(nc.gpsimd.affine_select(out=k.upto[:], in_=k.ones[:], pattern=[[1, P]],
                                         compare_op=ALU.is_ge, fill=0.0, base=0, channel_multiplier=-1))
            step(nc.gpsimd.affine_select(out=k.no_later[:, P:2 * P], in_=k.no_later[:, P:2 * P], pattern=[[-1, P]],
                                         compare_op=ALU.is_ge, fill=NEG, base=0, channel_multiplier=1))
            step(nc.gpsimd.affine_select(out=k.no_later_T[:], in_=k.no_later_T[:], pattern=[[1, P]],
                                         compare_op=ALU.is_ge, fill=NEG, base=0, channel_multiplier=-1))
            step(nc.gpsimd.affine_select(out=k.off_strict[:], in_=k.off_strict[:], pattern=[[-1, P]],
                                         compare_op=ALU.is_gt, fill=-NEG, base=0, channel_multiplier=1))
            step(nc.gpsimd.affine_select(out=k.block8[:], in_=k.block8[:], pattern=[[-8, P // 8], [0, 8]],
                                         compare_op=ALU.is_ge, fill=0.0, base=0, channel_multiplier=1))
            step(nc.gpsimd.affine_select(out=k.block8[:], in_=k.block8[:], pattern=[[8, P // 8], [0, 8]],
                                         compare_op=ALU.is_ge, fill=0.0, base=7, channel_multiplier=-1))
    ctx.close()



def layer_norm_vector(nc, dve, step, s, k, w, mix_ready, together):
    def statistics(t):
        dve.wait_ge(mix_ready, t + 1)
        for half in range(2):
            cols = slice(half * BANK, (half + 1) * BANK)
            step(nc.vector.scalar_tensor_tensor(w.resid[:, t, cols], k.x[:, t, cols], ALPHA,
                                                k.psum[:, 2 * t + half, :], ALU.mult, ALU.add))
            step(nc.vector.bn_stats(w.bn[:, t, half, :], w.resid[:, t, cols]))
        nc.vector.bn_aggr(w.meanvar[:, t, :], w.bn[:, t, :, :]).then_inc(s.variance, 1)
        dve.wait_ge(s.root, t + 1)
        step(nc.vector.reciprocal(w.rstd[:, t:t + 1], w.root[:, t:t + 1]))
        nc.vector.scalar_tensor_tensor(w.shift[:, t:t + 1], w.meanvar[:, t, 0:1], -1.0, w.rstd[:, t:t + 1],
                                       ALU.mult, ALU.mult).then_inc(s.rstd, 1)

    def finish(t):
        dve.wait_ge(s.centred, t + 1)
        step(nc.vector.tensor_tensor(w.resid[:, t, :], w.resid[:, t, :], k.ln[:, 0, :], ALU.mult))
        nc.vector.tensor_tensor(k.x[:, t, :], w.resid[:, t, :], k.ln[:, 1, :], ALU.add).then_inc(s.normed, 1)

    for t in range(NT):
        statistics(t)
        if not together:
            finish(t)
    if together:
        finish(1)


def layer_norm_scalar(nc, act, s, w):
    for t in range(NT):
        act.wait_ge(s.variance, t + 1)
        nc.scalar.activation(w.root[:, t:t + 1], w.meanvar[:, t, 1:2], ACT.Sqrt,
                             bias=w.ln_eps[:, 0:1]).then_inc(s.root, 1)
        act.wait_ge(s.rstd, t + 1)
        nc.scalar.activation(w.resid[:, t, :], w.resid[:, t, :], ACT.Identity, scale=w.rstd[:, t:t + 1],
                             bias=w.shift[:, t:t + 1]).then_inc(s.centred, 1)


def layer_norm_gpsimd(nc, pool, s, k, w):
    pool.wait_ge(s.centred, 1)
    nc.gpsimd.tensor_tensor(w.resid[:, 0, :], w.resid[:, 0, :], k.ln[:, 0, :], ALU.mult).then_inc(s.gained, 1)
    pool.wait_ge(s.gained, 1)
    nc.gpsimd.tensor_tensor(k.x[:, 0, :], w.resid[:, 0, :], k.ln[:, 1, :], ALU.add).then_inc(s.normed_first, 1)


def layer_norm_tiles(sb):
    return dict(resid=sb("resid", [P, NT, D]), bn=sb("bn", [P, NT, 2, 6]), meanvar=sb("meanvar", [P, NT, 2]),
                root=sb("root", [P, NT]), rstd=sb("rstd", [P, NT]), shift=sb("shift", [P, NT]), ln_eps=sb("ln_eps", [P, 1]))



def transpose_x_tensor(nc, pe, s, k):
    for b in range(KD // 2):
        for c in range(2):
            for t in range(NT):
                last = nc.tensor.transpose(k.psum[:, b, c * S + t * P:c * S + (t + 1) * P],
                                           k.x[:, t, 2 * b + c:D:KD], k.ident[:])
        last.then_inc(s.xT_psum, 1)


def transpose_x_scalar(nc, act, s, k):
    for b in range(KD // 2):
        act.wait_ge(s.xT_psum, b + 1)
        nc.scalar.copy(k.xT[:, 2 * b:2 * b + 2, :].rearrange("p c t -> p (c t)"),
                       k.psum[:, b, :]).then_inc(s.xT, 1)



def expert_semaphores(ctx, nc, layer):
    return semaphores(ctx, nc, f"experts{layer}", "router shared_w gu0 gu1 dn0 dn1")


def load_up(sp, k, d, layer, slot, e, sem):
    sp.dma_start(k.w_up[slot][:, 0:1].rearrange("p a k f -> p a (k f)"),
                 d.moe_w_gate[layer, bass.ds(e, 1)].rearrange("e (p k) f -> p e (k f)", k=KD)).then_inc(sem, 16)
    sp.dma_start(k.w_up[slot][:, 1:2].rearrange("p a k f -> p a (k f)"),
                 d.moe_w_up[layer, bass.ds(e, 1)].rearrange("e (p k) f -> p e (k f)", k=KD)).then_inc(sem, 16)


def load_down(sp, k, d, layer, slot, e, sem):
    sp.dma_start(k.w_down[slot][:], d.moe_w_down[layer, bass.ds(e, 1)].rearrange("e (j p) n -> p (e j) n", p=P)).then_inc(sem, 16)


def load_early_experts(sp, k, d, layer, x, places_0_1_free):
    sp.dma_start(k.router_w[:], d.router_w[layer].rearrange("(p k) e -> p k e", k=KD)).then_inc(x.router, 16)
    sp.dma_start(k.router_b[:], d.router_b[layer:layer + 1].to_broadcast([P, N_EXP])).then_inc(x.router, 16)
    for e in range(2):
        places_0_1_free(e)
        load_up(sp, k, d, layer, e, e, x.gu0)
    for e in range(2):
        load_down(sp, k, d, layer, e, e, x.dn0)


def load_shared(sp, k, d, layer, x):
    sp.dma_start(k.w_up[3][:, 0], d.shared_w_gate[layer].rearrange("(p k) f -> p k f", k=KD)).then_inc(x.shared_w, 16)
    sp.dma_start(k.w_up[3][:, 1], d.shared_w_up[layer].rearrange("(p k) f -> p k f", k=KD)).then_inc(x.shared_w, 16)
    sp.dma_start(k.w_down[3][:], d.shared_w_down[layer].rearrange("(j p) n -> p j n", p=P)).then_inc(x.shared_w, 16)
    load_up(sp, k, d, layer, 2, 2, x.gu1)
    load_down(sp, k, d, layer, 2, 2, x.dn1)


def moe_layer(nc, k, d, layer, x, out=None, fetch_next=None):
    ctx = ExitStack()
    names = ("tables xT_psum xT dve pool parts logits scores selected places routed table_sb table_dram "
             "table_back shared_up shared_h shared_silu shared_hT_psum shared_hT shared_down "
             "match pair_gates slot_gates gates_read silu h up gather_a gather_b xsel_a xsel_b turned turned_sb "
             "gate_parts high_a high_b rest_a rest_b middle split score_T score_T_psum "
             "down_a down_b combined "
             "v_back v_load v_shifted v_match v_silu v_h v_up v_gather v_xsel_a v_xsel_b v_turned v_turned_sb v_down v_high v_rest v_middle v_split v_gates_read "
             "v_combined y_ready variance root rstd centred gained normed normed_first stored eps")
    s = semaphores(ctx, nc, f"moe{layer}", names)

    def sb(name, shape, dt=F32):
        return ctx.enter_context(nc.sbuf_tensor(f"moe{layer}_{name}", shape, dt))

    w = named(**layer_norm_tiles(sb))
    part = [sb(f"x_part{i}", [P, NT, D], BF16) for i in range(3)]
    rest = w.resid
    match = [sb(f"match{i}", [P, NT, 2, SLOTS], BF16) for i in range(2)]
    pair_gates = [sb(f"pair_gates{i}", [P, NT, 2, 3], BF16) for i in range(2)]
    xsel = sb("x_selected", [P, KD, P])
    silu = sb("silu", [P, FE])
    h = sb("h", [P, FE])
    slot_gate = sb("slot_gate", [P, 1])
    hT = sb("hT", [P, KF * P])
    matchT = [sb(f"matchT{i}", [P, S], BF16) for i in range(2)]
    high = sb("out_high", [P, D], BF16)
    middle = sb("out_middle", [P, D], BF16)
    low = sb("out_low", [P, D], BF16)
    out_rest = sb("out_rest", [P, D])
    score_T = sb("score_T", [N_EXP, S])
    score = sb("score", [P, NT, N_EXP])
    biased = sb("biased", [P, NT, N_EXP])
    top8 = sb("top8", [P, NT * GROUPS, 8])
    gscore = sb("group_score", [P, NT, GROUPS])
    cmp_a = sb("cmp_a", [P, NT, GROUPS, GROUPS])
    cmp_b = sb("cmp_b", [P, NT, GROUPS, GROUPS])
    rank = sb("rank", [P, NT, GROUPS])
    gmask = sb("gmask", [P, NT, GROUPS])
    goff = sb("goff", [P, NT, GROUPS])
    best8 = sb("best8", [P, NT, 8])
    taken = sb("taken", [P, NT, N_EXP])
    sel = sb("sel", [P, NT, N_EXP])
    sel_bf = sb("sel_bf", [P, NT, N_EXP], BF16)
    gsum = sb("gsum", [P, NT])
    ginv = sb("ginv", [P, NT])
    gate = sb("gate", [P, NT, N_EXP])
    gate_part = sb("gate_parts", [P, NT, N_EXP, 3], BF16)
    place = sb("place", [P, NT, N_EXP])
    sh = sb("shared_h", [P, NT, FE])
    ssilu = sb("shared_silu", [P, NT, FE])
    shT = sb("shared_hT", [P, NT, KF, P])
    c1 = sb("over_64", [MAX_OVER, N_EXP])
    c2 = sb("over_128", [MAX_OVER, N_EXP])
    c3 = sb("extra_before", [MAX_OVER, N_EXP])
    table = sb("table", [MAX_OVER, 4])
    table_i = sb("table_i", [MAX_OVER, 4], I32)
    back_i = sb("back_i", [P, MAX_OVER, 4], I32)
    back = sb("back", [P, MAX_OVER, 4])
    shifted = sb("shifted", [P, NT, 2])

    up_ps, turn_ps = k.psum[:, 6, :], k.psum[:, 7, :]

    def up_view(slot, kk):
        return k.w_up[slot][:, :, kk, :]

    def pe_up(slots):
        for kk in range(KD):
            for e in range(2):
                last = nc.tensor.matmul(k.psum[e * SLOTS:(e + 1) * SLOTS, 6, :], xsel[:, kk, e * SLOTS:(e + 1) * SLOTS],
                                        up_view(slots[e], kk), start=kk == 0, stop=kk == KD - 1)
        return last

    def pe_gather(bank, m):
        for c in range(4):
            kk = 4 * (bank - 4) + c
            for i in range(3):
                for t in range(NT):
                    last = nc.tensor.matmul(k.psum[:, bank, c * P:(c + 1) * P], part[i][:, t, kk:D:KD],
                                            m[:, t, :, :].rearrange("p e s -> p (e s)"),
                                            start=i == 0 and t == 0, stop=i == 2 and t == NT - 1)
        return last

    def pe_slot_gates(m, g):
        for e in range(2):
            for t in range(NT):
                last = nc.tensor.matmul(k.psum[e * SLOTS:(e + 1) * SLOTS, 7, 0:3], m[:, t, e, :], g[:, t, e, :],
                                        start=t == 0, stop=t == NT - 1)
        return last

    def pe_turn(m):
        for j in range(KF):
            nc.tensor.transpose(turn_ps[:, j * P:(j + 1) * P], h[:, j * P:(j + 1) * P], k.ident[:])
        for t in range(NT):
            last = nc.tensor.matmul(turn_ps[:, FE + t * P:FE + (t + 1) * P],
                                    m[:, t, :, :].rearrange("p e s -> p (e s)"), k.ident_bf[:], start=True, stop=True)
        return last

    def pe_combine(par, t):
        for half in range(2):
            for o in (high, middle, low):
                last = nc.tensor.matmul(k.psum[:, 2 * t + half, :], matchT[par][:, t * P:(t + 1) * P],
                                        o[:, half * BANK:(half + 1) * BANK], start=False, stop=True,
                                        skip_group_check=True)
        return last

    def pe_down(slots, half, bank):
        for j in range(KF):
            for e in range(2):
                last = nc.tensor.matmul(k.psum[e * SLOTS:(e + 1) * SLOTS, bank, :], hT[:, j * P + e * SLOTS:j * P + (e + 1) * SLOTS],
                                        k.w_down[slots[e]][:, j, half * BANK:(half + 1) * BANK],
                                        start=j == 0, stop=j == KF - 1)
        return last

    def flat(ap):
        return ap.rearrange("p a b -> p (a b)")

    gu, dn = [x.gu0, x.gu1], [x.dn0, x.dn1]

    with nc.Block(no_gpsimd_drain=True) as block:
        @block.sync
        def _(sp):
            for i, src in enumerate((d.ln2_g, d.ln2_b)):
                sp.dma_start(k.ln[:, i, :], src[layer:layer + 1].to_broadcast([P, D])).then_inc(s.tables, 16)
            sp.wait_ge(s.shared_up, NT)
            load_up(sp, k, d, layer, 3, 3, gu[1])
            sp.wait_ge(s.shared_down, NT)
            load_down(sp, k, d, layer, 3, 3, dn[1])
            with sp.Fori(1, PAIRS // 2) as i:
                for par in range(2):
                    sp.wait_ge(s.up, 2 * i + par - 1)
                    for j in range(2):
                        load_up(sp, k, d, layer, 2 * par + j, 4 * i + 2 * par + j, gu[par])
                    sp.wait_ge(s.down_b, 2 * i + par - 1)
                    for j in range(2):
                        load_down(sp, k, d, layer, 2 * par + j, 4 * i + 2 * par + j, dn[par])
            sp.wait_ge(s.table_sb, 1)
            sp.dma_start(k.over_dram, table_i[:]).then_inc(s.table_dram, 16)
            sp.wait_ge(s.table_dram, 16)
            sp.dma_start(back_i[:].rearrange("p b c -> p (b c)"),
                         k.over_dram.rearrange("b c -> (b c)").unsqueeze(0).to_broadcast([P, MAX_OVER * 4])
                         ).then_inc(s.table_back, 16)
            sp.wait_ge(s.table_back, 16)
            n_over = sp.value_load(k.over_dram[0:1, 2:3], min_val=0, max_val=MAX_OVER)
            with sp.If(n_over > 0):
                sp.wait_ge(s.combined, PAIRS)
                with sp.Fori(0, (n_over + 1) // 2) as i:
                    experts = [sp.value_load(k.over_dram[bass.ds(2 * i + j, 1), 0:1], min_val=0,
                                             max_val=N_EXP - 1) for j in range(2)]
                    sp.wait_ge(s.v_combined, i + 1)
                    for j, e in enumerate(experts):
                        load_up(sp, k, d, layer, j, e, s.v_load)
                        load_down(sp, k, d, layer, j, e, s.v_load)
            if out is not None:
                for t in range(NT):
                    sp.wait_ge((s.normed_first, s.normed)[t], 1)
                    sp.dma_start(out[t * P:(t + 1) * P, :], k.x[:, t, :]).then_inc(s.stored, 16)
                sp.wait_ge(s.stored, 16 * NT)

        @block.tensor
        def _(pe):
            transpose_x_tensor(nc, pe, s, k)
            pe.wait_ge(x.router, 32)
            pe.wait_ge(s.xT, KD // 2)
            for kk in range(KD):
                last = nc.tensor.matmul(k.psum[0:N_EXP, 4, 0:S], k.router_w[:, kk, :], k.xT[:, kk, :],
                                        start=kk == 0, stop=kk == KD - 1)
            last.then_inc(s.logits, 1)
            pe.wait_ge(x.shared_w, 16 * 3)
            for t in range(NT):
                for kk in range(KD):
                    last = nc.tensor.matmul(k.psum[:, 5 + t, :], k.xT[:, kk, t * P:(t + 1) * P], up_view(3, kk),
                                            start=kk == 0, stop=kk == KD - 1)
                    if t == 0 and kk == 1:
                        pe.wait_ge(s.score_T, 1)
                        for u in range(NT):
                            turn = nc.tensor.transpose(k.psum[:, 4, S + u * N_EXP:S + (u + 1) * N_EXP],
                                                       score_T[:, u * P:(u + 1) * P], k.ident[0:N_EXP, 0:N_EXP])
                        turn.then_inc(s.score_T_psum, 1)
                last.then_inc(s.shared_up, 1)
            pe.wait_ge(s.selected, 1)
            for t in range(NT):
                nc.tensor.matmul(k.psum[:, 4, t * N_EXP:(t + 1) * N_EXP], k.before_bf[:], sel_bf[:, t, :],
                                 start=True, stop=t == 0)
                if t:
                    nc.tensor.matmul(k.psum[:, 4, t * N_EXP:(t + 1) * N_EXP], k.ones_bf[:], sel_bf[:, 0, :],
                                     start=False, stop=True)
            for t in range(NT):
                last = nc.tensor.matmul(k.psum[0:MAX_OVER, 4, 2 * N_EXP:3 * N_EXP], k.ones_bf[:, 0:MAX_OVER],
                                        sel_bf[:, t, :], start=t == 0, stop=t == NT - 1)
            last.then_inc(s.places, 1)
            pe.wait_ge(s.parts, 1)
            pe.wait_ge(s.routed, 1)
            pe.wait_ge(s.match, 1)
            pe_gather(4, match[0]).then_inc(s.gather_a, 1)
            pe_gather(5, match[0]).then_inc(s.gather_b, 1)
            for t in range(NT):
                pe.wait_ge(s.shared_h, t + 1)
                for j in range(KF):
                    last = nc.tensor.transpose(turn_ps[:, (t * KF + j) * P:(t * KF + j + 1) * P],
                                               sh[:, t, j * P:(j + 1) * P], k.ident[:])
            last.then_inc(s.shared_hT_psum, 1)
            pe.wait_ge(s.shared_hT, 1)
            for t in range(NT):
                for half in range(2):
                    for j in range(KF):
                        last = nc.tensor.matmul(k.psum[:, 2 * t + half, :], shT[:, t, j, :],
                                                k.w_down[3][:, j, half * BANK:(half + 1) * BANK],
                                                start=j == 0, stop=j == KF - 1)
                last.then_inc(s.shared_down, 1)
            pe.wait_ge(s.pair_gates, 1)
            pe_slot_gates(match[0], pair_gates[0]).then_inc(s.slot_gates, 1)

            def pair(p, turn, par, first=False, final=False):
                slots = (2 * par, 2 * par + 1)
                pe.wait_ge(s.xsel_a, p + 1)
                pe.wait_ge(s.xsel_b, p + 1)
                pe.wait_ge(gu[par], 64 * (turn + 1))
                if not first:
                    pe.wait_ge(s.h, p)
                pe_up(slots).then_inc(s.up, 1)
                if not final:
                    pe.wait_ge(s.match, p + 2)
                    pe.wait_ge(s.pair_gates, p + 2)
                    if not first:
                        pe.wait_ge(s.rest_b, p)
                    pe.wait_ge(s.gates_read, p + 1)
                    pe_slot_gates(match[1 - par], pair_gates[1 - par]).then_inc(s.slot_gates, 1)
                    if not first:
                        pe.wait_ge(s.rest_a, p)
                    pe_gather(4, match[1 - par]).then_inc(s.gather_a, 1)
                    pe_gather(5, match[1 - par]).then_inc(s.gather_b, 1)
                    pe.wait_ge(s.gates_read, p + 2)
                else:
                    pe.wait_ge(s.rest_b, p)
                pe.wait_ge(s.h, p + 1)
                pe_turn(match[par]).then_inc(s.turned, 1)
                if not first:
                    pe.wait_ge(s.split, 2 * p)
                    pe_combine(1 - par, 0)
                    pe_combine(1 - par, 1).then_inc(s.combined, 1)
                pe.wait_ge(s.turned_sb, 2 * p + 2)
                pe.wait_ge(dn[par], 32 * (turn + 1))
                if not final:
                    pe.wait_ge(s.xsel_a, p + 2)
                else:
                    pe.wait_ge(s.rest_a, p)
                pe_down(slots, 0, 4).then_inc(s.down_a, 1)
                pe_down(slots, 1, 7).then_inc(s.down_b, 1)

            pair(0, 0, 0, first=True)
            pair(1, 0, 1)
            with pe.Fori(1, PAIRS // 2 - 1) as i:
                pair(2 * i, i, 0)
                pair(2 * i + 1, i, 1)
            pair(PAIRS - 2, PAIRS // 2 - 1, 0)
            pair(PAIRS - 1, PAIRS // 2 - 1, 1, final=True)
            pe.wait_ge(s.table_back, 16)
            n_over = pe.value_load(k.over_dram[0:1, 2:3], min_val=0, max_val=MAX_OVER)
            pe.wait_ge(s.split, 2 * PAIRS)
            for t in range(NT):
                pe_combine(1, t).then_inc(s.combined, 1)
            with pe.If(n_over > 0):
                nc.tensor.transpose(k.psum[:, 6, 0:P], k.ident[:], k.ident[:]).then_inc(s.v_combined, 1)
                with pe.Fori(0, (n_over + 1) // 2) as i:
                    pe.wait_ge(s.v_match, 2 * i + 2)
                    pe_slot_gates(match[0], pair_gates[0])
                    pe_gather(4, match[0])
                    pe_gather(5, match[0]).then_inc(s.v_gather, 1)
                    pe.wait_ge(s.v_xsel_a, i + 1)
                    pe.wait_ge(s.v_xsel_b, i + 1)
                    pe.wait_ge(s.v_load, 96 * i + 96)
                    pe_up((0, 1)).then_inc(s.v_up, 1)
                    pe.wait_ge(s.v_h, i + 1)
                    pe_turn(match[0]).then_inc(s.v_turned, 1)
                    pe.wait_ge(s.v_turned_sb, 2 * i + 2)
                    pe_down((0, 1), 0, 4)
                    pe_down((0, 1), 1, 7).then_inc(s.v_down, 1)
                    pe.wait_ge(s.v_split, i + 1)
                    pe_combine(0, 0)
                    pe_combine(0, 1).then_inc(s.v_combined, 1)
            for t in range(NT):
                nc.tensor.transpose(k.psum[:, 6, 0:P], k.ident[:], k.ident[:]).then_inc(s.y_ready, 1)

        @block.scalar
        def _(act):
            transpose_x_scalar(nc, act, s, k)
            act.wait_ge(s.logits, 1)
            nc.scalar.activation(score_T[:], k.psum[0:N_EXP, 4, 0:S], ACT.Sigmoid).then_inc(s.score_T, 1)
            act.wait_ge(s.score_T_psum, 1)
            nc.scalar.copy(flat(score[:]), k.psum[:, 4, S:S + NT * N_EXP]).then_inc(s.scores, 1)
            for t in range(NT):
                act.wait_ge(s.shared_up, t + 1)
                nc.scalar.activation(ssilu[:, t, :], k.psum[:, 5 + t, 0:FE], ACT.Silu).then_inc(s.shared_silu, 1)
            act.wait_ge(s.gather_a, 1)
            nc.scalar.copy(flat(xsel[:, 0:4, :]), k.psum[:, 4, :]).then_inc(s.xsel_a, 1)

            def pair(p, par, final=False):
                act.wait_ge(s.up, p + 1)
                nc.scalar.activation(silu[:], up_ps[:, 0:FE], ACT.Silu).then_inc(s.silu, 1)
                if not final:
                    act.wait_ge(s.gather_a, p + 2)
                    nc.scalar.copy(flat(xsel[:, 0:4, :]), k.psum[:, 4, :]).then_inc(s.xsel_a, 1)
                act.wait_ge(s.turned, p + 1)
                nc.scalar.copy(hT[:], turn_ps[:, 0:FE]).then_inc(s.turned_sb, 1)
                nc.scalar.copy(matchT[par][:], turn_ps[:, FE:]).then_inc(s.turned_sb, 1)
                act.wait_ge(s.down_a, p + 1)
                nc.scalar.copy(high[:, 0:BANK], k.psum[:, 4, :]).then_inc(s.high_a, 1)
                act.wait_ge(s.down_b, p + 1)
                nc.scalar.copy(high[:, BANK:], turn_ps).then_inc(s.high_b, 1)
                act.wait_ge(s.rest_a, p + 1)
                nc.scalar.copy(middle[:, 0:BANK], out_rest[:, 0:BANK]).then_inc(s.middle, 1)
                act.wait_ge(s.rest_b, p + 1)
                nc.scalar.copy(middle[:, BANK:], out_rest[:, BANK:]).then_inc(s.middle, 1)

            with act.Fori(0, PAIRS // 2 - 1) as i:
                pair(2 * i, 0)
                pair(2 * i + 1, 1)
            pair(PAIRS - 2, 0)
            pair(PAIRS - 1, 1, final=True)

            act.wait_ge(s.table_back, 16)
            n_over = act.value_load(k.over_dram[0:1, 2:3], min_val=0, max_val=MAX_OVER)
            with act.If(n_over > 0):
                with act.Fori(0, (n_over + 1) // 2) as i:
                    act.wait_ge(s.v_gather, i + 1)
                    nc.scalar.copy(flat(xsel[:, 0:4, :]), k.psum[:, 4, :]).then_inc(s.v_xsel_a, 1)
                    act.wait_ge(s.v_up, i + 1)
                    nc.scalar.activation(silu[:], up_ps[:, 0:FE], ACT.Silu).then_inc(s.v_silu, 1)
                    act.wait_ge(s.v_turned, i + 1)
                    nc.scalar.copy(hT[:], turn_ps[:, 0:FE]).then_inc(s.v_turned_sb, 1)
                    nc.scalar.copy(matchT[0][:], turn_ps[:, FE:]).then_inc(s.v_turned_sb, 1)
                    act.wait_ge(s.v_down, i + 1)
                    nc.scalar.copy(high[:, 0:BANK], k.psum[:, 4, :]).then_inc(s.v_high, 1)
                    nc.scalar.copy(high[:, BANK:], turn_ps).then_inc(s.v_high, 1)
            act.wait_ge(s.eps, 1)
            layer_norm_scalar(nc, act, s, w)

        @block.gpsimd
        def _(pool):
            def gates_of(p, par):
                nc.gpsimd.tensor_tensor(pair_gates[par][:], gate_part[:, :, bass.ds(2 * p, 2), :], ones3, ALU.mult
                                        ).then_inc(s.pair_gates, 1)

            def pair(p, par, last_gates=False):
                if not last_gates:
                    pool.wait_ge(s.slot_gates, p + 1)
                    gates_of(p + 2, par)
                for half in range(2):
                    cols = slice(half * BANK, (half + 1) * BANK)
                    pool.wait_ge(s.middle, 2 * p + half + 1)
                    nc.gpsimd.tensor_tensor(low[:, cols], out_rest[:, cols], middle[:, cols], ALU.subtract).then_inc(s.split, 1)

            ones3 = over(over(k.ones_bf[:, 0:3], 1, 2), 1, NT)
            pool.wait_ge(s.gate_parts, 1)
            gates_of(0, 0)
            gates_of(1, 1)
            with pool.Fori(0, PAIRS // 2 - 1) as i:
                pair(2 * i, 0)
                pair(2 * i + 1, 1)
            pair(PAIRS - 2, 0, last_gates=True)
            pair(PAIRS - 1, 1, last_gates=True)
            pool.wait_ge(s.tables, 32)
            layer_norm_gpsimd(nc, pool, s, k, w)

        @block.vector
        def _(dve):
            step = Chain(dve, s.dve)
            nc.vector.memset(w.ln_eps[:], LN_EPS).then_inc(s.eps, 1)
            step(nc.vector.tensor_copy(part[0][:], k.x[:]))
            step(nc.vector.tensor_tensor(rest[:], k.x[:], part[0][:], ALU.subtract))
            step(nc.vector.tensor_copy(part[1][:], rest[:]))
            step(nc.vector.tensor_tensor(rest[:], rest[:], part[1][:], ALU.subtract))
            nc.vector.tensor_copy(part[2][:], rest[:]).then_inc(s.parts, 1)

            def shared_h(t):
                dve.wait_ge(s.shared_silu, t + 1)
                nc.vector.tensor_tensor(sh[:, t, :], ssilu[:, t, :], k.psum[:, 5 + t, FE:2 * FE],
                                        ALU.mult).then_inc(s.shared_h, 1)

            dve.wait_ge(s.scores, 1)
            dve.wait_ge(x.router, 32)
            step(nc.vector.tensor_tensor(biased[:], score[:], over(k.router_b[:], 1, NT), ALU.add))
            for t in range(NT):
                for g in range(GROUPS):
                    last = nc.vector.max(top8[:, t * GROUPS + g, :], biased[:, t, g * GROUP:(g + 1) * GROUP])
            step(last)
            step(nc.vector.tensor_tensor(flat(gscore[:]), top8[:, :, 0], top8[:, :, 1], ALU.add))
            other, own = over(gscore[:], 2, GROUPS), over(gscore[:], 3, GROUPS)
            step(nc.vector.tensor_tensor(cmp_a[:], other, own, ALU.is_gt))
            step(nc.vector.tensor_tensor(cmp_b[:], other, own, ALU.is_equal))
            step(nc.vector.tensor_tensor(cmp_b[:], cmp_b[:], over(k.earlier8[:], 1, NT), ALU.mult))
            step(nc.vector.tensor_tensor(cmp_a[:], cmp_a[:], cmp_b[:], ALU.add))
            step(nc.vector.tensor_reduce(rank[:], cmp_a[:], AX.X, ALU.add))
            step(nc.vector.tensor_scalar(gmask[:], rank[:], TOP_GROUPS - 0.5, None, ALU.is_lt))
            step(nc.vector.tensor_scalar(goff[:], gmask[:], 1.0, -OFF_GROUP, ALU.subtract, ALU.mult))
            grouped = biased[:].rearrange("p t (g e) -> p t g e", g=GROUPS)
            step(nc.vector.tensor_tensor(grouped, grouped, over(gmask[:], 3, GROUP), ALU.mult))
            step(nc.vector.tensor_tensor(grouped, grouped, over(goff[:], 3, GROUP), ALU.add))
            for t in range(NT):
                step(nc.vector.max(best8[:, t, :], biased[:, t, :]))
                step(nc.vector.match_replace(taken[:, t, :], best8[:, t, :], biased[:, t, :], TAKEN))
            step(nc.vector.tensor_tensor(sel[:], biased[:], taken[:], ALU.not_equal))
            nc.vector.tensor_copy(sel_bf[:], sel[:]).then_inc(s.selected, 1)
            step(nc.vector.tensor_tensor(gate[:], score[:], sel[:], ALU.mult))
            step(nc.vector.tensor_reduce(gsum[:], gate[:], AX.X, ALU.add))
            step(nc.vector.reciprocal(ginv[:], gsum[:]))
            for t in range(NT):
                step(nc.vector.tensor_scalar(gate[:, t, :], gate[:, t, :], ginv[:, t:t + 1], ROUTED_SCALE, ALU.mult, ALU.mult))
            step(nc.vector.tensor_copy(gate_part[:, :, :, 0], gate[:]))
            step(nc.vector.tensor_tensor(gate[:], gate[:], gate_part[:, :, :, 0], ALU.subtract))
            step(nc.vector.tensor_copy(gate_part[:, :, :, 1], gate[:]))
            nc.vector.tensor_tensor(gate_part[:, :, :, 2], gate[:], gate_part[:, :, :, 1], ALU.subtract).then_inc(s.gate_parts, 1)
            shared_h(0)
            dve.wait_ge(s.places, 1)
            for t in range(NT):
                step(nc.vector.scalar_tensor_tensor(place[:, t, :], k.psum[:, 4, t * N_EXP:(t + 1) * N_EXP], 1.0,
                                                    sel[:, t, :], ALU.add, ALU.mult))
            count = k.psum[0:MAX_OVER, 4, 2 * N_EXP:3 * N_EXP]
            step(nc.vector.tensor_scalar(c1[:], count, SLOTS + 0.5, None, ALU.is_gt))
            step(nc.vector.tensor_scalar(c2[:], count, 2 * SLOTS + 0.5, None, ALU.is_gt))
            step(nc.vector.tensor_scalar(c3[:], count, 3 * SLOTS + 0.5, None, ALU.is_gt))
            nc.vector.engine_nop().then_inc(s.routed, 1)

            def match_matrix(p, par):
                slot = over(over(k.slot_no[:], 1, 2), 1, NT)
                nc.vector.tensor_tensor(match[par][:], slot, over(place[:, :, bass.ds(2 * p, 2)], 3, SLOTS),
                                        ALU.is_equal).then_inc(s.match, 1)

            match_matrix(0, 0)
            match_matrix(1, 1)
            shared_h(1)
            dve.wait_ge(s.gather_b, 1)
            nc.vector.tensor_copy(flat(xsel[:, 4:8, :]), k.psum[:, 5, :]).then_inc(s.xsel_b, 1)
            dve.wait_ge(s.shared_hT_psum, 1)
            nc.vector.tensor_copy(shT[:].rearrange("p t j c -> p (t j c)"), turn_ps).then_inc(s.shared_hT, 1)
            dve.wait_ge(s.slot_gates, 1)
            nc.vector.tensor_reduce(slot_gate[:], k.psum[:, 7, 0:3], AX.X, ALU.add).then_inc(s.gates_read, 1)
            step(nc.vector.tensor_tensor(c1[:], c1[:], c2[:], ALU.add))
            step(nc.vector.tensor_tensor(c1[:], c1[:], c3[:], ALU.add))
            step(nc.vector.memset(c2[:], 0.0))
            step(nc.vector.tensor_tensor_scan(c3[:], c1[:], c2[:], 0.0, ALU.add, ALU.add))
            step(nc.vector.tensor_copy(table[:, 2:3], c3[:, N_EXP - 1:N_EXP]))
            step(nc.vector.tensor_scalar(c2[:], c3[:], k.pass_no[:, 0:1], None, ALU.is_le))
            step(nc.vector.tensor_reduce(table[:, 0:1], c2[:], AX.X, ALU.add))
            step(nc.vector.tensor_tensor(c1[:], c1[:], c2[:], ALU.mult))
            step(nc.vector.tensor_reduce(table[:, 1:2], c1[:], AX.X, ALU.add))
            step(nc.vector.tensor_tensor(table[:, 1:2], k.pass_no[:, 0:1], table[:, 1:2], ALU.subtract))
            step(nc.vector.tensor_scalar(table[:, 1:2], table[:, 1:2], 1.0, float(SLOTS), ALU.add, ALU.mult))
            step(nc.vector.tensor_scalar(table[:, 3:4], table[:, 0:1], N_EXP - 0.5, 4.0 * S, ALU.is_gt, ALU.mult))
            step(nc.vector.tensor_tensor(table[:, 1:2], table[:, 1:2], table[:, 3:4], ALU.add))
            step(nc.vector.tensor_scalar(table[:, 0:1], table[:, 0:1], N_EXP - 1.0, None, ALU.min))
            nc.vector.tensor_copy(table_i[:], table[:]).then_inc(s.table_sb, 1)

            def pair(p, par, first=False, final=False, last_match=False):
                dve.wait_ge(s.silu, p + 1)
                dve.wait_ge(s.gates_read, p + 1)
                nc.vector.scalar_tensor_tensor(h[:], silu[:], slot_gate[:, 0:1], up_ps[:, FE:2 * FE], ALU.mult,
                                               ALU.mult).then_inc(s.h, 1)
                if not final:
                    dve.wait_ge(s.slot_gates, p + 2)
                    dve.wait_ge(s.h, p + 1)
                    nc.vector.tensor_reduce(slot_gate[:], k.psum[:, 7, 0:3], AX.X, ALU.add).then_inc(s.gates_read, 1)
                    dve.wait_ge(s.gather_b, p + 2)
                    nc.vector.tensor_copy(flat(xsel[:, 4:8, :]), k.psum[:, 5, :]).then_inc(s.xsel_b, 1)
                if not last_match:
                    dve.wait_ge(s.turned, p + 1)
                    match_matrix(p + 2, par)
                if not first:
                    dve.wait_ge(s.split, 2 * p)
                dve.wait_ge(s.high_a, p + 1)
                nc.vector.tensor_tensor(out_rest[:, 0:BANK], k.psum[:, 4, :], high[:, 0:BANK], ALU.subtract).then_inc(s.rest_a, 1)
                dve.wait_ge(s.high_b, p + 1)
                nc.vector.tensor_tensor(out_rest[:, BANK:], turn_ps, high[:, BANK:], ALU.subtract).then_inc(s.rest_b, 1)

            pair(0, 0, first=True)
            pair(1, 1)
            with dve.Fori(1, PAIRS // 2 - 1) as i:
                pair(2 * i, 0)
                pair(2 * i + 1, 1)
            pair(PAIRS - 2, 0, last_match=True)
            pair(PAIRS - 1, 1, final=True, last_match=True)

            dve.wait_ge(s.table_back, 16)
            n_over = dve.value_load(k.over_dram[0:1, 2:3], min_val=0, max_val=MAX_OVER)
            with dve.If(n_over > 0):
                nc.vector.tensor_copy(back[:], back_i[:]).then_inc(s.v_back, 1)
                dve.wait_ge(s.v_back, 1)
                dve.wait_ge(s.combined, PAIRS + 1)
                slot = over(k.slot_no[:], 1, NT)
                with dve.Fori(0, (n_over + 1) // 2) as i:
                    experts = [dve.value_load(k.over_dram[bass.ds(2 * i + j, 1), 0:1], min_val=0,
                                              max_val=N_EXP - 1) for j in range(2)]
                    dve.wait_ge(s.v_combined, i + 1)
                    for j, e in enumerate(experts):
                        nc.vector.tensor_scalar(shifted[:, :, j], place[:, :, bass.ds(e, 1)].rearrange("p t o -> p (t o)"),
                                                back[:, bass.ds(2 * i + j, 1), 1], None, ALU.subtract
                                                ).then_inc(s.v_shifted, 1)
                        dve.wait_ge(s.v_shifted, 4 * i + 2 * j + 1)
                        nc.vector.tensor_tensor(match[0][:, :, j, :], slot, over(shifted[:, :, j], 2, SLOTS),
                                                ALU.is_equal).then_inc(s.v_shifted, 1)
                        dve.wait_ge(s.v_shifted, 4 * i + 2 * j + 2)
                        nc.vector.tensor_tensor(pair_gates[0][:, :, j, :],
                                                gate_part[:, :, bass.ds(e, 1), :].rearrange("p t o c -> p t (o c)"),
                                                over(k.ones_bf[:, 0:3], 1, NT), ALU.mult).then_inc(s.v_match, 1)
                    dve.wait_ge(s.v_gather, i + 1)
                    nc.vector.tensor_reduce(slot_gate[:], k.psum[:, 7, 0:3], AX.X, ALU.add).then_inc(s.v_gates_read, 1)
                    nc.vector.tensor_copy(flat(xsel[:, 4:8, :]), k.psum[:, 5, :]).then_inc(s.v_xsel_b, 1)
                    dve.wait_ge(s.v_silu, i + 1)
                    dve.wait_ge(s.v_gates_read, i + 1)
                    nc.vector.scalar_tensor_tensor(h[:], silu[:], slot_gate[:, 0:1], up_ps[:, FE:2 * FE], ALU.mult,
                                                   ALU.mult).then_inc(s.v_h, 1)
                    dve.wait_ge(s.v_high, 2 * i + 2)
                    nc.vector.tensor_tensor(out_rest[:, 0:BANK], k.psum[:, 4, :], high[:, 0:BANK], ALU.subtract).then_inc(s.v_rest, 1)
                    nc.vector.tensor_tensor(out_rest[:, BANK:], turn_ps, high[:, BANK:], ALU.subtract).then_inc(s.v_rest, 1)
                    dve.wait_ge(s.v_rest, 2 * i + 2)
                    nc.vector.tensor_copy(middle[:], out_rest[:]).then_inc(s.v_middle, 1)
                    dve.wait_ge(s.v_middle, i + 1)
                    nc.vector.tensor_tensor(low[:], out_rest[:], middle[:], ALU.subtract).then_inc(s.v_split, 1)
            dve.wait_ge(s.tables, 32)
            layer_norm_vector(nc, dve, step, s, k, w, s.y_ready, together=True)
    ctx.close()



def flat(ap):
    return ap.rearrange("p a b -> p (a b)")


EV_LAT = Q_LORA + KV_LORA + MLA_R
EV_G = EV_LAT
EV_GATES = EV_G + 3 * GH * GD
EV_Z = EV_GATES + 2 * GH
G_CHUNKS = 3 * GH
PAD = CONV_W - 1
TWO_PI_HIGH, TWO_PI_MID = 6.28125, 0.0019350051879882812
TWO_PI_LOW = float(2 * np.pi - TWO_PI_HIGH - TWO_PI_MID)
ROUND = 1.5 * 2.0 ** 23


def columns_of(k, slot):
    return k.w_up[slot][:].rearrange("p a k f -> p (a k f)").rearrange("p (k n) -> p k n", k=KD)


def even_project(nc, k, d, e):
    ctx = ExitStack()
    s = semaphores(ctx, nc, "evp", "x small w0 w1 w2 w3 wz xT_psum xT vec rows_T rows lat_psum lat g_psum tap conv "
                                   "conv_done g z_psum z pool freq angle sines zero_pad")

    def sb(name, shape, dt=F32):
        return ctx.enter_context(nc.sbuf_tensor(f"evp_{name}", shape, dt))

    rows = sb("row_vectors", [CONV_W * G_CHUNKS + 3, P])
    raw = sb("raw", [P, G_CHUNKS, PAD + S])
    acc = sb("acc", [P, 2, S])
    pos_i = sb("pos_i", [P, NT], I32)
    pos = sb("pos", [P, NT])
    freq = sb("freq", [P, (MLA_R + WD) // 2])
    ang = sb("ang", [P, NT, (MLA_R + WD) // 2])
    turns = sb("turns", [P, NT, (MLA_R + WD) // 2])
    n_conv = CONV_W * G_CHUNKS
    win = d.ev_w_in[0].rearrange("(p k) n -> p k n", k=KD)

    with nc.Block(no_gpsimd_drain=True) as block:
        @block.sync
        def _(sp):
            sp.dma_start(k.x[:], d.x.rearrange("b (t p) n -> p (b t) n", p=P)).then_inc(s.x, 16)
            w0 = columns_of(k, 0)
            sp.dma_start(w0[:, :, 0:EV_LAT], win[:, :, 0:EV_LAT]).then_inc(s.w0, 16)
            sp.dma_start(w0[:, :, EV_LAT:EV_LAT + 2 * GH], win[:, :, EV_GATES:EV_Z]).then_inc(s.w0, 16)
            sp.dma_start(rows[0:n_conv, :], d.gdn_conv[0].rearrange("w (c p) -> (w c) p", p=P)).then_inc(s.small, 16)
            sp.dma_start(rows[n_conv:n_conv + 2, :], d.mla_q_norm[0].rearrange("(c p) -> c p", p=P)).then_inc(s.small, 16)
            sp.dma_start(rows[n_conv + 2:n_conv + 3, :], d.mla_kv_norm).then_inc(s.small, 16)
            with nc.allow_non_contiguous_dma(reason="256 positions"):
                sp.dma_start(pos_i[:], d.positions.rearrange("b (t p) -> p (b t)", p=P)).then_inc(s.small, 16)
            for i, sem in enumerate((s.w1, s.w2, s.w3)):
                sp.dma_start(columns_of(k, 1 + i), win[:, :, EV_G + i * GH * GD:EV_G + (i + 1) * GH * GD]).then_inc(sem, 16)
            sp.wait_ge(s.lat_psum, NT)
            sp.dma_start(columns_of(k, 0), win[:, :, EV_Z:EV_Z + GH * GD]).then_inc(s.wz, 16)
            sp.dma_start(k.w_down[2][:].rearrange("p j n -> p (j n)")[:, 0:2 * MLA_H * MLA_QK].rearrange("p (c n) -> p c n", c=2),
                         d.mla_w_qb[0].rearrange("(c p) n -> p c n", p=P)).then_inc(k.s_mla_w, 16)
            sp.dma_start(k.w_down[3][:, 0, :], d.mla_w_kvb[0]).then_inc(k.s_mla_w, 16)

        @block.gpsimd
        def _(pool):
            half_m, half_s = MLA_R // 2, WD // 2
            for i in range(half_m):
                nc.gpsimd.memset(freq[:, i:i + 1], float(np.float32(ROPE_THETA) ** -np.float32(2 * i / MLA_R)))
            for i in range(half_s):
                last = nc.gpsimd.memset(freq[:, half_m + i:half_m + i + 1],
                                        float(np.float32(ROPE_THETA) ** -np.float32(2 * i / WD)))
            last.then_inc(s.freq, 1)

        @block.tensor
        def _(pe):
            pe.wait_ge(s.x, 16)
            transpose_x_tensor(nc, pe, s, k)
            pe.wait_ge(s.small, 64)
            nr = n_conv + 3
            nc.tensor.transpose(k.psum[:, 4, 0:nr], rows[:, :], k.ident[0:nr, 0:nr]).then_inc(s.rows_T, 1)
            pe.wait_ge(s.w0, 32)
            pe.wait_ge(s.xT, KD // 2)
            w = columns_of(k, 0)
            for t in range(NT):
                for kk in range(KD):
                    last = nc.tensor.matmul(k.psum[:, 5 + t, 0:EV_LAT + 2 * GH], k.xT[:, kk, t * P:(t + 1) * P],
                                            w[:, kk, 0:EV_LAT + 2 * GH], start=kk == 0, stop=kk == KD - 1)
                last.then_inc(s.lat_psum, 1)
            for c in range(G_CHUNKS):
                pe.wait_ge((s.w1, s.w2, s.w3)[c // GH], 16)
                if c >= 4:
                    pe.wait_ge(s.tap, c - 3)
                w = columns_of(k, 1 + c // GH)
                for kk in range(KD):
                    last = nc.tensor.matmul(k.psum[:, c % 4, 0:S], w[:, kk, (c % GH) * P:(c % GH + 1) * P], k.xT[:, kk, :],
                                            start=kk == 0, stop=kk == KD - 1)
                last.then_inc(s.g_psum, 1)
            pe.wait_ge(s.wz, 16)
            pe.wait_ge(s.lat, NT)
            w = columns_of(k, 0)
            for t in range(NT):
                for kk in range(KD):
                    last = nc.tensor.matmul(k.psum[:, 5 + t, :], k.xT[:, kk, t * P:(t + 1) * P], w[:, kk, :],
                                            start=kk == 0, stop=kk == KD - 1)
                last.then_inc(s.z_psum, 1)

        @block.scalar
        def _(act):
            transpose_x_scalar(nc, act, s, k)
            act.wait_ge(s.rows_T, 1)
            nc.scalar.copy(e.cols[:], k.psum[:, 4, 0:n_conv + 3]).then_inc(s.rows, 1)
            for t in range(NT):
                act.wait_ge(s.lat_psum, t + 1)
                nc.scalar.copy(e.lat[:, t, :], k.psum[:, 5 + t, 0:EV_LAT + 2 * GH]).then_inc(s.lat, 1)
            act.wait_ge(s.angle, 2)
            nc.scalar.activation(flat(k.sin[:]), flat(ang[:]), ACT.Sin).then_inc(s.sines, 1)
            nc.scalar.activation(flat(k.cos[:]), flat(turns[:]), ACT.Sin, bias=k.eps[:, 1:2], scale=-1.0).then_inc(s.sines, 1)
            for c in range(G_CHUNKS):
                act.wait_ge(s.g_psum, c + 1)
                nc.scalar.copy(raw[:, c, PAD:], k.psum[:, c % 4, 0:S]).then_inc(s.tap, 1)
                if c >= 1:
                    act.wait_ge(s.conv, c)
                    nc.scalar.activation(e.gT[:, c - 1, :], acc[:, (c - 1) % 2, :], ACT.Silu).then_inc(s.g, 1)
            act.wait_ge(s.conv, G_CHUNKS)
            nc.scalar.activation(e.gT[:, G_CHUNKS - 1, :], acc[:, (G_CHUNKS - 1) % 2, :], ACT.Silu).then_inc(s.g, 1)
            for t in range(NT):
                act.wait_ge(s.z_psum, t + 1)
                nc.scalar.activation(e.z[:, t, :], k.psum[:, 5 + t, :], ACT.Silu).then_inc(s.z, 1)

        @block.vector
        def _(dve):
            step = Chain(dve, s.vec)
            step(nc.vector.memset(raw[:, :, 0:PAD], 0.0))
            dve.wait_ge(s.small, 64)
            dve.wait_ge(s.freq, 1)
            step(nc.vector.tensor_copy(pos[:], pos_i[:]))
            for t in range(NT):
                step(nc.vector.tensor_scalar(ang[:, t, :], freq[:], pos[:, t:t + 1], None, ALU.mult))
            a, n = flat(ang[:]), flat(turns[:])
            step(nc.vector.tensor_scalar(n, a, float(1 / (2 * np.pi)), None, ALU.mult))
            step(nc.vector.tensor_scalar(n, n, ROUND, None, ALU.add))
            step(nc.vector.tensor_scalar(n, n, ROUND, None, ALU.subtract))
            for part in (TWO_PI_HIGH, TWO_PI_MID, TWO_PI_LOW):
                step(nc.vector.scalar_tensor_tensor(a, n, -part, a, ALU.mult, ALU.add))
            step(nc.vector.tensor_scalar(a, a, 3.1415925, -3.1415925, ALU.min, ALU.max))
            nc.vector.engine_nop().then_inc(s.angle, 1)
            nc.vector.scalar_tensor_tensor(n, a, -1.0, a, ALU.mult, ALU.max).then_inc(s.angle, 1)
            dve.wait_ge(s.rows, 1)
            for c in range(G_CHUNKS):
                dve.wait_ge(s.tap, c + 1)
                if c >= 2:
                    dve.wait_ge(s.g, c - 1)
                y = acc[:, c % 2, :]
                step(nc.vector.tensor_scalar(y, raw[:, c, 0:S], e.cols[:, c:c + 1], None, ALU.mult))
                for i in range(1, CONV_W):
                    last = nc.vector.scalar_tensor_tensor(y, raw[:, c, i:i + S], e.cols[:, i * G_CHUNKS + c:i * G_CHUNKS + c + 1],
                                                          y, ALU.mult, ALU.add)
                    if i < CONV_W - 1:
                        step(last)
                    else:
                        last.then_inc(s.conv, 1)
    ctx.close()



HEADS, HV = 8, 64


def attention_tensor(nc, pe, s, k, a):
    for t in range(NT):
        keys = (t + 1) * P
        for b in range(4):
            pe.wait_ge(s.qT, b + 1)
            pe.wait_ge(s.kT, b + 1)
            if t:
                pe.wait_ge(s.masked, b + 1)
            for i in range(2):
                last = nc.tensor.matmul(k.psum[:, 4 + b, i * S:i * S + keys], a.qT(2 * b + i, t),
                                        a.kT(2 * b + i, keys), start=True, stop=True)
            last.then_inc(s.scores, 1)
        for half in range(2):
            pe.wait_ge(s.scaled, 8 * t + 4 * half + 4)
            if t:
                pe.wait_ge(s.mixed, half + 1)
            for kt in range(t + 1):
                for i in range(4):
                    last = nc.tensor.transpose(k.psum[:, 2 * half + kt, i * P:(i + 1) * P],
                                               a.pr[:, 4 * half + i, kt * P:(kt + 1) * P], k.ident[:])
            last.then_inc(s.turned, 1)
        for half in range(2):
            pe.wait_ge(s.pT, half + 1 if t == 0 else 4 + 2 * half)
            for b in range(2):
                for i in range(2):
                    for kt in range(t + 1):
                        last = nc.tensor.matmul(k.psum[i * HV:(i + 1) * HV, 2 * half, b * P:(b + 1) * P],
                                                a.v(4 * half + 2 * b + i, kt),
                                                a.pT[:, half, kt, (2 * b + i) * P:(2 * b + i + 1) * P],
                                                start=kt == 0, stop=kt == t)
            last.then_inc(s.done, 1)


def attention_scalar(nc, act, s, k, a):
    for t in range(NT):
        keys = (t + 1) * P
        act.wait_ge(s.max, t + 1)
        for h in range(HEADS):
            nc.scalar.activation(a.pr[:, h, 0:keys], a.pr[:, h, 0:keys], ACT.Exp, bias=a.nb[:, h:h + 1], scale=a.scale,
                                 accum_out=a.den[:, h:h + 1]).then_inc(s.probs, 1)
        if a.sinks is not None:
            act.wait_ge(s.sunk, t + 1)
            nc.scalar.activation(a.sunk[:], a.sunk[:], ACT.Exp).then_inc(s.sink_exp, 1)
        for half in range(2):
            act.wait_ge(s.turned, 2 * t + half + 1)
            if t:
                act.wait_ge(s.done, half + 1)
            for kt in range(t + 1):
                nc.scalar.copy(a.pT[:, half, kt, :], k.psum[:, 2 * half + kt, :]).then_inc(s.pT, 1)


def attention_vector(nc, dve, step, s, k, a):
    for t in range(NT):
        keys = (t + 1) * P
        for b in range(4):
            dve.wait_ge(s.scores, 4 * t + b + 1)
            if t:
                dve.wait_ge(s.turned, 2)
            nc.vector.tensor_tensor(a.pr[:, 2 * b:2 * b + 2, 0:keys],
                                    k.psum[:, 4 + b, :].rearrange("p (h c) -> p h c", h=2)[:, :, 0:keys],
                                    over(a.mask[:, 2 * P - keys:], 1, 2), ALU.add).then_inc(s.masked, 1)
        dve.wait_ge(s.masked, 4 * t + 4)
        step(nc.vector.tensor_reduce(a.mx[:], a.pr[:, :, 0:keys], AX.X, ALU.max))
        if a.sinks is None:
            nc.vector.tensor_scalar(a.nb[:], a.mx[:], -a.scale, None, ALU.mult).then_inc(s.max, 1)
        else:
            step(nc.vector.scalar_tensor_tensor(a.mx[:], a.mx[:], a.scale, a.sinks[:], ALU.mult, ALU.max))
            nc.vector.tensor_scalar(a.nb[:], a.mx[:], -1.0, None, ALU.mult).then_inc(s.max, 1)
            nc.vector.tensor_tensor(a.sunk[:], a.sinks[:], a.mx[:], ALU.subtract).then_inc(s.sunk, 1)
        for half in range(2):
            hs = slice(4 * half, 4 * half + 4)
            dve.wait_ge(s.probs, 8 * t + 4 * half + 4)
            if a.sinks is not None:
                dve.wait_ge(s.sink_exp, t + 1)
                step(nc.vector.tensor_tensor(a.den[:, hs], a.den[:, hs], a.sunk[:, hs], ALU.add))
            step(nc.vector.reciprocal(a.dinv[:, hs], a.den[:, hs]))
            for h in range(4 * half, 4 * half + 4):
                nc.vector.tensor_scalar(a.pr[:, h, 0:keys], a.pr[:, h, 0:keys], a.dinv[:, h:h + 1], None,
                                        ALU.mult).then_inc(s.scaled, 1)
        for half in range(2):
            dve.wait_ge(s.done, 2 * t + half + 1)
            nc.vector.tensor_copy(k.mixT[:, a.chunk + 2 * half:a.chunk + 2 * half + 2, t * P:(t + 1) * P],
                                  k.psum[:, 2 * half, 0:2 * P].rearrange("p (b c) -> p b c", b=2)).then_inc(s.mixed, 1)


def rope(nc, step, tmp, first, second, out1, out2, c, sn):
    n = first.shape[1]
    t1, t2, t3, t4 = (x[:, 0:n, :] for x in tmp)
    cc, ss = over(c, 1, n), over(sn, 1, n)
    step(nc.vector.tensor_tensor(t1, first, cc, ALU.mult))
    step(nc.vector.tensor_tensor(t2, second, ss, ALU.mult))
    step(nc.vector.tensor_tensor(t3, second, cc, ALU.mult))
    step(nc.vector.tensor_tensor(t4, first, ss, ALU.mult))
    step(nc.vector.tensor_tensor(out1, t1, t2, ALU.subtract))
    step(nc.vector.tensor_tensor(out2, t3, t4, ALU.add))



def even_latent_attention(nc, k, d, e, x):
    ctx = ExitStack()
    s = semaphores(ctx, nc, "mla", "vec act sumsq root normed latT_psum latT_q latT_kv q_psum kv_psum q_sb kv_sb kv_freed q_ready k_ready "
                                   "qT_psum kT_psum qT kT scores masked max probs scaled turned pT mixed done act_ssq")

    def sb(name, shape, dt=F32):
        return ctx.enter_context(nc.sbuf_tensor(f"mla_{name}", shape, dt))

    H, QK, HR = MLA_H, MLA_QK, MLA_R // 2
    junk = sb("junk", [P, Q_LORA])
    ssq = sb("ssq", [P, NT, 2])
    root = sb("root", [P, NT, 2])
    rinv = sb("rinv", [P, NT, 2])
    latT = sb("latT", [P, 3, S])
    qk = sb("qk", [P, 2 * NT * H * QK])
    q = qk[:, 0:NT * H * QK].rearrange("p (t h c) -> p t h c", t=NT, h=H)
    kc = qk[:, NT * H * QK:].rearrange("p (t h c) -> p t h c", t=NT, h=H)
    v = sb("v", [P, NT, H, MLA_V])
    tmp = [sb(f"tmp{i}", [P, H, HR]) for i in range(4)]
    krot = sb("krot", [P, NT, MLA_R])
    qT = sb("qT", [QK, H, S])
    kT = sb("kT", [QK, H, S])
    pr = qk[:, 0:H * S].rearrange("p (h c) -> p h c", h=H)
    pT = sb("pT", [P, 2, 2, H // 2 * P])
    mx = sb("max", [P, H])
    nb = sb("negmax", [P, H])
    den = sb("den", [P, H])
    dinv = sb("dinv", [P, H])
    scale = float(QK ** -0.5)
    a = named(pr=pr, pT=pT, mx=mx, nb=nb, den=den, dinv=dinv, scale=scale, mask=k.no_later, sinks=None, chunk=0,
                        qT=lambda h, t: qT[:, h, t * P:(t + 1) * P], kT=lambda h, keys: kT[:, h, 0:keys],
                        v=lambda h, kt: v[:, kt, h, :])
    wq = k.w_down[2][:].rearrange("p j n -> p (j n)")[:, 0:2 * H * QK].rearrange("p (c n) -> p c n", c=2)
    wkv = k.w_down[3][:, 0, :]
    n_conv = CONV_W * G_CHUNKS

    with nc.Block(no_gpsimd_drain=True) as block:
        @block.sync
        def _(sp):
            for half in range(2):
                sp.dma_start(columns_of(k, 2 + half),
                             d.ev_w_out[0][:, half * BANK:(half + 1) * BANK].rearrange("(c p) n -> p c n", p=P)).then_inc(k.s_out_w, 16)
            for i, src in enumerate((d.ln1_g, d.ln1_b)):
                sp.dma_start(k.ln[:, i, :], src[0:1].to_broadcast([P, D])).then_inc(k.s_out_w, 16)
            sp.dma_start(e.o_gain[:], d.gdn_norm.to_broadcast([P, GD])).then_inc(k.s_gdn_w, 16)
            sp.dma_start(e.a_log[:], d.gdn_a_log.to_broadcast([P, GH])).then_inc(k.s_gdn_w, 16)
            sp.dma_start(e.dt_bias[:], d.gdn_dt_bias.to_broadcast([P, GH])).then_inc(k.s_gdn_w, 16)
            load_early_experts(sp, k, d, 0, x, lambda e: None)

        @block.scalar
        def _(act):
            for t in range(NT):
                nc.scalar.activation(junk[:], e.lat[:, t, 0:Q_LORA], ACT.Square, accum_out=ssq[:, t, 0:1]).then_inc(s.act_ssq, 1)
                act.wait_ge(s.act_ssq, 2 * t + 1)
                nc.scalar.activation(junk[:, 0:KV_LORA], e.lat[:, t, Q_LORA:Q_LORA + KV_LORA], ACT.Square,
                                     accum_out=ssq[:, t, 1:2]).then_inc(s.act_ssq, 1)
                act.wait_ge(s.act_ssq, 2 * t + 2)
            nc.scalar.activation(root[:, :, 0], ssq[:, :, 0], ACT.Sqrt, bias=k.eps[:, 0:1], scale=1.0 / Q_LORA).then_inc(s.root, 1)
            nc.scalar.activation(root[:, :, 1], ssq[:, :, 1], ACT.Sqrt, bias=k.eps[:, 0:1], scale=1.0 / KV_LORA).then_inc(s.root, 1)
            act.wait_ge(s.latT_psum, 1)
            for c in range(2):
                nc.scalar.activation(latT[:, c, :], k.psum[:, 0, c * S:(c + 1) * S], ACT.Copy,
                                     scale=e.cols[:, n_conv + c:n_conv + c + 1]).then_inc(s.latT_q, 1)
            nc.scalar.activation(latT[:, 2, :], k.psum[:, 1, 0:S], ACT.Copy,
                                 scale=e.cols[:, n_conv + 2:n_conv + 3]).then_inc(s.latT_kv, 1)
            for t in range(NT):
                act.wait_ge(s.q_psum, t + 1)
                for half in range(2):
                    nc.scalar.copy(q[:, t, 4 * half:4 * half + 4, :].rearrange("p h c -> p (h c)"),
                                   k.psum[:, 2 + 2 * t + half, 0:H * QK // 2]).then_inc(s.q_sb, 1)
                act.wait_ge(s.kv_psum, t + 1)
                for half in range(2):
                    bank = (6 if t == 0 else 0) + half
                    both = k.psum[:, bank, :].rearrange("p (h c) -> p h c", c=MLA_N + MLA_V)
                    nc.scalar.copy(kc[:, t, 4 * half:4 * half + 4, 0:MLA_N], both[:, :, 0:MLA_N]).then_inc(s.kv_sb, 1)
                    nc.scalar.copy(v[:, t, 4 * half:4 * half + 4, :], both[:, :, MLA_N:]).then_inc(s.kv_sb, 1)
            for b in range(4):
                act.wait_ge(s.qT_psum, b + 1)
                nc.scalar.copy(qT[:, 2 * b:2 * b + 2, :].rearrange("p h c -> p (h c)"), k.psum[0:QK, b, :]).then_inc(s.qT, 1)
            attention_scalar(nc, act, s, k, a)

        @block.tensor
        def _(pe):
            pe.wait_ge(s.normed, 1)
            for c in range(3):
                for t in range(NT):
                    last = nc.tensor.transpose(k.psum[:, c // 2, (c % 2) * S + t * P:(c % 2) * S + (t + 1) * P],
                                               e.lat[:, t, c * P:(c + 1) * P], k.ident[:])
            last.then_inc(s.latT_psum, 1)
            pe.wait_ge(k.s_mla_w, 32)
            pe.wait_ge(s.latT_q, 2)
            pe.wait_ge(s.latT_kv, 1)
            for t in range(NT):
                for half in range(2):
                    for c in range(2):
                        last = nc.tensor.matmul(k.psum[:, 2 + 2 * t + half, 0:H * QK // 2], latT[:, c, t * P:(t + 1) * P],
                                                wq[:, c, half * H * QK // 2:(half + 1) * H * QK // 2], start=c == 0, stop=c == 1)
                last.then_inc(s.q_psum, 1)
                for half in range(2):
                    last = nc.tensor.matmul(k.psum[:, (6 if t == 0 else 0) + half, :], latT[:, 2, t * P:(t + 1) * P],
                                            wkv[:, half * BANK:(half + 1) * BANK], start=True, stop=True)
                last.then_inc(s.kv_psum, 1)
            pe.wait_ge(s.kv_sb, 8)
            pe.wait_ge(s.q_ready, 1)
            for b in range(4):
                for i in range(2):
                    for t in range(NT):
                        last = nc.tensor.transpose(k.psum[0:QK, b, i * S + t * P:i * S + (t + 1) * P], q[:, t, 2 * b + i, :], k.ident[:])
                last.then_inc(s.qT_psum, 1)
            pe.wait_ge(s.k_ready, 1)
            for b in range(4):
                for i in range(2):
                    for t in range(NT):
                        last = nc.tensor.transpose(k.psum[0:QK, 4 + b, i * S + t * P:i * S + (t + 1) * P], kc[:, t, 2 * b + i, :], k.ident[:])
                last.then_inc(s.kT_psum, 1)
            attention_tensor(nc, pe, s, k, a)

        @block.vector
        def _(dve):
            step = Chain(dve, s.vec)
            dve.wait_ge(s.root, 2)
            step(nc.vector.reciprocal(flat(rinv[:]), flat(root[:])))
            for t in range(NT):
                step(nc.vector.tensor_scalar(e.lat[:, t, 0:Q_LORA], e.lat[:, t, 0:Q_LORA], rinv[:, t, 0:1], None, ALU.mult))
                step(nc.vector.tensor_scalar(e.lat[:, t, Q_LORA:Q_LORA + KV_LORA], e.lat[:, t, Q_LORA:Q_LORA + KV_LORA],
                                             rinv[:, t, 1:2], None, ALU.mult))
            nc.vector.engine_nop().then_inc(s.normed, 1)
            k0 = Q_LORA + KV_LORA
            for t in range(NT):
                rope(nc, step, tmp, e.lat[:, t:t + 1, k0:k0 + HR], e.lat[:, t:t + 1, k0 + HR:k0 + MLA_R],
                     krot[:, t:t + 1, 0:HR], krot[:, t:t + 1, HR:], k.cos[:, t, 0:HR], k.sin[:, t, 0:HR])
            for t in range(NT):
                step(nc.vector.tensor_copy(kc[:, t, :, MLA_N:], over(krot[:, t, :], 1, H)))
            nc.vector.engine_nop().then_inc(s.k_ready, 1)
            for t in range(NT):
                dve.wait_ge(s.q_sb, 2 * t + 2)
                r1, r2 = q[:, t, :, MLA_N:MLA_N + HR], q[:, t, :, MLA_N + HR:]
                rope(nc, step, tmp, r1, r2, r1, r2, k.cos[:, t, 0:HR], k.sin[:, t, 0:HR])
            nc.vector.engine_nop().then_inc(s.q_ready, 1)
            for b in range(4):
                dve.wait_ge(s.kT_psum, b + 1)
                nc.vector.tensor_copy(kT[:, 2 * b:2 * b + 2, :].rearrange("p h c -> p (h c)"), k.psum[0:QK, 4 + b, :]).then_inc(s.kT, 1)
            attention_vector(nc, dve, step, s, k, a)
    ctx.close()



def log1p_exp_vector(nc, dve, step, s, x, out, w):
    step(nc.vector.scalar_tensor_tensor(w.mag, x, -1.0, x, ALU.mult, ALU.max))
    nc.vector.engine_nop().then_inc(s.mag, 1)
    dve.wait_ge(s.exp_mag, 1)
    step(nc.vector.tensor_scalar(w.u, w.t, 1.0, None, ALU.add))
    nc.vector.engine_nop().then_inc(s.one_more, 1)
    step(nc.vector.tensor_scalar(w.d, w.u, 1.0, None, ALU.subtract))
    step(nc.vector.tensor_scalar(w.tiny, w.d, 0.0, None, ALU.is_equal))
    step(nc.vector.tensor_tensor(w.d, w.d, w.tiny, ALU.add))
    step(nc.vector.reciprocal(w.d, w.d))
    step(nc.vector.tensor_tensor(w.tiny, w.tiny, w.t, ALU.mult))
    dve.wait_ge(s.log_u, 1)
    step(nc.vector.tensor_tensor(out, w.log, w.t, ALU.mult))
    step(nc.vector.tensor_tensor(out, out, w.d, ALU.mult))
    step(nc.vector.tensor_tensor(out, out, w.tiny, ALU.add))


def log1p_exp_scalar(nc, act, s, w):
    act.wait_ge(s.mag, 1)
    nc.scalar.activation(w.t, w.mag, ACT.Exp, scale=-1.0).then_inc(s.exp_mag, 1)
    act.wait_ge(s.one_more, 1)
    nc.scalar.activation(w.log, w.u, ACT.Ln).then_inc(s.log_u, 1)


def even_delta_net(nc, k, e):
    ctx = ExitStack()
    s = semaphores(ctx, nc, "gdn", "vec mag exp_mag one_more log_u beta_exp gates wide cum_psum cum exps cumrow decay_in decay "
                                   "nat_psum nat ssq root scaled extra T_psum T_a T_v pair_psum lower prod sub_v sub_a "
                                   "v0 w1 vn0 nw1 st_psum st o0 vn1_psum vn1 o1 o_sb ssq_o root_o on onT onT_sb mixed "
                                   "variance root_ln normed eps alog")

    def sb(name, shape, dt=F32):
        return ctx.enter_context(nc.sbuf_tensor(f"gdn_{name}", shape, dt))

    H, C = GH, GH * GD
    beta, decay = e.lat[:, :, EV_LAT:EV_LAT + H], e.lat[:, :, EV_LAT + H:EV_LAT + 2 * H]
    small = {n: sb(n, [P, NT, H]) for n in ("x", "lp", "beta", "g", "cum", "last", "e_cum", "e_left", "mag", "t", "u", "d", "tiny", "log", "tb")}
    w = named(**{n: small[n][:] for n in small})
    ea = sb("ea", [P, H])
    D_t = sb("decay_t", [P, NT, C])
    Dn = sb("decay_n", [P, NT, C])
    q, kk_, v = (sb(n, [P, NT, C]) for n in ("q", "k", "v"))
    kb = sb("kb", [P, NT, C])
    qg1, kg0, kbg1 = (sb(n, [P, C]) for n in ("qg1", "kg0", "kbg1"))
    qgT1 = sb("qgT1", [P, H, GD])
    ssq = sb("ssq", [P, 2, NT, H])
    rs = sb("rs", [P, 2, NT, H])
    A, B, Cm, Z = (sb(n, [P, NT, C]) for n in ("ma", "mb", "mc", "mz"))
    Lo, AT = (k.xT[:, 4 * i:4 * i + 4, :].rearrange("p c t -> p (c t)").rearrange("p (t c) -> p t c", t=NT)
              for i in range(2))
    wide = Cm
    blk = sb("block8_before", [P, P])
    vn, o = D_t, Dn
    nw1 = qg1
    st = sb("state", [P, C])
    qT, kT, kbT = e.gT[:, 0:H, :], e.gT[:, H:2 * H, :], e.gT[:, 2 * H:3 * H, :]
    heads = lambda ap: ap.rearrange("p (h c) -> p h c", h=H)
    bank = lambda b: k.psum[:, b, :]
    per_head = lambda ap: over(ap, 2, GD)
    V_STAGES, A_STAGES = (1, 2, 3, 4, 5, 6, 7, 8), (1, 2, 4, 5, 6, 7, 9)

    def reached(stages, m, t):
        return NT * sum(1 for x in stages if x < m) + t + 1

    with nc.Block(no_gpsimd_drain=True) as block:
        @block.tensor
        def _(pe):
            for i in range(3):
                for t in range(NT):
                    for h in range(H):
                        last = nc.tensor.transpose(k.psum[:, 2 + 2 * i + t, h * P:(h + 1) * P],
                                                   e.gT[:, i * H + h, t * P:(t + 1) * P], k.ident[:])
                    last.then_inc(s.nat_psum, 1)
            pe.wait_ge(s.gates, 1)
            for t in range(NT):
                nc.tensor.matmul(k.psum[:, 0, t * H:(t + 1) * H], k.upto[:], w.g[:, t, :], start=True, stop=True)
                last = nc.tensor.matmul(k.psum[:, 0, (NT + t) * H:(NT + t + 1) * H], k.ones[:], w.g[:, t, :],
                                        start=True, stop=True)
            last.then_inc(s.cum_psum, 1)
            pe.wait_ge(s.wide, 1)
            pe.wait_ge(s.cum, 1)
            for t in range(NT):
                for h in range(H):
                    last = nc.tensor.matmul(k.psum[:, 1 - t, h * P:(h + 1) * P], wide[:, t, h * P:(h + 1) * P], k.upto[:],
                                            start=True, stop=True)
                last.then_inc(s.cumrow, 1)
            pe.wait_ge(s.nat, 6)
            for i, src in enumerate((q, kk_, kb)):
                pe.wait_ge(s.scaled, i + 1)
                for t in range(NT):
                    for h in range(H):
                        last = nc.tensor.transpose(k.psum[:, 2 + 2 * i + t, h * P:(h + 1) * P],
                                                   src[:, t, h * P:(h + 1) * P], k.ident[:])
                    last.then_inc(s.T_psum, 1)
            pe.wait_ge(s.extra, 1)
            pe.wait_ge(s.decay_in, NT)
            for h in range(H):
                last = nc.tensor.transpose(k.psum[:, 0, h * P:(h + 1) * P], qg1[:, h * P:(h + 1) * P], k.ident[:])
            last.then_inc(s.T_psum, 1)
            pe.wait_ge(s.T_a, 4)
            pe.wait_ge(s.T_v, 3)
            for t in range(NT):
                tok = slice(t * P, (t + 1) * P)
                for i, (lhs, rhs) in enumerate(((kT, qT), (kT, kbT), (kbT, kT))):
                    for h in range(H):
                        last = nc.tensor.matmul(k.psum[:, 4 * t + 1 + i, h * P:(h + 1) * P], lhs[:, h, tok], rhs[:, h, tok],
                                                start=True, stop=True)
                last.then_inc(s.pair_psum, 1)

            def mm(t, b, left_t, right):
                for h in range(H):
                    cols = slice(h * P, (h + 1) * P)
                    last = nc.tensor.matmul(k.psum[:, 4 * t + b, cols], left_t[:, t, cols], right[:, t, cols], start=True, stop=True)
                return last

            def turn(t, b, m):
                for h in range(H):
                    cols = slice(h * P, (h + 1) * P)
                    nc.tensor.transpose(k.psum[:, 4 * t + b, cols], m[:, t, cols], k.ident[:])

            def product(m, t):
                if m == 1:
                    mm(t, 0, B, A)
                    return mm(t, 1, A, B)
                if m == 2:
                    mm(t, 2, B, A)
                    return mm(t, 3, A, Z)
                if m == 3:
                    return mm(t, 0, B, Z)
                if m == 4:
                    turn(t, 1, Z)
                    mm(t, 2, Lo, Z)
                    return mm(t, 3, Z, Lo)
                if m == 5:
                    mm(t, 0, Cm, B)
                    return mm(t, 1, B, Cm)
                if m == 6:
                    mm(t, 2, Cm, B)
                    mm(t, 3, B, Cm)
                    return mm(t, 0, B, Z)
                if m == 7:
                    mm(t, 1, Cm, B)
                    return mm(t, 2, B, Z)
                if m == 8:
                    return mm(t, 3, B, Z)
                return mm(t, 0, A, Z)

            for m in range(1, 10):
                for t in range(NT):
                    if m == 1:
                        pe.wait_ge(s.lower, t + 1)
                    else:
                        pe.wait_ge(s.sub_v, reached(V_STAGES, m - 1, t))
                        pe.wait_ge(s.sub_a, reached(A_STAGES, m - 1, t) if m - 1 in A_STAGES else reached(A_STAGES, m - 2, t))
                    product(m, t).then_inc(s.prod, 1)

            pe.wait_ge(s.sub_a, reached(A_STAGES, 9, 1))
            for h in range(H):
                cols = slice(h * P, (h + 1) * P)
                last = nc.tensor.matmul(k.psum[:, 1, cols], B[:, 0, cols], v[:, 0, cols], start=True, stop=True)
            last.then_inc(s.v0, 1)
            pe.wait_ge(s.extra, 2)
            for h in range(H):
                cols = slice(h * P, (h + 1) * P)
                last = nc.tensor.matmul(k.psum[:, 5, cols], kbg1[:, cols], B[:, 1, cols], start=True, stop=True)
            last.then_inc(s.w1, 1)
            pe.wait_ge(s.vn0, 1)
            for h in range(H):
                cols = slice(h * P, (h + 1) * P)
                last = nc.tensor.matmul(k.psum[:, 2, cols], kg0[:, cols], vn[:, 0, cols], start=True, stop=True)
            last.then_inc(s.st_psum, 1)
            for h in range(H):
                cols = slice(h * P, (h + 1) * P)
                last = nc.tensor.matmul(k.psum[:, 3, cols], AT[:, 0, cols], vn[:, 0, cols], start=True, stop=True)
            last.then_inc(s.o0, 1)
            pe.wait_ge(s.st, 1)
            pe.wait_ge(s.nw1, 1)
            for h in range(H):
                cols = slice(h * P, (h + 1) * P)
                nc.tensor.matmul(k.psum[:, 6, cols], B[:, 1, cols], v[:, 1, cols], start=True, stop=False)
                last = nc.tensor.matmul(k.psum[:, 6, cols], nw1[:, cols], st[:, cols], start=False, stop=True)
            last.then_inc(s.vn1_psum, 1)
            pe.wait_ge(s.vn1, 1)
            for h in range(H):
                cols = slice(h * P, (h + 1) * P)
                nc.tensor.matmul(k.psum[:, 7, cols], qgT1[:, h, :], st[:, cols], start=True, stop=False)
                last = nc.tensor.matmul(k.psum[:, 7, cols], AT[:, 1, cols], vn[:, 1, cols], start=False, stop=True)
            last.then_inc(s.o1, 1)
            for t in range(NT):
                pe.wait_ge(s.on, t + 1)
                for h in range(H):
                    last = nc.tensor.transpose(k.psum[:, 4 + t, h * P:(h + 1) * P], o[:, t, h * P:(h + 1) * P], k.ident[:])
                last.then_inc(s.onT, 1)

        @block.scalar
        def _(act):
            act.wait_ge(k.s_gdn_w, 48)
            nc.scalar.activation(ea[:], e.a_log[:], ACT.Exp).then_inc(s.alog, 1)
            nc.scalar.activation(w.tb, beta, ACT.Exp, scale=-1.0).then_inc(s.beta_exp, 1)
            log1p_exp_scalar(nc, act, s, w)
            for i in range(6):
                act.wait_ge(s.nat_psum, i + 1)
                nc.scalar.copy((q, kk_, v)[i // 2][:, i % 2, :], bank(2 + i)).then_inc(s.nat, 1)
            act.wait_ge(s.cum, 1)
            nc.scalar.activation(w.e_cum, w.cum, ACT.Exp).then_inc(s.exps, 1)
            nc.scalar.activation(w.e_left, w.last, ACT.Exp).then_inc(s.exps, 1)
            for t in range(NT):
                act.wait_ge(s.decay_in, t + 1)
                nc.scalar.activation(D_t[:, t, :], D_t[:, t, :], ACT.Exp).then_inc(s.decay, 1)
                nc.scalar.activation(Dn[:, t, :], Dn[:, t, :], ACT.Exp, scale=-1.0).then_inc(s.decay, 1)
            act.wait_ge(s.ssq, 1)
            nc.scalar.activation(rs[:].rearrange("p a t h -> p (a t h)"), ssq[:].rearrange("p a t h -> p (a t h)"),
                                 ACT.Sqrt, bias=k.eps[:, 0:1]).then_inc(s.root, 1)
            for i in (0, 2):
                for t in range(NT):
                    act.wait_ge(s.T_psum, 2 * i + t + 1)
                    nc.scalar.copy((qT, kT, kbT)[i][:, :, t * P:(t + 1) * P], heads(bank(2 + 2 * i + t))).then_inc(s.T_a, 1)
            for m in A_STAGES:
                for t in range(NT):
                    act.wait_ge(s.prod, NT * (m - 1) + t + 1)
                    moves = {1: [(A, 0)], 2: [(B, 2)], 4: [(A, 1), (B, 3)], 5: [(B, 0)], 6: [(B, 2), (Cm, 3)], 7: [(B, 1)],
                             9: [(B, 0)]}[m]
                    for to, b in moves:
                        last = nc.scalar.copy(to[:, t, :], bank(4 * t + b))
                    last.then_inc(s.sub_a, 1)
            act.wait_ge(s.w1, 1)
            nc.scalar.mul(nw1[:], bank(5), -1.0).then_inc(s.nw1, 1)
            act.wait_ge(s.st_psum, 1)
            nc.scalar.copy(st[:], bank(2)).then_inc(s.st, 1)
            for t in range(NT):
                act.wait_ge((s.o0, s.o1)[t], 1)
                nc.scalar.copy(o[:, t, :], bank(3 + 4 * t)).then_inc(s.o_sb, 1)
                act.wait_ge(s.ssq_o, t + 1)
                nc.scalar.activation(rs[:, 0, t, :], ssq[:, 0, t, :], ACT.Sqrt, bias=k.eps[:, 0:1], scale=1.0 / GD).then_inc(s.root_o, 1)
            for t in range(NT):
                act.wait_ge(s.onT, t + 1)
                nc.scalar.copy(k.mixT[:, 4:8, t * P:(t + 1) * P], heads(bank(4 + t))).then_inc(s.mixed, 1)

        @block.gpsimd
        def _(pool):
            pool.wait_ge(s.gates, 1)
            nc.gpsimd.tensor_copy(wide[:].rearrange("p t (h c) -> p (t h) c", h=H),
                                  over(w.g.rearrange("p t h -> p (t h)"), 2, GD)).then_inc(s.wide, 1)
            pool.wait_ge(s.nat, 6)
            pool.wait_ge(s.gates, 1)
            for t in range(NT):
                last = nc.gpsimd.tensor_tensor(heads(v[:, t, :]), heads(v[:, t, :]), per_head(w.beta[:, t, :]), ALU.mult)
            pool.wait_ge(s.scaled, 3)
            pool.wait_ge(s.exps, 2)
            nc.gpsimd.tensor_tensor(heads(qg1[:]), heads(q[:, 1, :]), per_head(w.e_cum[:, 1, :]), ALU.mult).then_inc(s.extra, 1)
            nc.gpsimd.tensor_tensor(heads(kg0[:]), heads(kk_[:, 0, :]), per_head(w.e_left[:, 0, :]), ALU.mult)
            nc.gpsimd.tensor_tensor(heads(kbg1[:]), heads(kb[:, 1, :]), per_head(w.e_cum[:, 1, :]), ALU.mult).then_inc(s.extra, 1)

        @block.vector
        def _(dve):
            step = Chain(dve, s.vec)
            step(nc.vector.tensor_tensor(blk[:], k.block8[:], k.upto[:], ALU.mult))
            step(nc.vector.tensor_tensor(blk[:], blk[:], k.ident[:], ALU.subtract))
            dve.wait_ge(s.beta_exp, 1)
            step(nc.vector.tensor_scalar(w.tb, w.tb, 1.0, None, ALU.add))
            step(nc.vector.reciprocal(w.beta, w.tb))
            dve.wait_ge(k.s_gdn_w, 48)
            step(nc.vector.tensor_tensor(w.x, decay, over(e.dt_bias[:], 1, NT), ALU.add))
            log1p_exp_vector(nc, dve, step, s, w.x, w.lp, w)
            step(nc.vector.scalar_tensor_tensor(w.g, w.x, 0.0, w.lp, ALU.max, ALU.add))
            dve.wait_ge(s.alog, 1)
            for t in range(NT):
                step(nc.vector.scalar_tensor_tensor(w.g[:, t, :], w.g[:, t, :], -1.0, ea[:], ALU.mult, ALU.mult))
            nc.vector.engine_nop().then_inc(s.gates, 1)
            dve.wait_ge(s.cum_psum, 1)
            step(nc.vector.tensor_copy(w.cum.rearrange("p t h -> p (t h)"), k.psum[:, 0, 0:NT * H]))
            step(nc.vector.tensor_tensor(w.last.rearrange("p t h -> p (t h)"), k.psum[:, 0, NT * H:2 * NT * H],
                                         w.cum.rearrange("p t h -> p (t h)"), ALU.subtract))
            nc.vector.engine_nop().then_inc(s.cum, 1)
            for t in range(NT):
                dve.wait_ge(s.cumrow, t + 1)
                for h in range(H):
                    cols = slice(h * P, (h + 1) * P)
                    nc.vector.scalar_tensor_tensor(D_t[:, t, cols], k.psum[:, 1 - t, cols], w.cum[:, t, h:h + 1],
                                                   k.no_later_T[:], ALU.subtract, ALU.add)
                    last = nc.vector.scalar_tensor_tensor(Dn[:, t, cols], k.psum[:, 1 - t, cols], w.cum[:, t, h:h + 1],
                                                          k.off_strict[:], ALU.subtract, ALU.add)
                last.then_inc(s.decay_in, 1)
            dve.wait_ge(s.nat, 4)
            dve.wait_ge(s.cumrow, NT)
            for i, m in enumerate((q, kk_)):
                for t in range(NT):
                    step(nc.vector.tensor_tensor(A[:, t, :], m[:, t, :], m[:, t, :], ALU.mult))
                    step(nc.vector.tensor_reduce(ssq[:, i, t, :], heads(A[:, t, :]), AX.X, ALU.add))
            nc.vector.engine_nop().then_inc(s.ssq, 1)
            dve.wait_ge(s.root, 1)
            step(nc.vector.reciprocal(rs[:].rearrange("p a t h -> p (a t h)"), rs[:].rearrange("p a t h -> p (a t h)")))
            for t in range(NT):
                step(nc.vector.scalar_tensor_tensor(heads(q[:, t, :]), heads(q[:, t, :]), float(GD ** -0.5),
                                                    per_head(rs[:, 0, t, :]), ALU.mult, ALU.mult))
            nc.vector.engine_nop().then_inc(s.scaled, 1)
            for t in range(NT):
                step(nc.vector.tensor_tensor(heads(kk_[:, t, :]), heads(kk_[:, t, :]), per_head(rs[:, 1, t, :]), ALU.mult))
            nc.vector.engine_nop().then_inc(s.scaled, 1)
            for t in range(NT):
                step(nc.vector.tensor_tensor(heads(kb[:, t, :]), heads(kk_[:, t, :]), per_head(w.beta[:, t, :]), ALU.mult))
            nc.vector.engine_nop().then_inc(s.scaled, 1)
            for t in range(NT):
                dve.wait_ge(s.T_psum, 2 + t + 1)
                nc.vector.tensor_copy(kT[:, :, t * P:(t + 1) * P], heads(bank(4 + t))).then_inc(s.T_v, 1)
            dve.wait_ge(s.T_psum, 7)
            nc.vector.tensor_copy(qgT1[:], heads(bank(0))).then_inc(s.T_v, 1)
            dve.wait_ge(s.decay, 2 * NT)
            blocks, blocks_t = over(k.block8[:], 1, H), over(blk[:], 1, H)
            one = over(k.ident[:], 1, H)
            for t in range(NT):
                dve.wait_ge(s.pair_psum, t + 1)
                step(nc.vector.tensor_tensor(AT[:, t, :], bank(4 * t + 1), D_t[:, t, :], ALU.mult))
                step(nc.vector.tensor_tensor(B[:, t, :], bank(4 * t + 2), D_t[:, t, :], ALU.mult))
                step(nc.vector.tensor_tensor(heads(B[:, t, :]), heads(B[:, t, :]), blocks_t, ALU.mult))
                step(nc.vector.tensor_tensor(Lo[:, t, :], bank(4 * t + 3), Dn[:, t, :], ALU.mult))
                step(nc.vector.tensor_tensor(heads(A[:, t, :]), heads(Lo[:, t, :]), blocks, ALU.mult))
                step(nc.vector.tensor_tensor(Lo[:, t, :], Lo[:, t, :], A[:, t, :], ALU.subtract))
                step(nc.vector.tensor_tensor(heads(Z[:, t, :]), one, heads(B[:, t, :]), ALU.subtract))
                nc.vector.engine_nop().then_inc(s.lower, 1)
            for m in V_STAGES:
                for t in range(NT):
                    dve.wait_ge(s.prod, NT * (m - 1) + t + 1)
                    if m == 4:
                        step(nc.vector.tensor_copy(Cm[:, t, :], bank(4 * t + 2)))
                        last = nc.vector.tensor_tensor(heads(Z[:, t, :]), one, heads(Cm[:, t, :]), ALU.subtract)
                    elif m in (1, 5):
                        last = nc.vector.tensor_copy((B if m == 1 else Cm)[:, t, :], bank(4 * t + 1))
                    else:
                        b = {2: 3, 3: 0, 6: 0, 7: 2, 8: 3}[m]
                        last = nc.vector.tensor_tensor(Z[:, t, :], Z[:, t, :], bank(4 * t + b), ALU.add)
                    last.then_inc(s.sub_v, 1)
            dve.wait_ge(s.v0, 1)
            nc.vector.tensor_copy(vn[:, 0, :], bank(1)).then_inc(s.vn0, 1)
            dve.wait_ge(s.vn1_psum, 1)
            nc.vector.tensor_copy(vn[:, 1, :], bank(6)).then_inc(s.vn1, 1)
            for t in range(NT):
                dve.wait_ge(s.o_sb, t + 1)
                step(nc.vector.tensor_tensor(wide[:, t, :], o[:, t, :], o[:, t, :], ALU.mult))
                step(nc.vector.tensor_reduce(ssq[:, 0, t, :], heads(wide[:, t, :]), AX.X, ALU.add))
                nc.vector.engine_nop().then_inc(s.ssq_o, 1)
                dve.wait_ge(s.root_o, t + 1)
                step(nc.vector.reciprocal(rs[:, 0, t, :], rs[:, 0, t, :]))
                step(nc.vector.tensor_tensor(heads(o[:, t, :]), heads(o[:, t, :]), per_head(rs[:, 0, t, :]), ALU.mult))
                step(nc.vector.tensor_tensor(heads(o[:, t, :]), heads(o[:, t, :]), over(e.o_gain[:], 1, H), ALU.mult))
                step(nc.vector.tensor_tensor(o[:, t, :], o[:, t, :], e.z[:, t, :], ALU.mult))
                nc.vector.engine_nop().then_inc(s.on, 1)
    ctx.close()


def mixer_output(nc, k, d, layer, x, weights_ready, n_ready):
    ctx = ExitStack()
    s = semaphores(ctx, nc, f"out{layer}", "vec mixed variance root rstd centred normed eps")
    ln = named(**layer_norm_tiles(lambda n, sh, dt=F32: ctx.enter_context(nc.sbuf_tensor(f"out{layer}_{n}", sh, dt))))
    with nc.Block(no_gpsimd_drain=True) as block:
        @block.sync
        def _(sp):
            sp.wait_ge(s.mixed, NT)
            load_shared(sp, k, d, layer, x)

        @block.tensor
        def _(pe):
            pe.wait_ge(weights_ready, n_ready)
            for t in range(NT):
                for half in range(2):
                    w = columns_of(k, 2 + half)
                    for c in range(KD):
                        last = nc.tensor.matmul(k.psum[:, 2 * t + half, :], k.mixT[:, c, t * P:(t + 1) * P], w[:, c, :],
                                                start=c == 0, stop=c == KD - 1)
                last.then_inc(s.mixed, 1)

        @block.scalar
        def _(act):
            act.wait_ge(s.eps, 1)
            layer_norm_scalar(nc, act, s, ln)

        @block.vector
        def _(dve):
            step = Chain(dve, s.vec)
            nc.vector.memset(ln.ln_eps[:], LN_EPS).then_inc(s.eps, 1)
            dve.wait_ge(weights_ready, n_ready)
            layer_norm_vector(nc, dve, step, s, k, ln, s.mixed, together=False)
    ctx.close()


def even_shared(ctx, nc, k):
    def sb(name, shape, dt=F32):
        return ctx.enter_context(nc.sbuf_tensor(f"ev_{name}", shape, dt))

    e = named()
    e.lat = sb("lat", [P, NT, EV_LAT + 2 * GH])
    e.cols = sb("cols", [P, CONV_W * G_CHUNKS + 3])
    e.gT = sb("gT", [P, G_CHUNKS, S])
    e.z = sb("z", [P, NT, GH * GD])
    e.o_gain = sb("o_gain", [P, GD])
    e.a_log = sb("a_log", [P, GH])
    e.dt_bias = sb("dt_bias", [P, GH])
    w = semaphores(ctx, nc, "even", "mla_weights out_weights gdn_small_weights")
    k.s_mla_w, k.s_out_w, k.s_gdn_w = w.mla_weights, w.out_weights, w.gdn_small_weights
    return e



OD_K = LH * LK
OD_V = 2 * OD_K
OD_GATES = OD_V + LH * LV
OD_O = OD_GATES + 2 * LH
OD_SQ = OD_O + LH * LV
OD_SK = OD_SQ + WH * WD
OD_END = OD_SK + 2 * WKV * WD


def odd_shared(ctx, nc, k):
    def sb(name, shape, dt=F32):
        return ctx.enter_context(nc.sbuf_tensor(f"od_{name}", shape, dt))

    e = named()
    e.mqT = sb("mqT", [P, 2, S])
    e.mkT = sb("mkT", [P, LH, S])
    e.v1 = sb("v1", [P, NT, LH, LV + 1])
    e.gate_o = sb("gate_o", [P, NT, LH * LV])
    e.m_gain = sb("m_gain", [P, LH * LV])
    e.rows = {n: sb(n, [LH, S]) for n in ("decay", "rest", "stab")}
    e.sq = sb("sq", [P, NT, WH, WD])
    e.sk = sb("sk", [P, NT, WKV, 2, 2, WD])
    e.sv = sb("sv", [P, NT, WKV, WD])
    e.sinks = sb("sinks", [P, WH])
    e.window = sb("window", [P, 2 * P])
    w = semaphores(ctx, nc, "odd", "out_weights small_weights")
    k.s_odd_out_w, k.s_odd_small = w.out_weights, w.small_weights
    return e


def odd_project(nc, k, d, e, x):
    ctx = ExitStack()
    s = semaphores(ctx, nc, "odp", "gates_w qk_w kv_w sq_w v_w o_w xT_psum xT vec gates_psum gates_read mq_psum mk_psum mqT mkT "
                                   "skv_psum skv sq_psum sq v_psum v o_psum o zeros pool mag exp_mag one_more log_u")

    def sb(name, shape, dt=F32):
        return ctx.enter_context(nc.sbuf_tensor(f"odp_{name}", shape, dt))

    wg = sb("w_gates", [P, KD, 2 * LH])
    bias = sb("gate_bias", [LH, 2])
    raw_i, raw_f, lp, run, off = (sb(n, [LH, S]) for n in ("raw_i", "raw_f", "lp", "run", "none"))
    w = named(**{n: sb(n, [LH, S])[:] for n in ("mag", "t", "u", "d", "tiny", "log")})
    sk_raw = sb("sk_raw", [P, NT, WKV, WD])
    tmp = [sb(f"tmp{i}", [P, WH, WD // 2]) for i in range(4)]
    win = d.od_w_in[0].rearrange("(p k) n -> p k n", k=KD)
    skv_w = k.w_down[2][:].rearrange("p j n -> p (j n)").rearrange("p (k n) -> p k n", k=KD)

    with nc.Block(no_gpsimd_drain=True) as block:
        @block.sync
        def _(sp):
            sp.dma_start(columns_of(k, 0), win[:, :, 0:OD_V]).then_inc(s.qk_w, 16)
            sp.dma_start(wg[:], win[:, :, OD_GATES:OD_O]).then_inc(s.gates_w, 16)
            with nc.allow_non_contiguous_dma(reason="four biases"):
                for i, src in enumerate((d.mlstm_b_i, d.mlstm_b_f)):
                    sp.dma_start(bias[:, i:i + 1], src.rearrange("o h -> h o")).then_inc(s.gates_w, 16)
            sp.dma_start(skv_w, win[:, :, OD_SK:OD_END]).then_inc(s.kv_w, 16)
            sp.dma_start(columns_of(k, 1), win[:, :, OD_SQ:OD_SK]).then_inc(s.sq_w, 16)
            sp.dma_start(columns_of(k, 2), win[:, :, OD_V:OD_GATES]).then_inc(s.v_w, 16)
            sp.dma_start(columns_of(k, 3), win[:, :, OD_O:OD_SQ]).then_inc(s.o_w, 16)
            sp.dma_start(e.m_gain[:], d.mlstm_norm.to_broadcast([P, LH * LV])).then_inc(k.s_odd_small, 16)
            sp.dma_start(e.sinks[:], d.swa_sinks.to_broadcast([P, WH])).then_inc(k.s_odd_small, 16)
            for i, src in enumerate((d.ln1_g, d.ln1_b)):
                sp.dma_start(k.ln[:, i, :], src[1:2].to_broadcast([P, D])).then_inc(k.s_odd_out_w, 16)
            for half, used in enumerate((s.v_psum, s.o_psum)):
                sp.wait_ge(used, NT)
                sp.dma_start(columns_of(k, 2 + half),
                             d.od_w_out[0][:, half * BANK:(half + 1) * BANK].rearrange("(c p) n -> p c n", p=P)
                             ).then_inc(k.s_odd_out_w, 16)
            load_early_experts(sp, k, d, 1, x, lambda e: sp.wait_ge((s.mk_psum, s.sq_psum)[e], (1, NT)[e]))

        @block.gpsimd
        def _(pool):
            nc.gpsimd.memset(e.mkT[:], 0.0).then_inc(s.zeros, 1)
            nc.gpsimd.memset(e.sk[:], 0.0).then_inc(s.zeros, 1)
            nc.gpsimd.memset(e.v1[:, :, :, LV:], 1.0).then_inc(s.zeros, 1)
            nc.gpsimd.memset(e.window[:], 0.0).then_inc(s.zeros, 1)
            pool.wait_ge(s.zeros, 4)
            nc.gpsimd.affine_select(out=e.window[:, 0:P], in_=e.window[:, 0:P], pattern=[[1, P]],
                                    compare_op=ALU.is_gt, fill=NEG, base=0, channel_multiplier=-1).then_inc(s.pool, 1)
            nc.gpsimd.affine_select(out=e.window[:, P:], in_=e.window[:, P:], pattern=[[-1, P]],
                                    compare_op=ALU.is_ge, fill=NEG, base=0, channel_multiplier=1).then_inc(s.pool, 1)
            pool.wait_ge(s.pool, 2)

        @block.tensor
        def _(pe):
            transpose_x_tensor(nc, pe, s, k)
            pe.wait_ge(s.xT, KD // 2)
            pe.wait_ge(s.gates_w, 48)
            for i in range(2):
                for kk in range(KD):
                    last = nc.tensor.matmul(k.psum[0:LH, 4, i * S:(i + 1) * S], wg[:, kk, i * LH:(i + 1) * LH], k.xT[:, kk, :],
                                            start=kk == 0, stop=kk == KD - 1)
            last.then_inc(s.gates_psum, 1)
            pe.wait_ge(s.qk_w, 16)
            for i, sem in enumerate((s.mq_psum, s.mk_psum)):
                w0 = columns_of(k, 0)
                for c in range(2):
                    for kk in range(KD):
                        last = nc.tensor.matmul(k.psum[:, 5 + i, c * S:(c + 1) * S],
                                                w0[:, kk, i * OD_K + c * P:i * OD_K + (c + 1) * P], k.xT[:, kk, :],
                                                start=kk == 0, stop=kk == KD - 1)
                last.then_inc(sem, 1)

            def natural(weights, bank, cols, sem):
                for t in range(NT):
                    place = k.psum[:, bank + t, :] if cols == BANK else k.psum[:, bank, t * cols:(t + 1) * cols]
                    for kk in range(KD):
                        last = nc.tensor.matmul(place, k.xT[:, kk, t * P:(t + 1) * P], weights[:, kk, :],
                                                start=kk == 0, stop=kk == KD - 1)
                    last.then_inc(sem, 1)

            pe.wait_ge(s.kv_w, 16)
            natural(skv_w, 7, S, s.skv_psum)
            pe.wait_ge(s.sq_w, 16)
            natural(columns_of(k, 1), 0, BANK, s.sq_psum)
            pe.wait_ge(s.v_w, 16)
            natural(columns_of(k, 2), 2, BANK, s.v_psum)
            pe.wait_ge(s.o_w, 16)
            pe.wait_ge(s.gates_read, 1)
            pe.wait_ge(s.mqT, 1)
            natural(columns_of(k, 3), 4, BANK, s.o_psum)

        @block.scalar
        def _(act):
            transpose_x_scalar(nc, act, s, k)
            log1p_exp_scalar(nc, act, s, w)
            act.wait_ge(s.mq_psum, 1)
            nc.scalar.copy(flat(e.mqT[:]), k.psum[:, 5, :]).then_inc(s.mqT, 1)
            act.wait_ge(s.zeros, 4)
            act.wait_ge(s.mk_psum, 1)
            for h in range(LH):
                part = slice((h % 2) * LK, (h % 2 + 1) * LK)
                nc.scalar.mul(e.mkT[part, h, :], k.psum[part, 6, (h // 2) * S:(h // 2 + 1) * S], float(LK ** -0.5)).then_inc(s.mkT, 1)
            act.wait_ge(s.skv_psum, NT)
            both = k.psum[:, 7, :].rearrange("p (t c) -> p t c", t=NT)
            nc.scalar.copy(sk_raw[:].rearrange("p t g c -> p t (g c)"), both[:, :, 0:WKV * WD]).then_inc(s.skv, 1)
            nc.scalar.copy(e.sv[:].rearrange("p t g c -> p t (g c)"), both[:, :, WKV * WD:]).then_inc(s.skv, 1)
            for t in range(NT):
                act.wait_ge(s.sq_psum, t + 1)
                nc.scalar.copy(e.sq[:, t, :, :].rearrange("p h c -> p (h c)"), k.psum[:, t, :]).then_inc(s.sq, 1)
            for t in range(NT):
                act.wait_ge(s.v_psum, t + 1)
                nc.scalar.copy(e.v1[:, t, :, 0:LV], k.psum[:, 2 + t, :].rearrange("p (h c) -> p h c", h=LH)).then_inc(s.v, 1)
            for t in range(NT):
                act.wait_ge(s.o_psum, t + 1)
                nc.scalar.activation(e.gate_o[:, t, :], k.psum[:, 4 + t, :], ACT.Sigmoid).then_inc(s.o, 1)

        @block.vector
        def _(dve):
            step = Chain(dve, s.vec)
            step(nc.vector.memset(off[:], 0.0))
            dve.wait_ge(s.gates_psum, 1)
            dve.wait_ge(s.gates_w, 48)
            step(nc.vector.tensor_scalar(raw_i[:], k.psum[0:LH, 4, 0:S], bias[:, 0:1], None, ALU.add))
            step(nc.vector.tensor_scalar(raw_f[:], k.psum[0:LH, 4, S:2 * S], bias[:, 1:2], None, ALU.add))
            nc.vector.engine_nop().then_inc(s.gates_read, 1)
            log1p_exp_vector(nc, dve, step, s, raw_f[:], lp[:], w)
            step(nc.vector.scalar_tensor_tensor(raw_f[:], raw_f[:], 0.0, lp[:], ALU.min, ALU.subtract))
            step(nc.vector.tensor_tensor_scan(run[:], raw_f[:], off[:], 0.0, ALU.add, ALU.add))
            step(nc.vector.tensor_tensor_scan(e.rows["stab"][:], raw_f[:], raw_i[:], 0.0, ALU.add, ALU.max))
            step(nc.vector.tensor_tensor(e.rows["decay"][:], run[:], e.rows["stab"][:], ALU.subtract))
            step(nc.vector.tensor_tensor(e.rows["rest"][:], raw_i[:], run[:], ALU.subtract))
            half = WD // 2
            own = slice(MLA_R // 2, None)
            dve.wait_ge(s.zeros, 4)
            dve.wait_ge(s.skv, 1)
            for t in range(NT):
                rope(nc, step, tmp, sk_raw[:, t, :, 0:half], sk_raw[:, t, :, half:], e.sk[:, t, :, 0, 0, 0:half],
                     e.sk[:, t, :, 0, 0, half:], k.cos[:, t, own], k.sin[:, t, own])
                step(nc.vector.tensor_copy(e.sk[:, t, :, 1, 1, :], e.sk[:, t, :, 0, 0, :]))
            for t in range(NT):
                dve.wait_ge(s.sq, t + 1)
                q1, q2 = e.sq[:, t, :, 0:half], e.sq[:, t, :, half:]
                rope(nc, step, tmp, q1, q2, q1, q2, k.cos[:, t, own], k.sin[:, t, own])
    ctx.close()


def odd_memory(nc, k, e):
    ctx = ExitStack()
    s = semaphores(ctx, nc, "mem", "vec sel wide_psum cols_psum cols neg_m qk_psum exps_in far exps pairs out_psum num "
                                   "ssq root normed turned mixed")

    def sb(name, shape, dt=F32):
        return ctx.enter_context(nc.sbuf_tensor(f"mem_{name}", shape, dt))

    H, C = LH, LH * LV
    sel = sb("head_rows", [H, H, P])
    cols = sb("cols", [P, 2 * NT, H])
    floor = sb("floor", [P, NT, H])
    ex = sb("exps", [P, H, S + P])
    w = sb("weights", [P, H, S + P])
    num = sb("num", [P, NT, H, LV + 1])
    den = sb("den", [P, NT, H])
    rden = sb("rden", [P, NT, H])
    o = sb("out", [P, NT, C])
    sq = sb("squares", [P, NT, C])
    ssq = sb("ssq", [P, NT, H])
    root = sb("root", [P, NT, H])
    heads = lambda ap: ap.rearrange("p (h c) -> p h c", h=H)
    wide = lambda h: k.psum[:, 4 + h // 2, (h % 2) * S:(h % 2 + 1) * S]

    with nc.Block(no_gpsimd_drain=True) as block:
        @block.tensor
        def _(pe):
            for i, r in enumerate(("rest", "stab")):
                for t in range(NT):
                    last = nc.tensor.transpose(k.psum[:, 6, (NT * i + t) * H:(NT * i + t + 1) * H],
                                               e.rows[r][:, t * P:(t + 1) * P], k.ident[0:H, 0:H])
            last.then_inc(s.cols_psum, 1)
            pe.wait_ge(s.sel, 1)
            for h in range(H):
                last = nc.tensor.matmul(wide(h), sel[:, h, :], e.rows["decay"][:], start=True, stop=True)
            last.then_inc(s.wide_psum, 1)
            for h in range(H):
                nc.tensor.matmul(k.psum[:, h, 0:S], e.mkT[:, h, 0:P], e.mqT[:, h // 2, :], start=True, stop=True)
                nc.tensor.matmul(k.psum[:, h, S:S + P], e.mkT[:, h, P:], e.mqT[:, h // 2, P:], start=True,
                                 stop=True).then_inc(s.qk_psum, 1)
            pe.wait_ge(s.pairs, H)
            for t in range(NT):
                for h in range(H):
                    place = k.psum[:, 4 + 2 * t + h // 2, (h % 2) * (LV + 1):(h % 2 + 1) * (LV + 1)]
                    for kt in range(t + 1):
                        first = S if kt else t * P
                        last = nc.tensor.matmul(place, w[:, h, first:first + P], e.v1[:, kt, h, :], start=kt == 0, stop=kt == t)
                last.then_inc(s.out_psum, 1)
            for t in range(NT):
                pe.wait_ge(s.normed, t + 1)
                for h in range(H):
                    last = nc.tensor.transpose(k.psum[:, t, h * P:(h + 1) * P], o[:, t, h * P:(h + 1) * P], k.ident[:])
                last.then_inc(s.turned, 1)

        @block.scalar
        def _(act):
            act.wait_ge(s.cols, 1)
            nc.scalar.activation(flat(floor[:]), flat(cols[:, NT:, :]), ACT.Exp, scale=-1.0).then_inc(s.neg_m, 1)
            act.wait_ge(s.exps_in, 1)
            for h in range(H):
                nc.scalar.activation(ex[:, h, P:S], wide(h)[:, P:], ACT.Exp, bias=cols[:, 0, h:h + 1]).then_inc(s.exps, 1)
                nc.scalar.activation(ex[:, h, 0:P], ex[:, h, 0:P], ACT.Exp).then_inc(s.exps, 1)
                nc.scalar.activation(ex[:, h, S:], ex[:, h, S:], ACT.Exp).then_inc(s.exps, 1)
            for t in range(NT):
                act.wait_ge(s.out_psum, t + 1)
                for half in range(2):
                    nc.scalar.copy(num[:, t, 2 * half:2 * half + 2, :].rearrange("p h c -> p (h c)"),
                                   k.psum[:, 4 + 2 * t + half, 0:2 * (LV + 1)]).then_inc(s.num, 1)
            act.wait_ge(s.ssq, 1)
            nc.scalar.activation(flat(root[:]), flat(ssq[:]), ACT.Sqrt, bias=k.eps[:, 0:1], scale=1.0 / LV).then_inc(s.root, 1)
            for t in range(NT):
                act.wait_ge(s.turned, t + 1)
                nc.scalar.copy(k.mixT[:, 0:H, t * P:(t + 1) * P], heads(k.psum[:, t, :])).then_inc(s.mixed, 1)

        @block.vector
        def _(dve):
            step = Chain(dve, s.vec)
            nc.vector.tensor_copy(sel[:], over(k.ident[0:H, 0:H], 2, P)).then_inc(s.sel, 1)
            dve.wait_ge(s.cols_psum, 1)
            nc.vector.tensor_copy(cols[:].rearrange("p i h -> p (i h)"), k.psum[:, 6, 0:2 * NT * H]).then_inc(s.cols, 1)
            dve.wait_ge(s.cols, 1)
            dve.wait_ge(s.wide_psum, 1)
            for h in range(H):
                for t in range(NT):
                    place = slice(S, S + P) if t else slice(0, P)
                    last = nc.vector.scalar_tensor_tensor(ex[:, h, place], wide(h)[:, t * P:(t + 1) * P], cols[:, t, h:h + 1],
                                                          k.no_later_T[:], ALU.add, ALU.add)
            last.then_inc(s.exps_in, 1)
            for h in range(H):
                dve.wait_ge(s.exps, 3 * h + 3)
                dve.wait_ge(s.qk_psum, h + 1)
                nc.vector.tensor_tensor(w[:, h, :], ex[:, h, :], k.psum[:, h, 0:S + P], ALU.mult).then_inc(s.pairs, 1)
            dve.wait_ge(s.neg_m, 1)
            dve.wait_ge(k.s_odd_small, 32)
            for t in range(NT):
                dve.wait_ge(s.num, 2 * t + 2)
                step(nc.vector.scalar_tensor_tensor(den[:, t, :], num[:, t, :, LV], -1.0, num[:, t, :, LV], ALU.mult, ALU.max))
                step(nc.vector.tensor_tensor(den[:, t, :], den[:, t, :], floor[:, t, :], ALU.max))
                step(nc.vector.reciprocal(rden[:, t, :], den[:, t, :]))
                step(nc.vector.tensor_tensor(heads(o[:, t, :]), num[:, t, :, 0:LV], over(rden[:, t, :], 2, LV), ALU.mult))
                step(nc.vector.tensor_tensor(sq[:, t, :], o[:, t, :], o[:, t, :], ALU.mult))
                step(nc.vector.tensor_reduce(ssq[:, t, :], heads(sq[:, t, :]), AX.X, ALU.add))
            nc.vector.engine_nop().then_inc(s.ssq, 1)
            for t in range(NT):
                step(nc.vector.tensor_tensor(e.gate_o[:, t, :], e.gate_o[:, t, :], e.m_gain[:], ALU.mult))
            dve.wait_ge(s.root, 1)
            step(nc.vector.reciprocal(flat(root[:]), flat(root[:])))
            for t in range(NT):
                step(nc.vector.tensor_tensor(heads(o[:, t, :]), heads(o[:, t, :]), over(root[:, t, :], 2, LV), ALU.mult))
                nc.vector.tensor_tensor(o[:, t, :], o[:, t, :], e.gate_o[:, t, :], ALU.mult).then_inc(s.normed, 1)
    ctx.close()


def odd_window(nc, k, e):
    ctx = ExitStack()
    s = semaphores(ctx, nc, "win", "vec qT_psum kT_psum qT kT scores masked max sunk sink_exp probs scaled turned pT mixed done")

    def sb(name, shape, dt=F32):
        return ctx.enter_context(nc.sbuf_tensor(f"win_{name}", shape, dt))

    qT = sb("qT", [P, WH // 2, S])
    kT = sb("kT", [P, WKV, 2, S])
    group = WH // WKV
    a = named(pr=sb("pr", [P, WH, S]), pT=sb("pT", [P, 2, 2, WH // 2 * P]), mx=sb("max", [P, WH]),
                        nb=sb("negmax", [P, WH]), den=sb("den", [P, WH]), dinv=sb("dinv", [P, WH]),
                        sunk=sb("sunk", [P, WH]), scale=float(WD ** -0.5), mask=e.window, sinks=e.sinks, chunk=4,
                        qT=lambda h, t: qT[:, h // 2, t * P:(t + 1) * P],
                        kT=lambda h, keys: kT[:, h // group, h % 2, 0:keys],
                        v=lambda h, kt: e.sv[:, kt, h // group, :])

    with nc.Block(no_gpsimd_drain=True) as block:
        @block.tensor
        def _(pe):
            for b in range(2):
                for i in range(2):
                    for t in range(NT):
                        last = nc.tensor.transpose(k.psum[:, b, i * S + t * P:i * S + (t + 1) * P],
                                                   e.sq[:, t, 4 * b + 2 * i:4 * b + 2 * i + 2, :].rearrange("p h c -> p (h c)"), k.ident[:])
                last.then_inc(s.qT_psum, 1)
            for g in range(WKV):
                for i in range(2):
                    for t in range(NT):
                        last = nc.tensor.transpose(k.psum[:, 2 + g, i * S + t * P:i * S + (t + 1) * P],
                                                   e.sk[:, t, g, i, :, :].rearrange("p u c -> p (u c)"), k.ident[:])
                last.then_inc(s.kT_psum, 1)
            attention_tensor(nc, pe, s, k, a)

        @block.scalar
        def _(act):
            for b in range(2):
                act.wait_ge(s.qT_psum, b + 1)
                nc.scalar.copy(flat(qT[:, 2 * b:2 * b + 2, :]), k.psum[:, b, :]).then_inc(s.qT, 2)
            attention_scalar(nc, act, s, k, a)

        @block.vector
        def _(dve):
            step = Chain(dve, s.vec)
            for g in range(WKV):
                dve.wait_ge(s.kT_psum, g + 1)
                nc.vector.tensor_copy(flat(kT[:, g, :, :]), k.psum[:, 2 + g, :]).then_inc(s.kT, 2)
            attention_vector(nc, dve, step, s, k, a)
    ctx.close()



def decoder_trunk(nc, d):
    with ExitStack() as ctx:
        k = persistent(ctx, nc)
        constants(nc, k)
        with ExitStack() as layer:
            x = expert_semaphores(layer, nc, 0)
            with ExitStack() as mixer:
                e = even_shared(mixer, nc, k)
                even_project(nc, k, d, e)
                even_latent_attention(nc, k, d, e, x)
                even_delta_net(nc, k, e)
                mixer_output(nc, k, d, 0, x, k.s_out_w, 64)
            moe_layer(nc, k, d, 0, x)
        with ExitStack() as layer:
            x = expert_semaphores(layer, nc, 1)
            with ExitStack() as mixer:
                e = odd_shared(mixer, nc, k)
                odd_project(nc, k, d, e, x)
                odd_memory(nc, k, e)
                odd_window(nc, k, e)
                mixer_output(nc, k, d, 1, x, k.s_odd_out_w, 64)
            moe_layer(nc, k, d, 1, x, out=d.out[0])


INPUTS = ("x", "positions", "ev_w_in", "mla_q_norm", "mla_w_qb", "mla_kv_norm", "mla_w_kvb", "gdn_conv", "gdn_a_log",
          "gdn_dt_bias", "gdn_norm", "ev_w_out", "od_w_in", "mlstm_b_i", "mlstm_b_f", "mlstm_norm", "swa_sinks", "od_w_out",
          "ln1_g", "ln1_b", "router_w", "router_b", "moe_w_gate", "moe_w_up", "moe_w_down", "shared_w_gate", "shared_w_up",
          "shared_w_down", "ln2_g", "ln2_b")


def kernel(**inputs):
    import concourse.bacc as bacc
    from concourse.bass_utils import run_bass_kernel_spmd

    nc = bacc.Bacc("TRN2", target_bir_lowering=False, num_devices=1)
    arrays = {f"in_{name}": np.ascontiguousarray(inputs[name]) for name in INPUTS}
    d = named(**{name: nc.dram_tensor(f"in_{name}", list(arrays[f"in_{name}"].shape),
                                                mybir.dt.from_np(arrays[f"in_{name}"].dtype), kind="ExternalInput").ap()
                           for name in INPUTS})
    d.out = nc.dram_tensor("out_x", [1, S, D], F32, kind="ExternalOutput").ap()
    decoder_trunk(nc, d)
    result = run_bass_kernel_spmd(nc, [arrays], core_ids=[0])
    return result.results[0]["out_x"]
```

```python
from contextlib import ExitStack

import numpy as np
import concourse.bass as bass
from concourse import mybir

F32 = mybir.dt.float32
BF16 = mybir.dt.bfloat16
I32 = mybir.dt.int32
ALU = mybir.AluOpType
ACT = mybir.ActivationFunctionType
AX = mybir.AxisListType

P = 128
D = 1024
S = 256
NT = S // P
KD = D // P
BANK = 512

N_EXP = 64
GROUPS = 8
GROUP = N_EXP // GROUPS
TOP_GROUPS = 4
TOP_K = 8
FE = 256
KF = FE // P
SLOTS = 64
PAIRS = N_EXP // 2
MAX_OVER = 32
ROUTED_SCALE = 2.5
ALPHA = float(4 ** 0.25)
LN_EPS = 1e-5
RMS_EPS = 1e-6
NEG = -1e30
OFF_GROUP = -3.0e38
TAKEN = -3.3e38

MLA_H, MLA_N, MLA_R, MLA_V = 8, 64, 32, 64
MLA_QK = MLA_N + MLA_R
Q_LORA, KV_LORA = 256, 128
GH, GD = 4, 128
CONV_W = 4
LH, LK, LV = 4, 64, 128
WH, WKV, WD = 8, 2, 64
ROPE_THETA = 10000.0


def named(**parts):
    return type("Parts", (), parts)


def semaphores(ctx, nc, prefix, names):
    made = {n: nc.alloc_semaphore(f"{prefix}_{n}") for n in names.split()}

    def clear():
        nc.clear_and_free_semaphores(list(made.values()))
        nc.all_engine_barrier()

    ctx.callback(clear)
    return named(**made)


class Chain:

    def __init__(self, eng, sem):
        self.eng, self.sem, self.n = eng, sem, 0

    def __call__(self, instruction):
        self.n += 1
        instruction.then_inc(self.sem, 1)
        self.eng.wait_ge(self.sem, self.n)


def over(ap, axis, n):
    v = ap.unsqueeze(axis)
    shape = list(v.shape)
    shape[axis] = n
    return v.to_broadcast(shape)


def persistent(ctx, nc):
    def sb(name, shape, dt=F32):
        return ctx.enter_context(nc.sbuf_tensor(name, shape, dt))

    k = named()
    k.x = sb("x_tokens", [P, NT, D])
    k.xT = sb("x_transposed", [P, KD, S])
    k.w_up = [sb(f"w_up_ring{i}", [P, 2, KD, FE]) for i in range(4)]
    k.w_down = [sb(f"w_down_ring{i}", [P, KF, D]) for i in range(4)]
    k.ln = sb("ln_gain_bias", [P, 2, D])
    k.mixT = sb("mixed_transposed", [P, KD, S])
    k.cos = sb("rope_cos", [P, NT, MLA_R // 2 + WD // 2])
    k.sin = sb("rope_sin", [P, NT, MLA_R // 2 + WD // 2])
    k.upto = sb("upto", [P, P])
    k.no_later = sb("no_later", [P, 2 * P])
    k.no_later_T = sb("no_later_T", [P, P])
    k.off_strict = sb("off_strict", [P, P])
    k.block8 = sb("block8", [P, P])
    k.eps = sb("epsilons", [P, 2])
    k.router_w = sb("router_w_sb", [P, KD, N_EXP])
    k.router_b = sb("router_b_sb", [P, N_EXP])
    k.gates_w = sb("mlstm_gates_w", [P, KD, 2 * LH])
    k.gate_bias = sb("mlstm_gate_bias", [LH, 2])
    k.ident = sb("identity", [P, P])
    k.ident_bf = sb("identity_bf", [P, P], BF16)
    k.ones = sb("ones", [P, P])
    k.ones_bf = sb("ones_bf", [P, P], BF16)
    k.before_bf = sb("before_bf", [P, P], BF16)
    k.slot_no = sb("slot_no", [P, SLOTS])
    k.earlier8 = sb("earlier8", [P, GROUPS, GROUPS])
    k.pass_no = sb("pass_no", [MAX_OVER, 1])
    k.psum = ctx.enter_context(nc.psum_tensor("psum", [P, 8, BANK], F32))
    k.over_dram = nc.dram_tensor("overflow_table", [MAX_OVER, 4], I32, kind="Internal").ap()
    return k


def constants(nc, k, first_loads):
    ctx = ExitStack()
    s = semaphores(ctx, nc, "const", "pool zeros")
    with nc.Block(no_gpsimd_drain=True) as block:
        @block.sync
        def _(sp):
            first_loads(sp)

        @block.vector
        def _(dve):
            nc.vector.memset(k.ident[:], 0.0)
            nc.vector.memset(k.ones[:], 1.0)
            nc.vector.memset(k.ones_bf[:], 1.0)
            nc.vector.memset(k.no_later[:], 0.0)
            nc.vector.memset(k.no_later_T[:], 0.0)
            nc.vector.memset(k.off_strict[:], 0.0)
            nc.vector.memset(k.block8[:], 1.0)
            nc.vector.memset(k.eps[:, 0:1], RMS_EPS)
            nc.vector.memset(k.eps[:, 1:2], float(np.pi / 2))
            nc.vector.memset(k.earlier8[:], 1.0).then_inc(s.zeros, 1)

        @block.gpsimd
        def _(pool):
            step = Chain(pool, s.pool)
            step(nc.gpsimd.iota(k.slot_no[:], [[1, SLOTS]], base=1, channel_multiplier=0,
                                allow_small_or_imprecise_dtypes=True))
            step(nc.gpsimd.iota(k.pass_no[:], [[1, 1]], base=0, channel_multiplier=1,
                                allow_small_or_imprecise_dtypes=True))
            pool.wait_ge(s.zeros, 1)
            step(nc.gpsimd.affine_select(out=k.ident[:], in_=k.ident[:], pattern=[[-1, P]],
                                         compare_op=ALU.not_equal, fill=1.0, base=0, channel_multiplier=1))
            step(nc.gpsimd.tensor_copy(k.ident_bf[:], k.ident[:]))
            step(nc.gpsimd.affine_select(out=k.before_bf[:], in_=k.ones_bf[:], pattern=[[1, P]],
                                         compare_op=ALU.is_gt, fill=0.0, base=0, channel_multiplier=-1))
            step(nc.gpsimd.affine_select(out=k.earlier8[:], in_=k.earlier8[:], pattern=[[1, GROUPS], [-1, GROUPS]],
                                         compare_op=ALU.is_gt, fill=0.0, base=0, channel_multiplier=0))
            step(nc.gpsimd.affine_select(out=k.upto[:], in_=k.ones[:], pattern=[[1, P]],
                                         compare_op=ALU.is_ge, fill=0.0, base=0, channel_multiplier=-1))
            step(nc.gpsimd.affine_select(out=k.no_later[:, P:2 * P], in_=k.no_later[:, P:2 * P], pattern=[[-1, P]],
                                         compare_op=ALU.is_ge, fill=NEG, base=0, channel_multiplier=1))
            step(nc.gpsimd.affine_select(out=k.no_later_T[:], in_=k.no_later_T[:], pattern=[[1, P]],
                                         compare_op=ALU.is_ge, fill=NEG, base=0, channel_multiplier=-1))
            step(nc.gpsimd.affine_select(out=k.off_strict[:], in_=k.off_strict[:], pattern=[[-1, P]],
                                         compare_op=ALU.is_gt, fill=-NEG, base=0, channel_multiplier=1))
            step(nc.gpsimd.affine_select(out=k.block8[:], in_=k.block8[:], pattern=[[-8, P // 8], [0, 8]],
                                         compare_op=ALU.is_ge, fill=0.0, base=0, channel_multiplier=1))
            step(nc.gpsimd.affine_select(out=k.block8[:], in_=k.block8[:], pattern=[[8, P // 8], [0, 8]],
                                         compare_op=ALU.is_ge, fill=0.0, base=7, channel_multiplier=-1))
    ctx.close()



def layer_norm_vector(nc, dve, step, s, k, w, mix_ready, together):
    def statistics(t):
        for half in range(2):
            dve.wait_ge(mix_ready, 2 * t + half + 1)
            cols = slice(half * BANK, (half + 1) * BANK)
            step(nc.vector.scalar_tensor_tensor(w.resid[:, t, cols], k.x[:, t, cols], ALPHA,
                                                k.psum[:, 2 * t + half, :], ALU.mult, ALU.add))
            step(nc.vector.bn_stats(w.bn[:, t, half, :], w.resid[:, t, cols]))
        nc.vector.bn_aggr(w.meanvar[:, t, :], w.bn[:, t, :, :]).then_inc(s.variance, 1)
        dve.wait_ge(s.root, t + 1)
        step(nc.vector.reciprocal(w.rstd[:, t:t + 1], w.root[:, t:t + 1]))
        nc.vector.scalar_tensor_tensor(w.shift[:, t:t + 1], w.meanvar[:, t, 0:1], -1.0, w.rstd[:, t:t + 1],
                                       ALU.mult, ALU.mult).then_inc(s.rstd, 1)

    def finish(t):
        dve.wait_ge(s.centred, t + 1)
        step(nc.vector.tensor_tensor(w.resid[:, t, :], w.resid[:, t, :], k.ln[:, 0, :], ALU.mult))
        nc.vector.tensor_tensor(k.x[:, t, :], w.resid[:, t, :], k.ln[:, 1, :], ALU.add).then_inc(s.normed, 1)

    for t in range(NT):
        statistics(t)
        if not together:
            finish(t)
    if together:
        finish(1)


def layer_norm_scalar(nc, act, s, w):
    nc.scalar.activation(w.early[:], w.ln_eps[:], ACT.Sqrt)
    for t in range(NT):
        act.wait_ge(s.variance, t + 1)
        nc.scalar.activation(w.root[:, t:t + 1], w.meanvar[:, t, 1:2], ACT.Sqrt,
                             bias=w.ln_eps[:, 0:1]).then_inc(s.root, 1)
        act.wait_ge(s.rstd, t + 1)
        nc.scalar.activation(w.resid[:, t, :], w.resid[:, t, :], ACT.Identity, scale=w.rstd[:, t:t + 1],
                             bias=w.shift[:, t:t + 1]).then_inc(s.centred, 1)


def layer_norm_gpsimd(nc, pool, s, k, w):
    pool.wait_ge(s.centred, 1)
    nc.gpsimd.tensor_tensor(w.resid[:, 0, :], w.resid[:, 0, :], k.ln[:, 0, :], ALU.mult).then_inc(s.gained, 1)
    pool.wait_ge(s.gained, 1)
    nc.gpsimd.tensor_tensor(k.x[:, 0, :], w.resid[:, 0, :], k.ln[:, 1, :], ALU.add).then_inc(s.normed_first, 1)


def layer_norm_tiles(sb):
    return dict(resid=sb("resid", [P, NT, D]), bn=sb("bn", [P, NT, 2, 6]), meanvar=sb("meanvar", [P, NT, 2]),
                root=sb("root", [P, NT]), rstd=sb("rstd", [P, NT]), shift=sb("shift", [P, NT]), ln_eps=sb("ln_eps", [P, 1]), early=sb("early", [P, 1]))



def transpose_x_tensor(nc, pe, s, k):
    for b in range(KD // 2):
        for c in range(2):
            for t in range(NT):
                last = nc.tensor.transpose(k.psum[:, b, c * S + t * P:c * S + (t + 1) * P],
                                           k.x[:, t, 2 * b + c:D:KD], k.ident[:])
        last.then_inc(s.xT_psum, 1)


def transpose_x_scalar(nc, act, s, k):
    for b in range(KD // 2):
        act.wait_ge(s.xT_psum, b + 1)
        nc.scalar.copy(k.xT[:, 2 * b:2 * b + 2, :].rearrange("p c t -> p (c t)"),
                       k.psum[:, b, :]).then_inc(s.xT, 1)



def expert_semaphores(ctx, nc, layer):
    return semaphores(ctx, nc, f"experts{layer}", "router gu0 gu1 dn0 dn1")


def load_up(sp, k, d, layer, slot, e, sem):
    sp.dma_start(k.w_up[slot][:, 0:1].rearrange("p a k f -> p a (k f)"),
                 d.moe_w_gate[layer, bass.ds(e, 1)].rearrange("e (p k) f -> p e (k f)", k=KD)).then_inc(sem, 16)
    sp.dma_start(k.w_up[slot][:, 1:2].rearrange("p a k f -> p a (k f)"),
                 d.moe_w_up[layer, bass.ds(e, 1)].rearrange("e (p k) f -> p e (k f)", k=KD)).then_inc(sem, 16)


def load_down(sp, k, d, layer, slot, e, sem):
    sp.dma_start(k.w_down[slot][:], d.moe_w_down[layer, bass.ds(e, 1)].rearrange("e (j p) n -> p (e j) n", p=P)).then_inc(sem, 16)


def load_early_experts(sp, k, d, layer, x, places_0_1_free):
    sp.dma_start(k.router_w[:], d.router_w[layer].rearrange("(p k) e -> p k e", k=KD)).then_inc(x.router, 16)
    sp.dma_start(k.router_b[:], d.router_b[layer:layer + 1].to_broadcast([P, N_EXP])).then_inc(x.router, 16)
    for e in range(2):
        places_0_1_free(e)
        load_up(sp, k, d, layer, e, e, x.gu0)
    for e in range(2):
        load_down(sp, k, d, layer, e, e, x.dn0)


def moe_layer(nc, k, d, layer, x, out=None, fetch_next=None):
    ctx = ExitStack()
    names = ("tables shared_w xT_psum xT dve pool parts logits scores selected places routed table_sb table_dram "
             "table_back shared_up shared_h shared_silu shared_hT_psum shared_hT "
             "match pair_gates slot_gates gates_read silu h up gather_a gather_b xsel_a xsel_b turned turned_sb "
             "gate_parts high_a high_b rest_a rest_b middle split score_T score_T_psum "
             "down_a down_b combined "
             "v_back v_load v_shifted v_match v_silu v_h v_up v_gather v_xsel_a v_xsel_b v_turned v_turned_sb v_down v_high v_rest v_middle v_split v_gates_read "
             "v_combined y_ready variance root rstd centred gained normed normed_first stored eps")
    s = semaphores(ctx, nc, f"moe{layer}", names)

    def sb(name, shape, dt=F32):
        return ctx.enter_context(nc.sbuf_tensor(f"moe{layer}_{name}", shape, dt))

    w = named(**layer_norm_tiles(sb))
    part = [sb(f"x_part{i}", [P, NT, D], BF16) for i in range(3)]
    rest = w.resid
    match = [sb(f"match{i}", [P, NT, 2, SLOTS], BF16) for i in range(2)]
    pair_gates = [sb(f"pair_gates{i}", [P, NT, 2, 3], BF16) for i in range(2)]
    xsel = sb("x_selected", [P, KD, P])
    shared_w = sb("shared_weights", [P, 2, KD, FE])
    shared_wd = k.mixT[:].rearrange("p (j c) t -> p j (c t)", j=KF)
    silu = sb("silu", [P, FE])
    h = sb("h", [P, FE])
    slot_gate = sb("slot_gate", [P, 1])
    hT = sb("hT", [P, KF * P])
    matchT = [sb(f"matchT{i}", [P, S], BF16) for i in range(2)]
    high = sb("out_high", [P, D], BF16)
    middle = sb("out_middle", [P, D], BF16)
    low = sb("out_low", [P, D], BF16)
    out_rest = sb("out_rest", [P, D])
    score_T = sb("score_T", [N_EXP, S])
    score = sb("score", [P, NT, N_EXP])
    biased = sb("biased", [P, NT, N_EXP])
    top8 = sb("top8", [P, NT * GROUPS, 8])
    gscore = sb("group_score", [P, NT, GROUPS])
    cmp_a = sb("cmp_a", [P, NT, GROUPS, GROUPS])
    cmp_b = sb("cmp_b", [P, NT, GROUPS, GROUPS])
    rank = sb("rank", [P, NT, GROUPS])
    gmask = sb("gmask", [P, NT, GROUPS])
    goff = sb("goff", [P, NT, GROUPS])
    best8 = sb("best8", [P, NT, 8])
    taken = sb("taken", [P, NT, N_EXP])
    sel = sb("sel", [P, NT, N_EXP])
    sel_bf = sb("sel_bf", [P, NT, N_EXP], BF16)
    gsum = sb("gsum", [P, NT])
    ginv = sb("ginv", [P, NT])
    gate = sb("gate", [P, NT, N_EXP])
    gate_part = sb("gate_parts", [P, NT, N_EXP, 3], BF16)
    place = sb("place", [P, NT, N_EXP])
    sh = sb("shared_h", [P, NT, FE])
    ssilu = sb("shared_silu", [P, NT, FE])
    shT = sb("shared_hT", [P, NT, KF, P])
    count = sb("expert_tokens", [MAX_OVER, N_EXP])
    c1 = sb("over_64", [MAX_OVER, N_EXP])
    c2 = sb("over_128", [MAX_OVER, N_EXP])
    c3 = sb("extra_before", [MAX_OVER, N_EXP])
    table = sb("table", [MAX_OVER, 4])
    table_i = sb("table_i", [MAX_OVER, 4], I32)
    back_i = sb("back_i", [P, MAX_OVER, 4], I32)
    back = sb("back", [P, MAX_OVER, 4])
    shifted = sb("shifted", [P, NT, 2])

    up_ps, turn_ps = k.psum[:, 6, :], k.psum[:, 7, :]

    def up_view(slot, kk):
        return k.w_up[slot][:, :, kk, :]

    def pe_up(slots):
        for kk in range(KD):
            for e in range(2):
                last = nc.tensor.matmul(k.psum[e * SLOTS:(e + 1) * SLOTS, 6, :], xsel[:, kk, e * SLOTS:(e + 1) * SLOTS],
                                        up_view(slots[e], kk), start=kk == 0, stop=kk == KD - 1)
        return last

    def pe_gather(bank, m):
        for c in range(4):
            kk = 4 * (bank - 4) + c
            for i in range(3):
                for t in range(NT):
                    last = nc.tensor.matmul(k.psum[:, bank, c * P:(c + 1) * P], part[i][:, t, kk:D:KD],
                                            m[:, t, :, :].rearrange("p e s -> p (e s)"),
                                            start=i == 0 and t == 0, stop=i == 2 and t == NT - 1)
        return last

    def pe_slot_gates(m, g):
        for e in range(2):
            for t in range(NT):
                last = nc.tensor.matmul(k.psum[e * SLOTS:(e + 1) * SLOTS, 7, 0:3], m[:, t, e, :], g[:, t, e, :],
                                        start=t == 0, stop=t == NT - 1)
        return last

    def pe_turn(m):
        for j in range(KF):
            nc.tensor.transpose(turn_ps[:, j * P:(j + 1) * P], h[:, j * P:(j + 1) * P], k.ident[:])
        for t in range(NT):
            last = nc.tensor.matmul(turn_ps[:, FE + t * P:FE + (t + 1) * P],
                                    m[:, t, :, :].rearrange("p e s -> p (e s)"), k.ident_bf[:], start=True, stop=True)
        return last

    def pe_combine(par, t, halves=(0, 1), begin=False):
        for half in halves:
            for o in (high, middle, low):
                last = nc.tensor.matmul(k.psum[:, 2 * t + half, :], matchT[par][:, t * P:(t + 1) * P],
                                        o[:, half * BANK:(half + 1) * BANK], start=begin and o is high, stop=True,
                                        skip_group_check=True)
        return last

    def pe_down(slots, half, bank):
        for j in range(KF):
            for e in range(2):
                last = nc.tensor.matmul(k.psum[e * SLOTS:(e + 1) * SLOTS, bank, :], hT[:, j * P + e * SLOTS:j * P + (e + 1) * SLOTS],
                                        k.w_down[slots[e]][:, j, half * BANK:(half + 1) * BANK],
                                        start=j == 0, stop=j == KF - 1)
        return last

    def flat(ap):
        return ap.rearrange("p a b -> p (a b)")

    gu, dn = [x.gu0, x.gu1], [x.dn0, x.dn1]

    with nc.Block(no_gpsimd_drain=True) as block:
        @block.sync
        def _(sp):
            sp.dma_start(shared_w[:, 0], d.shared_w_gate[layer].rearrange("(p k) f -> p k f", k=KD)).then_inc(s.shared_w, 16)
            sp.dma_start(shared_w[:, 1], d.shared_w_up[layer].rearrange("(p k) f -> p k f", k=KD)).then_inc(s.shared_w, 16)
            sp.dma_start(shared_wd, d.shared_w_down[layer].rearrange("(j p) n -> p j n", p=P)).then_inc(s.shared_w, 16)
            load_down(sp, k, d, layer, 2, 2, dn[1])
            load_up(sp, k, d, layer, 3, 3, gu[1])
            load_down(sp, k, d, layer, 3, 3, dn[1])
            for i, src in enumerate((d.ln2_g, d.ln2_b)):
                sp.dma_start(k.ln[:, i, :], src[layer:layer + 1].to_broadcast([P, D])).then_inc(s.tables, 16)

            def refill_up(p, i, par):
                sp.wait_ge(s.up, p - 1)
                for j in range(2):
                    load_up(sp, k, d, layer, 2 * par + j, 4 * i + 2 * par + j, gu[par])

            def refill_down(p, i, par):
                sp.wait_ge(s.down_b, p - 1)
                for j in range(2):
                    load_down(sp, k, d, layer, 2 * par + j, 4 * i + 2 * par + j, dn[par])

            with sp.Fori(1, PAIRS // 2) as i:
                for par in range(2):
                    refill_up(2 * i + par, i, par)
                    refill_down(2 * i + par, i, par)
            sp.wait_ge(s.table_sb, 1)
            sp.dma_start(k.over_dram, table_i[:]).then_inc(s.table_dram, 16)
            sp.wait_ge(s.table_dram, 16)
            sp.dma_start(back_i[:].rearrange("p b c -> p (b c)"),
                         k.over_dram.rearrange("b c -> (b c)").unsqueeze(0).to_broadcast([P, MAX_OVER * 4])
                         ).then_inc(s.table_back, 16)
            sp.wait_ge(s.table_back, 16)
            n_over = sp.value_load(k.over_dram[0:1, 2:3], min_val=0, max_val=MAX_OVER)
            with sp.If(n_over > 0):
                sp.wait_ge(s.combined, PAIRS)
                with sp.Fori(0, (n_over + 1) // 2) as i:
                    experts = [sp.value_load(k.over_dram[bass.ds(2 * i + j, 1), 0:1], min_val=0,
                                             max_val=N_EXP - 1) for j in range(2)]
                    sp.wait_ge(s.v_combined, i + 1)
                    for j, e in enumerate(experts):
                        load_up(sp, k, d, layer, 2 + j, e, s.v_load)
                        load_down(sp, k, d, layer, 2 + j, e, s.v_load)
            if fetch_next is not None:
                fetch_next(sp, s)
            if out is not None:
                for t in range(NT):
                    sp.wait_ge((s.normed_first, s.normed)[t], 1)
                    sp.dma_start(out[t * P:(t + 1) * P, :], k.x[:, t, :]).then_inc(s.stored, 16)
                sp.wait_ge(s.stored, 16 * NT)

        @block.tensor
        def _(pe):
            transpose_x_tensor(nc, pe, s, k)
            pe.wait_ge(x.router, 32)
            pe.wait_ge(s.xT, KD // 2)
            for kk in range(KD):
                last = nc.tensor.matmul(k.psum[0:N_EXP, 4, 0:S], k.router_w[:, kk, :], k.xT[:, kk, :],
                                        start=kk == 0, stop=kk == KD - 1)
            last.then_inc(s.logits, 1)
            def shared_up(t, rows):
                for kk in rows:
                    last = nc.tensor.matmul(k.psum[:, (6, 5)[t], :], k.xT[:, kk, t * P:(t + 1) * P], shared_w[:, :, kk, :],
                                            start=kk == 0, stop=kk == KD - 1)
                return last

            pe.wait_ge(s.score_T, 1)
            for t in range(NT):
                last = nc.tensor.transpose(k.psum[:, 4, S + t * N_EXP:S + (t + 1) * N_EXP],
                                           score_T[:, t * P:(t + 1) * P], k.ident[0:N_EXP, 0:N_EXP])
            last.then_inc(s.score_T_psum, 1)
            pe.wait_ge(s.shared_w, 16 * 3)
            shared_up(0, range(KD)).then_inc(s.shared_up, 1)
            pe.wait_ge(s.selected, 1)
            for t in range(NT):
                nc.tensor.matmul(k.psum[:, 4, t * N_EXP:(t + 1) * N_EXP], k.before_bf[:], sel_bf[:, t, :],
                                 start=True, stop=t == 0)
                if t:
                    nc.tensor.matmul(k.psum[:, 4, t * N_EXP:(t + 1) * N_EXP], k.ones_bf[:], sel_bf[:, 0, :],
                                     start=False, stop=True)
            for t in range(NT):
                last = nc.tensor.matmul(k.psum[0:MAX_OVER, 4, 2 * N_EXP:3 * N_EXP], k.ones_bf[:, 0:MAX_OVER],
                                        sel_bf[:, t, :], start=t == 0, stop=t == NT - 1)
            last.then_inc(s.places, 1)
            pe.wait_ge(s.parts, 1)
            pe.wait_ge(s.routed, 1)
            pe.wait_ge(s.match, 1)
            pe_gather(4, match[0]).then_inc(s.gather_a, 1)
            pe_gather(5, match[0]).then_inc(s.gather_b, 1)
            pe.wait_ge(s.pair_gates, 1)
            pe_slot_gates(match[0], pair_gates[0]).then_inc(s.slot_gates, 1)

            def pair(p, turn, par, first=False, second=False, final=False):
                slots = (2 * par, 2 * par + 1)
                pe.wait_ge(s.xsel_a, p + 1)
                pe.wait_ge(s.xsel_b, p + 1)
                pe.wait_ge(gu[par], 64 * (turn + 1))
                if first:
                    pe.wait_ge(s.shared_h, 1)
                else:
                    pe.wait_ge(s.h, p)
                pe_up(slots).then_inc(s.up, 1)
                if not final:
                    pe.wait_ge(s.match, p + 2)
                    pe.wait_ge(s.pair_gates, p + 2)
                    if not first:
                        pe.wait_ge(s.rest_b, p)
                    pe.wait_ge(s.gates_read, p + 1)
                    pe_slot_gates(match[1 - par], pair_gates[1 - par]).then_inc(s.slot_gates, 1)
                    if not first:
                        pe.wait_ge(s.rest_a, p)
                    pe_gather(4, match[1 - par]).then_inc(s.gather_a, 1)
                    pe_gather(5, match[1 - par]).then_inc(s.gather_b, 1)
                    pe.wait_ge(s.gates_read, p + 2)
                else:
                    pe.wait_ge(s.rest_b, p)
                pe.wait_ge(s.h, p + 1)
                pe_turn(match[par]).then_inc(s.turned, 1)
                if not first:
                    pe.wait_ge(s.split, 2 * p)
                    pe_combine(1 - par, 0, begin=second)
                    pe_combine(1 - par, 1, begin=second).then_inc(s.combined, 1)
                pe.wait_ge(s.turned_sb, 2 * p + 2)
                pe.wait_ge(dn[par], 32 * (turn + 1))
                if not final:
                    pe.wait_ge(s.xsel_a, p + 2)
                else:
                    pe.wait_ge(s.rest_a, p)
                pe_down(slots, 0, 4).then_inc(s.down_a, 1)
                pe_down(slots, 1, 7).then_inc(s.down_b, 1)

            pair(0, 0, 0, first=True)
            pair(1, 0, 1, second=True)
            with pe.Fori(1, PAIRS // 4) as i:
                pair(2 * i, i, 0)
                pair(2 * i + 1, i, 1)
            pe.wait_ge(s.xsel_b, PAIRS // 2 + 1)
            shared_up(1, range(KD)).then_inc(s.shared_up, 1)
            pe.wait_ge(s.shared_h, NT)
            for t in range(NT):
                for j in range(KF):
                    last = nc.tensor.transpose(up_ps[:, (t * KF + j) * P:(t * KF + j + 1) * P],
                                               sh[:, t, j * P:(j + 1) * P], k.ident[:])
            last.then_inc(s.shared_hT_psum, 1)
            pe.wait_ge(s.shared_hT, 1)
            for t in range(NT):
                for half in range(2):
                    for j in range(KF):
                        nc.tensor.matmul(k.psum[:, 2 * t + half, :], shT[:, t, j, :],
                                         shared_wd[:, j, half * BANK:(half + 1) * BANK],
                                         start=False, stop=True, skip_group_check=True)
            with pe.Fori(PAIRS // 4, PAIRS // 2 - 1) as i:
                pair(2 * i, i, 0)
                pair(2 * i + 1, i, 1)
            pair(PAIRS - 2, PAIRS // 2 - 1, 0)
            pair(PAIRS - 1, PAIRS // 2 - 1, 1, final=True)
            pe.wait_ge(s.table_back, 16)
            n_over = pe.value_load(k.over_dram[0:1, 2:3], min_val=0, max_val=MAX_OVER)
            pe.wait_ge(s.split, 2 * PAIRS)
            with pe.If(n_over < 1):
                for t in range(NT):
                    for half in range(2):
                        pe_combine(1, t, (half,)).then_inc(s.y_ready, 1)
            with pe.If(n_over > 0):
                for t in range(NT):
                    pe_combine(1, t).then_inc(s.combined, 1)
                nc.tensor.transpose(k.psum[:, 6, 0:P], k.ident[:], k.ident[:]).then_inc(s.v_combined, 1)
                with pe.Fori(0, (n_over + 1) // 2) as i:
                    pe.wait_ge(s.v_match, 2 * i + 2)
                    pe_slot_gates(match[0], pair_gates[0])
                    pe_gather(4, match[0])
                    pe_gather(5, match[0]).then_inc(s.v_gather, 1)
                    pe.wait_ge(s.v_xsel_a, i + 1)
                    pe.wait_ge(s.v_xsel_b, i + 1)
                    pe.wait_ge(s.v_load, 96 * i + 96)
                    pe_up((2, 3)).then_inc(s.v_up, 1)
                    pe.wait_ge(s.v_h, i + 1)
                    pe_turn(match[0]).then_inc(s.v_turned, 1)
                    pe.wait_ge(s.v_turned_sb, 2 * i + 2)
                    pe_down((2, 3), 0, 4)
                    pe_down((2, 3), 1, 7).then_inc(s.v_down, 1)
                    pe.wait_ge(s.v_split, i + 1)
                    pe_combine(0, 0)
                    pe_combine(0, 1).then_inc(s.v_combined, 1)
                nc.tensor.transpose(k.psum[:, 6, 0:P], k.ident[:], k.ident[:]).then_inc(s.y_ready, 2 * NT)

        @block.scalar
        def _(act):
            transpose_x_scalar(nc, act, s, k)
            act.wait_ge(s.logits, 1)
            nc.scalar.activation(score_T[:], k.psum[0:N_EXP, 4, 0:S], ACT.Sigmoid).then_inc(s.score_T, 1)
            act.wait_ge(s.score_T_psum, 1)
            nc.scalar.copy(flat(score[:]), k.psum[:, 4, S:S + NT * N_EXP]).then_inc(s.scores, 1)

            def shared_silu(t):
                act.wait_ge(s.shared_up, t + 1)
                nc.scalar.activation(ssilu[:, t, :], k.psum[:, (6, 5)[t], 0:FE], ACT.Silu).then_inc(s.shared_silu, 1)

            shared_silu(0)
            act.wait_ge(s.gather_a, 1)
            nc.scalar.copy(flat(xsel[:, 0:4, :]), k.psum[:, 4, :]).then_inc(s.xsel_a, 1)

            def pair(p, par, final=False):
                act.wait_ge(s.up, p + 1)
                nc.scalar.activation(silu[:], up_ps[:, 0:FE], ACT.Silu).then_inc(s.silu, 1)
                if not final:
                    act.wait_ge(s.gather_a, p + 2)
                    nc.scalar.copy(flat(xsel[:, 0:4, :]), k.psum[:, 4, :]).then_inc(s.xsel_a, 1)
                act.wait_ge(s.turned, p + 1)
                nc.scalar.copy(hT[:], turn_ps[:, 0:FE]).then_inc(s.turned_sb, 1)
                nc.scalar.copy(matchT[par][:], turn_ps[:, FE:]).then_inc(s.turned_sb, 1)
                act.wait_ge(s.down_a, p + 1)
                nc.scalar.copy(high[:, 0:BANK], k.psum[:, 4, :]).then_inc(s.high_a, 1)
                act.wait_ge(s.down_b, p + 1)
                nc.scalar.copy(high[:, BANK:], turn_ps).then_inc(s.high_b, 1)
                act.wait_ge(s.rest_a, p + 1)
                nc.scalar.copy(middle[:, 0:BANK], out_rest[:, 0:BANK]).then_inc(s.middle, 1)
                act.wait_ge(s.rest_b, p + 1)
                nc.scalar.copy(middle[:, BANK:], out_rest[:, BANK:]).then_inc(s.middle, 1)

            with act.Fori(0, PAIRS // 4) as i:
                pair(2 * i, 0)
                pair(2 * i + 1, 1)
            shared_silu(1)
            with act.Fori(PAIRS // 4, PAIRS // 2 - 1) as i:
                pair(2 * i, 0)
                pair(2 * i + 1, 1)
            pair(PAIRS - 2, 0)
            pair(PAIRS - 1, 1, final=True)

            act.wait_ge(s.table_back, 16)
            n_over = act.value_load(k.over_dram[0:1, 2:3], min_val=0, max_val=MAX_OVER)
            with act.If(n_over > 0):
                with act.Fori(0, (n_over + 1) // 2) as i:
                    act.wait_ge(s.v_gather, i + 1)
                    nc.scalar.copy(flat(xsel[:, 0:4, :]), k.psum[:, 4, :]).then_inc(s.v_xsel_a, 1)
                    act.wait_ge(s.v_up, i + 1)
                    nc.scalar.activation(silu[:], up_ps[:, 0:FE], ACT.Silu).then_inc(s.v_silu, 1)
                    act.wait_ge(s.v_turned, i + 1)
                    nc.scalar.copy(hT[:], turn_ps[:, 0:FE]).then_inc(s.v_turned_sb, 1)
                    nc.scalar.copy(matchT[0][:], turn_ps[:, FE:]).then_inc(s.v_turned_sb, 1)
                    act.wait_ge(s.v_down, i + 1)
                    nc.scalar.copy(high[:, 0:BANK], k.psum[:, 4, :]).then_inc(s.v_high, 1)
                    nc.scalar.copy(high[:, BANK:], turn_ps).then_inc(s.v_high, 1)
            act.wait_ge(s.eps, 1)
            layer_norm_scalar(nc, act, s, w)

        @block.gpsimd
        def _(pool):
            def gates_of(p, par):
                nc.gpsimd.tensor_tensor(pair_gates[par][:], gate_part[:, :, bass.ds(2 * p, 2), :], ones3, ALU.mult
                                        ).then_inc(s.pair_gates, 1)

            def pair(p, par, last_gates=False):
                if not last_gates:
                    pool.wait_ge(s.slot_gates, p + 1)
                    gates_of(p + 2, par)
                for half in range(2):
                    cols = slice(half * BANK, (half + 1) * BANK)
                    pool.wait_ge(s.middle, 2 * p + half + 1)
                    nc.gpsimd.tensor_tensor(low[:, cols], out_rest[:, cols], middle[:, cols], ALU.subtract).then_inc(s.split, 1)

            ones3 = over(over(k.ones_bf[:, 0:3], 1, 2), 1, NT)
            pool.wait_ge(s.gate_parts, 1)
            gates_of(0, 0)
            gates_of(1, 1)
            with pool.Fori(0, PAIRS // 2 - 1) as i:
                pair(2 * i, 0)
                pair(2 * i + 1, 1)
            pair(PAIRS - 2, 0, last_gates=True)
            pair(PAIRS - 1, 1, last_gates=True)
            pool.wait_ge(s.tables, 32)
            layer_norm_gpsimd(nc, pool, s, k, w)

        @block.vector
        def _(dve):
            step = Chain(dve, s.dve)
            nc.vector.memset(w.ln_eps[:], LN_EPS).then_inc(s.eps, 1)
            step(nc.vector.tensor_copy(part[0][:], k.x[:]))
            step(nc.vector.tensor_tensor(rest[:], k.x[:], part[0][:], ALU.subtract))
            step(nc.vector.tensor_copy(part[1][:], rest[:]))
            step(nc.vector.tensor_tensor(rest[:], rest[:], part[1][:], ALU.subtract))
            nc.vector.tensor_copy(part[2][:], rest[:]).then_inc(s.parts, 1)

            def shared_h(t):
                dve.wait_ge(s.shared_silu, t + 1)
                nc.vector.tensor_tensor(sh[:, t, :], ssilu[:, t, :], k.psum[:, (6, 5)[t], FE:2 * FE],
                                        ALU.mult).then_inc(s.shared_h, 1)

            dve.wait_ge(s.scores, 1)
            dve.wait_ge(x.router, 32)
            step(nc.vector.tensor_tensor(biased[:], score[:], over(k.router_b[:], 1, NT), ALU.add))
            for t in range(NT):
                for g in range(GROUPS):
                    last = nc.vector.max(top8[:, t * GROUPS + g, :], biased[:, t, g * GROUP:(g + 1) * GROUP])
            step(last)
            step(nc.vector.tensor_tensor(flat(gscore[:]), top8[:, :, 0], top8[:, :, 1], ALU.add))
            other, own = over(gscore[:], 2, GROUPS), over(gscore[:], 3, GROUPS)
            step(nc.vector.tensor_tensor(cmp_a[:], other, own, ALU.is_gt))
            step(nc.vector.tensor_tensor(cmp_b[:], other, own, ALU.is_equal))
            step(nc.vector.tensor_tensor(cmp_b[:], cmp_b[:], over(k.earlier8[:], 1, NT), ALU.mult))
            step(nc.vector.tensor_tensor(cmp_a[:], cmp_a[:], cmp_b[:], ALU.add))
            step(nc.vector.tensor_reduce(rank[:], cmp_a[:], AX.X, ALU.add))
            step(nc.vector.tensor_scalar(gmask[:], rank[:], TOP_GROUPS - 0.5, None, ALU.is_lt))
            step(nc.vector.tensor_scalar(goff[:], gmask[:], 1.0, -OFF_GROUP, ALU.subtract, ALU.mult))
            grouped = biased[:].rearrange("p t (g e) -> p t g e", g=GROUPS)
            step(nc.vector.tensor_tensor(grouped, grouped, over(gmask[:], 3, GROUP), ALU.mult))
            step(nc.vector.tensor_tensor(grouped, grouped, over(goff[:], 3, GROUP), ALU.add))
            for t in range(NT):
                step(nc.vector.max(best8[:, t, :], biased[:, t, :]))
                step(nc.vector.match_replace(taken[:, t, :], best8[:, t, :], biased[:, t, :], TAKEN))
            step(nc.vector.tensor_tensor(sel[:], biased[:], taken[:], ALU.not_equal))
            nc.vector.tensor_copy(sel_bf[:], sel[:]).then_inc(s.selected, 1)
            dve.wait_ge(s.places, 1)
            for t in range(NT):
                step(nc.vector.scalar_tensor_tensor(place[:, t, :], k.psum[:, 4, t * N_EXP:(t + 1) * N_EXP], 1.0,
                                                    sel[:, t, :], ALU.add, ALU.mult))
            step(nc.vector.tensor_copy(count[:], k.psum[0:MAX_OVER, 4, 2 * N_EXP:3 * N_EXP]))
            nc.vector.engine_nop().then_inc(s.routed, 1)

            def match_matrix(p, par):
                slot = over(over(k.slot_no[:], 1, 2), 1, NT)
                nc.vector.tensor_tensor(match[par][:], slot, over(place[:, :, bass.ds(2 * p, 2)], 3, SLOTS),
                                        ALU.is_equal).then_inc(s.match, 1)

            match_matrix(0, 0)
            match_matrix(1, 1)
            step(nc.vector.tensor_tensor(gate[:], score[:], sel[:], ALU.mult))
            step(nc.vector.tensor_reduce(gsum[:], gate[:], AX.X, ALU.add))
            step(nc.vector.reciprocal(ginv[:], gsum[:]))
            for t in range(NT):
                step(nc.vector.tensor_scalar(gate[:, t, :], gate[:, t, :], ginv[:, t:t + 1], ROUTED_SCALE, ALU.mult, ALU.mult))
            step(nc.vector.tensor_copy(gate_part[:, :, :, 0], gate[:]))
            step(nc.vector.tensor_tensor(gate[:], gate[:], gate_part[:, :, :, 0], ALU.subtract))
            step(nc.vector.tensor_copy(gate_part[:, :, :, 1], gate[:]))
            nc.vector.tensor_tensor(gate_part[:, :, :, 2], gate[:], gate_part[:, :, :, 1], ALU.subtract).then_inc(s.gate_parts, 1)
            shared_h(0)
            dve.wait_ge(s.gather_b, 1)
            nc.vector.tensor_copy(flat(xsel[:, 4:8, :]), k.psum[:, 5, :]).then_inc(s.xsel_b, 1)
            dve.wait_ge(s.slot_gates, 1)
            nc.vector.tensor_reduce(slot_gate[:], k.psum[:, 7, 0:3], AX.X, ALU.add).then_inc(s.gates_read, 1)
            step(nc.vector.tensor_scalar(c1[:], count[:], SLOTS + 0.5, None, ALU.is_gt))
            step(nc.vector.tensor_scalar(c2[:], count[:], 2 * SLOTS + 0.5, None, ALU.is_gt))
            step(nc.vector.tensor_scalar(c3[:], count[:], 3 * SLOTS + 0.5, None, ALU.is_gt))
            step(nc.vector.tensor_tensor(c1[:], c1[:], c2[:], ALU.add))
            step(nc.vector.tensor_tensor(c1[:], c1[:], c3[:], ALU.add))
            step(nc.vector.memset(c2[:], 0.0))
            step(nc.vector.tensor_tensor_scan(c3[:], c1[:], c2[:], 0.0, ALU.add, ALU.add))
            step(nc.vector.tensor_copy(table[:, 2:3], c3[:, N_EXP - 1:N_EXP]))
            step(nc.vector.tensor_scalar(c2[:], c3[:], k.pass_no[:, 0:1], None, ALU.is_le))
            step(nc.vector.tensor_reduce(table[:, 0:1], c2[:], AX.X, ALU.add))
            step(nc.vector.tensor_tensor(c1[:], c1[:], c2[:], ALU.mult))
            step(nc.vector.tensor_reduce(table[:, 1:2], c1[:], AX.X, ALU.add))
            step(nc.vector.tensor_tensor(table[:, 1:2], k.pass_no[:, 0:1], table[:, 1:2], ALU.subtract))
            step(nc.vector.tensor_scalar(table[:, 1:2], table[:, 1:2], 1.0, float(SLOTS), ALU.add, ALU.mult))
            step(nc.vector.tensor_scalar(table[:, 3:4], table[:, 0:1], N_EXP - 0.5, 4.0 * S, ALU.is_gt, ALU.mult))
            step(nc.vector.tensor_tensor(table[:, 1:2], table[:, 1:2], table[:, 3:4], ALU.add))
            step(nc.vector.tensor_scalar(table[:, 0:1], table[:, 0:1], N_EXP - 1.0, None, ALU.min))
            nc.vector.tensor_copy(table_i[:], table[:]).then_inc(s.table_sb, 1)

            def pair(p, par, first=False, final=False, last_match=False):
                dve.wait_ge(s.silu, p + 1)
                dve.wait_ge(s.gates_read, p + 1)
                nc.vector.scalar_tensor_tensor(h[:], silu[:], slot_gate[:, 0:1], up_ps[:, FE:2 * FE], ALU.mult,
                                               ALU.mult).then_inc(s.h, 1)
                if not final:
                    dve.wait_ge(s.slot_gates, p + 2)
                    dve.wait_ge(s.h, p + 1)
                    nc.vector.tensor_reduce(slot_gate[:], k.psum[:, 7, 0:3], AX.X, ALU.add).then_inc(s.gates_read, 1)
                    dve.wait_ge(s.gather_b, p + 2)
                    nc.vector.tensor_copy(flat(xsel[:, 4:8, :]), k.psum[:, 5, :]).then_inc(s.xsel_b, 1)
                if not last_match:
                    dve.wait_ge(s.turned, p + 1)
                    match_matrix(p + 2, par)
                if not first:
                    dve.wait_ge(s.split, 2 * p)
                dve.wait_ge(s.high_a, p + 1)
                nc.vector.tensor_tensor(out_rest[:, 0:BANK], k.psum[:, 4, :], high[:, 0:BANK], ALU.subtract).then_inc(s.rest_a, 1)
                dve.wait_ge(s.high_b, p + 1)
                nc.vector.tensor_tensor(out_rest[:, BANK:], turn_ps, high[:, BANK:], ALU.subtract).then_inc(s.rest_b, 1)

            pair(0, 0, first=True)
            pair(1, 1)
            with dve.Fori(1, PAIRS // 4) as i:
                pair(2 * i, 0)
                pair(2 * i + 1, 1)
            shared_h(1)
            dve.wait_ge(s.shared_hT_psum, 1)
            nc.vector.tensor_copy(shT[:].rearrange("p t j c -> p (t j c)"), up_ps).then_inc(s.shared_hT, 1)
            with dve.Fori(PAIRS // 4, PAIRS // 2 - 1) as i:
                pair(2 * i, 0)
                pair(2 * i + 1, 1)
            pair(PAIRS - 2, 0, last_match=True)
            pair(PAIRS - 1, 1, final=True, last_match=True)

            dve.wait_ge(s.table_back, 16)
            n_over = dve.value_load(k.over_dram[0:1, 2:3], min_val=0, max_val=MAX_OVER)
            with dve.If(n_over > 0):
                nc.vector.tensor_copy(back[:], back_i[:]).then_inc(s.v_back, 1)
                dve.wait_ge(s.v_back, 1)
                dve.wait_ge(s.combined, PAIRS + 1)
                slot = over(k.slot_no[:], 1, NT)
                with dve.Fori(0, (n_over + 1) // 2) as i:
                    experts = [dve.value_load(k.over_dram[bass.ds(2 * i + j, 1), 0:1], min_val=0,
                                              max_val=N_EXP - 1) for j in range(2)]
                    dve.wait_ge(s.v_combined, i + 1)
                    for j, e in enumerate(experts):
                        nc.vector.tensor_scalar(shifted[:, :, j], place[:, :, bass.ds(e, 1)].rearrange("p t o -> p (t o)"),
                                                back[:, bass.ds(2 * i + j, 1), 1], None, ALU.subtract
                                                ).then_inc(s.v_shifted, 1)
                        dve.wait_ge(s.v_shifted, 4 * i + 2 * j + 1)
                        nc.vector.tensor_tensor(match[0][:, :, j, :], slot, over(shifted[:, :, j], 2, SLOTS),
                                                ALU.is_equal).then_inc(s.v_shifted, 1)
                        dve.wait_ge(s.v_shifted, 4 * i + 2 * j + 2)
                        nc.vector.tensor_tensor(pair_gates[0][:, :, j, :],
                                                gate_part[:, :, bass.ds(e, 1), :].rearrange("p t o c -> p t (o c)"),
                                                over(k.ones_bf[:, 0:3], 1, NT), ALU.mult).then_inc(s.v_match, 1)
                    dve.wait_ge(s.v_gather, i + 1)
                    nc.vector.tensor_reduce(slot_gate[:], k.psum[:, 7, 0:3], AX.X, ALU.add).then_inc(s.v_gates_read, 1)
                    nc.vector.tensor_copy(flat(xsel[:, 4:8, :]), k.psum[:, 5, :]).then_inc(s.v_xsel_b, 1)
                    dve.wait_ge(s.v_silu, i + 1)
                    dve.wait_ge(s.v_gates_read, i + 1)
                    nc.vector.scalar_tensor_tensor(h[:], silu[:], slot_gate[:, 0:1], up_ps[:, FE:2 * FE], ALU.mult,
                                                   ALU.mult).then_inc(s.v_h, 1)
                    dve.wait_ge(s.v_high, 2 * i + 2)
                    nc.vector.tensor_tensor(out_rest[:, 0:BANK], k.psum[:, 4, :], high[:, 0:BANK], ALU.subtract).then_inc(s.v_rest, 1)
                    nc.vector.tensor_tensor(out_rest[:, BANK:], turn_ps, high[:, BANK:], ALU.subtract).then_inc(s.v_rest, 1)
                    dve.wait_ge(s.v_rest, 2 * i + 2)
                    nc.vector.tensor_copy(middle[:], out_rest[:]).then_inc(s.v_middle, 1)
                    dve.wait_ge(s.v_middle, i + 1)
                    nc.vector.tensor_tensor(low[:], out_rest[:], middle[:], ALU.subtract).then_inc(s.v_split, 1)
            dve.wait_ge(s.tables, 32)
            layer_norm_vector(nc, dve, step, s, k, w, s.y_ready, together=True)
    ctx.close()



def flat(ap):
    return ap.rearrange("p a b -> p (a b)")


EV_LAT = Q_LORA + KV_LORA + MLA_R
EV_G = EV_LAT
EV_GATES = EV_G + 3 * GH * GD
EV_Z = EV_GATES + 2 * GH
G_CHUNKS = 3 * GH
ATTENTION, DELTA = range(0, 4), range(4, 8)
QK_CHUNKS = 2 * GH
PAD = CONV_W - 1
TWO_PI_HIGH, TWO_PI_MID = 6.28125, 0.0019350051879882812
TWO_PI_LOW = float(2 * np.pi - TWO_PI_HIGH - TWO_PI_MID)
ROUND = 1.5 * 2.0 ** 23


def columns_of(k, slot):
    return k.w_up[slot][:].rearrange("p a k f -> p (a k f)").rearrange("p (k n) -> p k n", k=KD)


def channel_chunk(nc, k, c, place):
    w = columns_of(k, 1 + c // GH)
    for kk in range(KD):
        last = nc.tensor.matmul(place, w[:, kk, (c % GH) * P:(c % GH + 1) * P], k.xT[:, kk, :],
                                start=kk == 0, stop=kk == KD - 1)
    return last


def causal_convolution(nc, step, e, c, raw, y):
    step(nc.vector.tensor_scalar(y, raw[:, 0:S], e.cols[:, c:c + 1], None, ALU.mult))
    for i in range(1, CONV_W):
        last = nc.vector.scalar_tensor_tensor(y, raw[:, i:i + S], e.cols[:, i * G_CHUNKS + c:i * G_CHUNKS + c + 1],
                                              y, ALU.mult, ALU.add)
        if i < CONV_W - 1:
            step(last)
    return last


def even_first_loads(sp, k, d, first):
    win = d.ev_w_in[0].rearrange("(p k) n -> p k n", k=KD)
    sp.dma_start(k.x[:], d.x.rearrange("b (t p) n -> p (b t) n", p=P)).then_inc(first.x, 16)
    w0 = columns_of(k, 0)
    sp.dma_start(w0[:, :, 0:EV_LAT], win[:, :, 0:EV_LAT]).then_inc(first.w0, 16)
    sp.dma_start(w0[:, :, EV_LAT:EV_LAT + 2 * GH], win[:, :, EV_GATES:EV_Z]).then_inc(first.w0, 16)


def even_project(nc, k, d, e, first):
    ctx = ExitStack()
    s = semaphores(ctx, nc, "evp", "small w1 w2 xT_psum xT vec rows_T rows lat_psum lat g_psum tap conv "
                                   "g freq angle sines")

    def sb(name, shape, dt=F32):
        return ctx.enter_context(nc.sbuf_tensor(f"evp_{name}", shape, dt))

    rows = sb("row_vectors", [CONV_W * G_CHUNKS + 3, P])
    raw = sb("raw", [P, QK_CHUNKS, PAD + S])
    acc = sb("acc", [P, 2, S])
    pos_i = sb("pos_i", [P, NT], I32)
    pos = sb("pos", [P, NT])
    freq = sb("freq", [P, (MLA_R + WD) // 2])
    ang = sb("ang", [P, NT, (MLA_R + WD) // 2])
    turns = sb("turns", [P, NT, (MLA_R + WD) // 2])
    n_conv = CONV_W * G_CHUNKS
    win = d.ev_w_in[0].rearrange("(p k) n -> p k n", k=KD)

    with nc.Block(no_gpsimd_drain=True) as block:
        @block.sync
        def _(sp):
            sp.dma_start(rows[0:n_conv, :], d.gdn_conv[0].rearrange("w (c p) -> (w c) p", p=P)).then_inc(s.small, 16)
            sp.dma_start(rows[n_conv:n_conv + 2, :], d.mla_q_norm[0].rearrange("(c p) -> c p", p=P)).then_inc(s.small, 16)
            sp.dma_start(rows[n_conv + 2:n_conv + 3, :], d.mla_kv_norm).then_inc(s.small, 16)
            with nc.allow_non_contiguous_dma(reason="256 positions"):
                sp.dma_start(pos_i[:], d.positions.rearrange("b (t p) -> p (b t)", p=P)).then_inc(s.small, 16)
            for i, sem in enumerate((s.w1, s.w2, k.s_gv_w)):
                sp.dma_start(columns_of(k, 1 + i), win[:, :, EV_G + i * GH * GD:EV_G + (i + 1) * GH * GD]).then_inc(sem, 16)
            sp.wait_ge(s.lat_psum, NT)
            sp.dma_start(columns_of(k, 0), win[:, :, EV_Z:EV_Z + GH * GD]).then_inc(k.s_z_w, 16)
            sp.dma_start(k.w_down[2][:].rearrange("p j n -> p (j n)")[:, 0:2 * MLA_H * MLA_QK].rearrange("p (c n) -> p c n", c=2),
                         d.mla_w_qb[0].rearrange("(c p) n -> p c n", p=P)).then_inc(k.s_mla_w, 16)
            sp.dma_start(k.w_down[3][:, 0, :], d.mla_w_kvb[0]).then_inc(k.s_mla_w, 16)

        @block.gpsimd
        def _(pool):
            half_m, half_s = MLA_R // 2, WD // 2
            for i in range(half_m):
                nc.gpsimd.memset(freq[:, i:i + 1], float(np.float32(ROPE_THETA) ** -np.float32(2 * i / MLA_R)))
            for i in range(half_s):
                last = nc.gpsimd.memset(freq[:, half_m + i:half_m + i + 1],
                                        float(np.float32(ROPE_THETA) ** -np.float32(2 * i / WD)))
            last.then_inc(s.freq, 1)

        @block.tensor
        def _(pe):
            pe.wait_ge(first.x, 16)
            transpose_x_tensor(nc, pe, s, k)
            pe.wait_ge(s.small, 64)
            nr = n_conv + 3
            nc.tensor.transpose(k.psum[:, 4, 0:nr], rows[:, :], k.ident[0:nr, 0:nr]).then_inc(s.rows_T, 1)
            pe.wait_ge(first.w0, 32)
            pe.wait_ge(s.xT, KD // 2)
            w = columns_of(k, 0)
            for t in range(NT):
                for kk in range(KD):
                    last = nc.tensor.matmul(k.psum[:, 5 + t, 0:EV_LAT + 2 * GH], k.xT[:, kk, t * P:(t + 1) * P],
                                            w[:, kk, 0:EV_LAT + 2 * GH], start=kk == 0, stop=kk == KD - 1)
                last.then_inc(s.lat_psum, 1)
            for c in range(QK_CHUNKS):
                pe.wait_ge((s.w1, s.w2)[c // GH], 16)
                if c >= 4:
                    pe.wait_ge(s.tap, c - 3)
                channel_chunk(nc, k, c, k.psum[:, c % 4, 0:S]).then_inc(s.g_psum, 1)

        @block.scalar
        def _(act):
            transpose_x_scalar(nc, act, s, k)
            act.wait_ge(s.rows_T, 1)
            nc.scalar.copy(e.cols[:], k.psum[:, 4, 0:n_conv + 3]).then_inc(s.rows, 1)
            for t in range(NT):
                act.wait_ge(s.lat_psum, t + 1)
                nc.scalar.copy(e.lat[:, t, :], k.psum[:, 5 + t, 0:EV_LAT + 2 * GH]).then_inc(s.lat, 1)
            act.wait_ge(s.angle, 2)
            nc.scalar.activation(flat(k.sin[:]), flat(ang[:]), ACT.Sin).then_inc(s.sines, 1)
            nc.scalar.activation(flat(k.cos[:]), flat(turns[:]), ACT.Sin, bias=k.eps[:, 1:2], scale=-1.0).then_inc(s.sines, 1)
            for c in range(QK_CHUNKS):
                act.wait_ge(s.g_psum, c + 1)
                nc.scalar.copy(raw[:, c, PAD:], k.psum[:, c % 4, 0:S]).then_inc(s.tap, 1)
                if c >= 1:
                    act.wait_ge(s.conv, c)
                    nc.scalar.activation(e.gT[:, c - 1, :], acc[:, (c - 1) % 2, :], ACT.Silu).then_inc(s.g, 1)
            act.wait_ge(s.conv, QK_CHUNKS)
            nc.scalar.activation(e.gT[:, QK_CHUNKS - 1, :], acc[:, (QK_CHUNKS - 1) % 2, :], ACT.Silu).then_inc(s.g, 1)

        @block.vector
        def _(dve):
            step = Chain(dve, s.vec)
            step(nc.vector.memset(raw[:, :, 0:PAD], 0.0))
            dve.wait_ge(s.small, 64)
            dve.wait_ge(s.freq, 1)
            step(nc.vector.tensor_copy(pos[:], pos_i[:]))
            for t in range(NT):
                step(nc.vector.tensor_scalar(ang[:, t, :], freq[:], pos[:, t:t + 1], None, ALU.mult))
            a, n = flat(ang[:]), flat(turns[:])
            step(nc.vector.tensor_scalar(n, a, float(1 / (2 * np.pi)), None, ALU.mult))
            step(nc.vector.tensor_scalar(n, n, ROUND, None, ALU.add))
            step(nc.vector.tensor_scalar(n, n, ROUND, None, ALU.subtract))
            for part in (TWO_PI_HIGH, TWO_PI_MID, TWO_PI_LOW):
                step(nc.vector.scalar_tensor_tensor(a, n, -part, a, ALU.mult, ALU.add))
            step(nc.vector.tensor_scalar(a, a, 3.1415925, -3.1415925, ALU.min, ALU.max))
            nc.vector.engine_nop().then_inc(s.angle, 1)
            nc.vector.scalar_tensor_tensor(n, a, -1.0, a, ALU.mult, ALU.max).then_inc(s.angle, 1)
            dve.wait_ge(s.rows, 1)
            for c in range(QK_CHUNKS):
                dve.wait_ge(s.tap, c + 1)
                if c >= 2:
                    dve.wait_ge(s.g, c - 1)
                causal_convolution(nc, step, e, c, raw[:, c, :], acc[:, c % 2, :]).then_inc(s.conv, 1)
    ctx.close()



HEADS, HV = 8, 64


def attention_tensor(nc, pe, s, k, a, meanwhile=None):
    for t in range(NT):
        keys = (t + 1) * P
        for b in range(4):
            pe.wait_ge(s.qT, b + 1)
            pe.wait_ge(s.kT, b + 1)
            if t:
                pe.wait_ge(s.masked, b + 1)
            for i in range(2):
                last = nc.tensor.matmul(k.psum[:, 4 + b, i * S:i * S + keys], a.qT(2 * b + i, t),
                                        a.kT(2 * b + i, keys), start=True, stop=True)
            last.then_inc(s.scores, 1)
        if meanwhile is not None:
            meanwhile(t)
        for half in range(2):
            pe.wait_ge(s.scaled, 8 * t + 4 * half + 4)
            if t:
                pe.wait_ge(s.mixed, half + 1)
            for kt in range(t + 1):
                for i in range(4):
                    last = nc.tensor.transpose(k.psum[:, 2 * half + kt, i * P:(i + 1) * P],
                                               a.pr[:, 4 * half + i, kt * P:(kt + 1) * P], k.ident[:])
            last.then_inc(s.turned, 1)
        for half in range(2):
            pe.wait_ge(s.pT, half + 1 if t == 0 else 4 + 2 * half)
            for b in range(2):
                for i in range(2):
                    for kt in range(t + 1):
                        last = nc.tensor.matmul(k.psum[i * HV:(i + 1) * HV, 2 * half, b * P:(b + 1) * P],
                                                a.v(4 * half + 2 * b + i, kt),
                                                a.pT[:, half, kt, (2 * b + i) * P:(2 * b + i + 1) * P],
                                                start=kt == 0, stop=kt == t)
            last.then_inc(s.done, 1)


def attention_scalar(nc, act, s, k, a, meanwhile=None):
    for t in range(NT):
        keys = (t + 1) * P
        act.wait_ge(s.max, t + 1)
        for h in range(HEADS):
            nc.scalar.activation(a.pr[:, h, 0:keys], a.pr[:, h, 0:keys], ACT.Exp, bias=a.nb[:, h:h + 1], scale=a.scale,
                                 accum_out=a.den[:, h:h + 1]).then_inc(s.probs, 1)
        if meanwhile is not None:
            meanwhile(t)
        if a.sinks is not None:
            act.wait_ge(s.sunk, t + 1)
            nc.scalar.activation(a.sunk[:], a.sunk[:], ACT.Exp).then_inc(s.sink_exp, 1)
        for half in range(2):
            act.wait_ge(s.turned, 2 * t + half + 1)
            if t:
                act.wait_ge(s.done, half + 1)
            for kt in range(t + 1):
                nc.scalar.copy(a.pT[:, half, kt, :], k.psum[:, 2 * half + kt, :]).then_inc(s.pT, 1)


def attention_vector(nc, dve, step, s, k, a, meanwhile=None):
    for t in range(NT):
        keys = (t + 1) * P
        for b in range(4):
            dve.wait_ge(s.scores, 4 * t + b + 1)
            if t:
                dve.wait_ge(s.turned, 2)
            nc.vector.tensor_tensor(a.pr[:, 2 * b:2 * b + 2, 0:keys],
                                    k.psum[:, 4 + b, :].rearrange("p (h c) -> p h c", h=2)[:, :, 0:keys],
                                    over(a.mask[:, 2 * P - keys:], 1, 2), ALU.add).then_inc(s.masked, 1)
        dve.wait_ge(s.masked, 4 * t + 4)
        step(nc.vector.tensor_reduce(a.mx[:], a.pr[:, :, 0:keys], AX.X, ALU.max))
        if a.sinks is None:
            nc.vector.tensor_scalar(a.nb[:], a.mx[:], -a.scale, None, ALU.mult).then_inc(s.max, 1)
        else:
            step(nc.vector.scalar_tensor_tensor(a.mx[:], a.mx[:], a.scale, a.sinks[:], ALU.mult, ALU.max))
            nc.vector.tensor_scalar(a.nb[:], a.mx[:], -1.0, None, ALU.mult).then_inc(s.max, 1)
            nc.vector.tensor_tensor(a.sunk[:], a.sinks[:], a.mx[:], ALU.subtract).then_inc(s.sunk, 1)
        for half in range(2):
            hs = slice(4 * half, 4 * half + 4)
            dve.wait_ge(s.probs, 8 * t + 4 * half + 4)
            if a.sinks is not None:
                dve.wait_ge(s.sink_exp, t + 1)
                step(nc.vector.tensor_tensor(a.den[:, hs], a.den[:, hs], a.sunk[:, hs], ALU.add))
            step(nc.vector.reciprocal(a.dinv[:, hs], a.den[:, hs]))
            for h in range(4 * half, 4 * half + 4):
                nc.vector.tensor_scalar(a.pr[:, h, 0:keys], a.pr[:, h, 0:keys], a.dinv[:, h:h + 1], None,
                                        ALU.mult).then_inc(s.scaled, 1)
        if meanwhile is not None:
            meanwhile(t)
        for half in range(2):
            dve.wait_ge(s.done, 2 * t + half + 1)
            nc.vector.tensor_copy(k.mixT[:, a.chunk + 2 * half:a.chunk + 2 * half + 2, t * P:(t + 1) * P],
                                  k.psum[:, 2 * half, 0:2 * P].rearrange("p (b c) -> p b c", b=2)).then_inc(s.mixed, 1)


def rope(nc, step, tmp, first, second, out1, out2, c, sn):
    n = first.shape[1]
    t1, t2, t3, t4 = (x[:, 0:n, :] for x in tmp)
    cc, ss = over(c, 1, n), over(sn, 1, n)
    step(nc.vector.tensor_tensor(t1, first, cc, ALU.mult))
    step(nc.vector.tensor_tensor(t2, second, ss, ALU.mult))
    step(nc.vector.tensor_tensor(t3, second, cc, ALU.mult))
    step(nc.vector.tensor_tensor(t4, first, ss, ALU.mult))
    step(nc.vector.tensor_tensor(out1, t1, t2, ALU.subtract))
    step(nc.vector.tensor_tensor(out2, t3, t4, ALU.add))



def even_latent_attention(nc, k, d, e):
    ctx = ExitStack()
    s = semaphores(ctx, nc, "mla", "gv_psum tap conv gv z0_psum z0 vec root normed latT_psum latT_q latT_kv q_psum kv_psum q_sb kv_sb q_ready k_ready "
                                   "qT_psum kT_psum qT kT scores masked max probs scaled turned pT mixed done act_ssq")

    def sb(name, shape, dt=F32):
        return ctx.enter_context(nc.sbuf_tensor(f"mla_{name}", shape, dt))

    H, QK, HR = MLA_H, MLA_QK, MLA_R // 2
    junk = sb("junk", [P, Q_LORA])
    raw = sb("raw", [P, GH, PAD + S])
    acc = k.mixT[:, 4:8, :]
    ssq = sb("ssq", [P, NT, 2])
    root = sb("root", [P, NT, 2])
    rinv = sb("rinv", [P, NT, 2])
    latT = sb("latT", [P, 3, S])
    qk = sb("qk", [P, 2 * NT * H * QK])
    q = qk[:, 0:NT * H * QK].rearrange("p (t h c) -> p t h c", t=NT, h=H)
    kc = qk[:, NT * H * QK:].rearrange("p (t h c) -> p t h c", t=NT, h=H)
    v = sb("v", [P, NT, H, MLA_V])
    tmp = [sb(f"tmp{i}", [P, H, HR]) for i in range(4)]
    krot = sb("krot", [P, NT, MLA_R])
    qT = sb("qT", [QK, H, S])
    kT = sb("kT", [QK, H, S])
    pr = qk[:, 0:H * S].rearrange("p (h c) -> p h c", h=H)
    pT = sb("pT", [P, 2, 2, H // 2 * P])
    mx = sb("max", [P, H])
    nb = sb("negmax", [P, H])
    den = sb("den", [P, H])
    dinv = sb("dinv", [P, H])
    scale = float(QK ** -0.5)
    a = named(pr=pr, pT=pT, mx=mx, nb=nb, den=den, dinv=dinv, scale=scale, mask=k.no_later, sinks=None, chunk=0,
                        qT=lambda h, t: qT[:, h, t * P:(t + 1) * P], kT=lambda h, keys: kT[:, h, 0:keys],
                        v=lambda h, kt: v[:, kt, h, :])
    wq = k.w_down[2][:].rearrange("p j n -> p (j n)")[:, 0:2 * H * QK].rearrange("p (c n) -> p c n", c=2)
    wkv = k.w_down[3][:, 0, :]
    n_conv = CONV_W * G_CHUNKS

    with nc.Block(no_gpsimd_drain=True) as block:
        @block.sync
        def _(sp):
            for i, src in enumerate((d.ln1_g, d.ln1_b)):
                sp.dma_start(k.ln[:, i, :], src[0:1].to_broadcast([P, D])).then_inc(k.s_out_w, 16)
            sp.dma_start(e.o_gain[:], d.gdn_norm.to_broadcast([P, GD])).then_inc(k.s_gdn_w, 16)
            sp.dma_start(e.a_log[:], d.gdn_a_log.to_broadcast([P, GH])).then_inc(k.s_gdn_w, 16)
            sp.dma_start(e.dt_bias[:], d.gdn_dt_bias.to_broadcast([P, GH])).then_inc(k.s_gdn_w, 16)
            for half in range(2):
                if half:
                    sp.wait_ge(s.gv_psum, GH)
                sp.dma_start(columns_of(k, 2 + half),
                             d.ev_w_out[0][:, half * BANK:(half + 1) * BANK].rearrange("(c p) n -> p c n", p=P)).then_inc(k.s_out_w, 16)

        @block.scalar
        def _(act):
            def take_chunk(c):
                act.wait_ge(s.gv_psum, c + 1)
                nc.scalar.copy(raw[:, c, PAD:], k.psum[:, 4 + c % 2, 0:S]).then_inc(s.tap, 1)

            for t in range(NT):
                nc.scalar.activation(junk[:], e.lat[:, t, 0:Q_LORA], ACT.Square, accum_out=ssq[:, t, 0:1]).then_inc(s.act_ssq, 1)
                act.wait_ge(s.act_ssq, 2 * t + 1)
                nc.scalar.activation(junk[:, 0:KV_LORA], e.lat[:, t, Q_LORA:Q_LORA + KV_LORA], ACT.Square,
                                     accum_out=ssq[:, t, 1:2]).then_inc(s.act_ssq, 1)
                act.wait_ge(s.act_ssq, 2 * t + 2)
            nc.scalar.activation(root[:, :, 0], ssq[:, :, 0], ACT.Sqrt, bias=k.eps[:, 0:1], scale=1.0 / Q_LORA).then_inc(s.root, 1)
            nc.scalar.activation(root[:, :, 1], ssq[:, :, 1], ACT.Sqrt, bias=k.eps[:, 0:1], scale=1.0 / KV_LORA).then_inc(s.root, 1)
            act.wait_ge(s.latT_psum, 1)
            for c in range(2):
                nc.scalar.activation(latT[:, c, :], k.psum[:, 0, c * S:(c + 1) * S], ACT.Copy,
                                     scale=e.cols[:, n_conv + c:n_conv + c + 1]).then_inc(s.latT_q, 1)
            nc.scalar.activation(latT[:, 2, :], k.psum[:, 1, 0:S], ACT.Copy,
                                 scale=e.cols[:, n_conv + 2:n_conv + 3]).then_inc(s.latT_kv, 1)
            take_chunk(0)
            take_chunk(1)
            for t in range(NT):
                act.wait_ge(s.q_psum, t + 1)
                for half in range(2):
                    nc.scalar.copy(q[:, t, 4 * half:4 * half + 4, :].rearrange("p h c -> p (h c)"),
                                   k.psum[:, 2 + 2 * t + half, 0:H * QK // 2]).then_inc(s.q_sb, 1)
                act.wait_ge(s.kv_psum, t + 1)
                for half in range(2):
                    bank = (6 if t == 0 else 0) + half
                    both = k.psum[:, bank, :].rearrange("p (h c) -> p h c", c=MLA_N + MLA_V)
                    nc.scalar.copy(kc[:, t, 4 * half:4 * half + 4, 0:MLA_N], both[:, :, 0:MLA_N]).then_inc(s.kv_sb, 1)
                    nc.scalar.copy(v[:, t, 4 * half:4 * half + 4, :], both[:, :, MLA_N:]).then_inc(s.kv_sb, 1)
            for b in range(4):
                act.wait_ge(s.qT_psum, b + 1)
                nc.scalar.copy(qT[:, 2 * b:2 * b + 2, :].rearrange("p h c -> p (h c)"), k.psum[0:QK, b, :]).then_inc(s.qT, 1)
            def meanwhile(t):
                if t == 0:
                    act.wait_ge(s.z0_psum, 1)
                    nc.scalar.copy(e.z[:, 0, :], k.psum[:, 1, :]).then_inc(s.z0, 1)
                else:
                    take_chunk(2)
                    take_chunk(3)

            attention_scalar(nc, act, s, k, a, meanwhile)
            for c in range(GH):
                act.wait_ge(s.conv, c + 1)
                nc.scalar.activation(e.gT[:, QK_CHUNKS + c, :], acc[:, c, :], ACT.Silu).then_inc(s.gv, 1)

        @block.tensor
        def _(pe):
            pe.wait_ge(k.s_gv_w, 16)
            for c in range(2):
                channel_chunk(nc, k, QK_CHUNKS + c, k.psum[:, 4 + c, 0:S]).then_inc(s.gv_psum, 1)
            pe.wait_ge(s.normed, 1)
            for c in range(3):
                for t in range(NT):
                    last = nc.tensor.transpose(k.psum[:, c // 2, (c % 2) * S + t * P:(c % 2) * S + (t + 1) * P],
                                               e.lat[:, t, c * P:(c + 1) * P], k.ident[:])
            last.then_inc(s.latT_psum, 1)
            pe.wait_ge(k.s_mla_w, 32)
            pe.wait_ge(s.latT_q, 2)
            pe.wait_ge(s.latT_kv, 1)
            pe.wait_ge(s.tap, 2)
            for t in range(NT):
                for half in range(2):
                    for c in range(2):
                        last = nc.tensor.matmul(k.psum[:, 2 + 2 * t + half, 0:H * QK // 2], latT[:, c, t * P:(t + 1) * P],
                                                wq[:, c, half * H * QK // 2:(half + 1) * H * QK // 2], start=c == 0, stop=c == 1)
                last.then_inc(s.q_psum, 1)
                for half in range(2):
                    last = nc.tensor.matmul(k.psum[:, (6 if t == 0 else 0) + half, :], latT[:, 2, t * P:(t + 1) * P],
                                            wkv[:, half * BANK:(half + 1) * BANK], start=True, stop=True)
                last.then_inc(s.kv_psum, 1)
            pe.wait_ge(s.kv_sb, 8)
            pe.wait_ge(s.q_ready, 1)
            for b in range(4):
                for i in range(2):
                    for t in range(NT):
                        last = nc.tensor.transpose(k.psum[0:QK, b, i * S + t * P:i * S + (t + 1) * P], q[:, t, 2 * b + i, :], k.ident[:])
                last.then_inc(s.qT_psum, 1)
            pe.wait_ge(s.k_ready, 1)
            for b in range(4):
                for i in range(2):
                    for t in range(NT):
                        last = nc.tensor.transpose(k.psum[0:QK, 4 + b, i * S + t * P:i * S + (t + 1) * P], kc[:, t, 2 * b + i, :], k.ident[:])
                last.then_inc(s.kT_psum, 1)
            def meanwhile(t):
                if t == 0:
                    pe.wait_ge(k.s_z_w, 16)
                    for kk in range(KD):
                        last = nc.tensor.matmul(k.psum[:, 1, :], k.xT[:, kk, 0:P], columns_of(k, 0)[:, kk, :],
                                                start=kk == 0, stop=kk == KD - 1)
                    last.then_inc(s.z0_psum, 1)
                else:
                    pe.wait_ge(s.masked, 8)
                    for c in range(2, GH):
                        channel_chunk(nc, k, QK_CHUNKS + c, k.psum[:, 2 + c, 0:S]).then_inc(s.gv_psum, 1)
                    pe.wait_ge(s.z0, 1)

            attention_tensor(nc, pe, s, k, a, meanwhile)

        @block.vector
        def _(dve):
            step = Chain(dve, s.vec)
            step(nc.vector.memset(raw[:, :, 0:PAD], 0.0))
            dve.wait_ge(s.root, 2)
            step(nc.vector.reciprocal(flat(rinv[:]), flat(root[:])))
            for t in range(NT):
                step(nc.vector.tensor_scalar(e.lat[:, t, 0:Q_LORA], e.lat[:, t, 0:Q_LORA], rinv[:, t, 0:1], None, ALU.mult))
                step(nc.vector.tensor_scalar(e.lat[:, t, Q_LORA:Q_LORA + KV_LORA], e.lat[:, t, Q_LORA:Q_LORA + KV_LORA],
                                             rinv[:, t, 1:2], None, ALU.mult))
            nc.vector.engine_nop().then_inc(s.normed, 1)
            k0 = Q_LORA + KV_LORA
            for t in range(NT):
                rope(nc, step, tmp, e.lat[:, t:t + 1, k0:k0 + HR], e.lat[:, t:t + 1, k0 + HR:k0 + MLA_R],
                     krot[:, t:t + 1, 0:HR], krot[:, t:t + 1, HR:], k.cos[:, t, 0:HR], k.sin[:, t, 0:HR])
            for t in range(NT):
                step(nc.vector.tensor_copy(kc[:, t, :, MLA_N:], over(krot[:, t, :], 1, H)))
            nc.vector.engine_nop().then_inc(s.k_ready, 1)
            for t in range(NT):
                dve.wait_ge(s.q_sb, 2 * t + 2)
                r1, r2 = q[:, t, :, MLA_N:MLA_N + HR], q[:, t, :, MLA_N + HR:]
                rope(nc, step, tmp, r1, r2, r1, r2, k.cos[:, t, 0:HR], k.sin[:, t, 0:HR])
            nc.vector.engine_nop().then_inc(s.q_ready, 1)
            for b in range(4):
                dve.wait_ge(s.kT_psum, b + 1)
                nc.vector.tensor_copy(kT[:, 2 * b:2 * b + 2, :].rearrange("p h c -> p (h c)"), k.psum[0:QK, 4 + b, :]).then_inc(s.kT, 1)
            def convolve(first):
                for c in (first, first + 1):
                    dve.wait_ge(s.tap, c + 1)
                    causal_convolution(nc, step, e, QK_CHUNKS + c, raw[:, c, :], acc[:, c, :]).then_inc(s.conv, 1)

            attention_vector(nc, dve, step, s, k, a, lambda t: convolve(2 * t))
    ctx.close()



def log1p_exp_vector(nc, dve, step, s, x, out, w):
    step(nc.vector.scalar_tensor_tensor(w.mag, x, -1.0, x, ALU.mult, ALU.max))
    nc.vector.engine_nop().then_inc(s.mag, 1)
    dve.wait_ge(s.exp_mag, 1)
    step(nc.vector.tensor_scalar(w.u, w.t, 1.0, None, ALU.add))
    nc.vector.engine_nop().then_inc(s.one_more, 1)
    step(nc.vector.tensor_scalar(w.d, w.u, 1.0, None, ALU.subtract))
    step(nc.vector.tensor_scalar(w.tiny, w.d, 0.0, None, ALU.is_equal))
    step(nc.vector.tensor_tensor(w.d, w.d, w.tiny, ALU.add))
    step(nc.vector.reciprocal(w.d, w.d))
    step(nc.vector.tensor_tensor(w.tiny, w.tiny, w.t, ALU.mult))
    dve.wait_ge(s.log_u, 1)
    step(nc.vector.tensor_tensor(out, w.log, w.t, ALU.mult))
    step(nc.vector.tensor_tensor(out, out, w.d, ALU.mult))
    step(nc.vector.tensor_tensor(out, out, w.tiny, ALU.add))


def log1p_exp_scalar(nc, act, s, w):
    act.wait_ge(s.mag, 1)
    nc.scalar.activation(w.t, w.mag, ACT.Exp, scale=-1.0).then_inc(s.exp_mag, 1)
    act.wait_ge(s.one_more, 1)
    nc.scalar.activation(w.log, w.u, ACT.Ln).then_inc(s.log_u, 1)


def even_delta_net(nc, k, d, e, x):
    ctx = ExitStack()
    s = semaphores(ctx, nc, "gdn", "z_psum z vec mag exp_mag one_more log_u beta_exp gates wide cum_psum cum exps cumrow decay_in decay "
                                   "nat_psum nat ssq root scaled extra T_psum T_a T_v pair_psum lower prod sub_v sub_a "
                                   "v0 w1 vn0 nw1 st_psum st o0 vn1_psum vn1 o1 o_sb ssq_o root_o on onT mixed "
                                   "alog")

    def sb(name, shape, dt=F32):
        return ctx.enter_context(nc.sbuf_tensor(f"gdn_{name}", shape, dt))

    H, C = GH, GH * GD
    beta, decay = e.lat[:, :, EV_LAT:EV_LAT + H], e.lat[:, :, EV_LAT + H:EV_LAT + 2 * H]
    small = {n: sb(n, [P, NT, H]) for n in ("x", "lp", "beta", "g", "cum", "last", "e_cum", "e_left", "mag", "t", "u", "d", "tiny", "log", "tb")}
    w = named(**{n: small[n][:] for n in small})
    ea = sb("ea", [P, H])
    D_t = sb("decay_t", [P, NT, C])
    Dn = sb("decay_n", [P, NT, C])
    q, kk_, v = (sb(n, [P, NT, C]) for n in ("q", "k", "v"))
    kb = sb("kb", [P, NT, C])
    qg1, kg0, kbg1 = (sb(n, [P, C]) for n in ("qg1", "kg0", "kbg1"))
    qgT1 = sb("qgT1", [P, H, GD])
    ssq = sb("ssq", [P, 2, NT, H])
    rs = sb("rs", [P, 2, NT, H])
    A, B, Cm, Z = (sb(n, [P, NT, C]) for n in ("ma", "mb", "mc", "mz"))
    Lo, AT = (k.xT[:, 4 * i:4 * i + 4, :].rearrange("p c t -> p (c t)").rearrange("p (t c) -> p t c", t=NT)
              for i in range(2))
    wide = Cm
    blk = sb("block8_before", [P, P])
    vn, o = D_t, Dn
    nw1 = qg1
    st = sb("state", [P, C])
    qT, kT, kbT = e.gT[:, 0:H, :], e.gT[:, H:2 * H, :], e.gT[:, 2 * H:3 * H, :]
    heads = lambda ap: ap.rearrange("p (h c) -> p h c", h=H)
    bank = lambda b: k.psum[:, b, :]
    per_head = lambda ap: over(ap, 2, GD)
    V_STAGES, A_STAGES = (1, 2, 3, 4, 5, 6, 7, 8), (1, 2, 4, 5, 6, 7, 9)

    def reached(stages, m, t):
        return NT * sum(1 for x in stages if x < m) + t + 1

    with nc.Block(no_gpsimd_drain=True) as block:
        @block.sync
        def _(sp):
            load_early_experts(sp, k, d, 0, x, lambda e: sp.wait_ge(s.z_psum, 1))

        @block.tensor
        def _(pe):
            for i in range(3):
                for t in range(NT):
                    for h in range(H):
                        last = nc.tensor.transpose(k.psum[:, 2 + 2 * i + t, h * P:(h + 1) * P],
                                                   e.gT[:, i * H + h, t * P:(t + 1) * P], k.ident[:])
                    last.then_inc(s.nat_psum, 1)
            for kk in range(KD):
                last = nc.tensor.matmul(bank(1), k.xT[:, kk, P:], columns_of(k, 0)[:, kk, :], start=kk == 0, stop=kk == KD - 1)
            last.then_inc(s.z_psum, 1)
            pe.wait_ge(s.gates, 1)
            for t in range(NT):
                nc.tensor.matmul(k.psum[:, 0, t * H:(t + 1) * H], k.upto[:], w.g[:, t, :], start=True, stop=True)
                last = nc.tensor.matmul(k.psum[:, 0, (NT + t) * H:(NT + t + 1) * H], k.ones[:], w.g[:, t, :],
                                        start=True, stop=True)
            last.then_inc(s.cum_psum, 1)
            pe.wait_ge(s.wide, 1)
            pe.wait_ge(s.cum, 1)
            pe.wait_ge(s.z, 1)
            for t in range(NT):
                for h in range(H):
                    last = nc.tensor.matmul(k.psum[:, 1 - t, h * P:(h + 1) * P], wide[:, t, h * P:(h + 1) * P], k.upto[:],
                                            start=True, stop=True)
                last.then_inc(s.cumrow, 1)
            pe.wait_ge(s.nat, 6)
            for i, src in enumerate((q, kk_, kb)):
                pe.wait_ge(s.scaled, i + 1)
                for t in range(NT):
                    for h in range(H):
                        last = nc.tensor.transpose(k.psum[:, 2 + 2 * i + t, h * P:(h + 1) * P],
                                                   src[:, t, h * P:(h + 1) * P], k.ident[:])
                    last.then_inc(s.T_psum, 1)
            pe.wait_ge(s.extra, 1)
            pe.wait_ge(s.decay_in, NT)
            for h in range(H):
                last = nc.tensor.transpose(k.psum[:, 0, h * P:(h + 1) * P], qg1[:, h * P:(h + 1) * P], k.ident[:])
            last.then_inc(s.T_psum, 1)
            pe.wait_ge(s.T_a, 4)
            pe.wait_ge(s.T_v, 3)
            for t in range(NT):
                tok = slice(t * P, (t + 1) * P)
                for i, (lhs, rhs) in enumerate(((kT, qT), (kT, kbT), (kbT, kT))):
                    for h in range(H):
                        last = nc.tensor.matmul(k.psum[:, 4 * t + 1 + i, h * P:(h + 1) * P], lhs[:, h, tok], rhs[:, h, tok],
                                                start=True, stop=True)
                last.then_inc(s.pair_psum, 1)

            def mm(t, b, left_t, right):
                for h in range(H):
                    cols = slice(h * P, (h + 1) * P)
                    last = nc.tensor.matmul(k.psum[:, 4 * t + b, cols], left_t[:, t, cols], right[:, t, cols], start=True, stop=True)
                return last

            def turn(t, b, m):
                for h in range(H):
                    cols = slice(h * P, (h + 1) * P)
                    nc.tensor.transpose(k.psum[:, 4 * t + b, cols], m[:, t, cols], k.ident[:])

            def product(m, t):
                if m == 1:
                    mm(t, 0, B, A)
                    return mm(t, 1, A, B)
                if m == 2:
                    mm(t, 2, B, A)
                    return mm(t, 3, A, Z)
                if m == 3:
                    return mm(t, 0, B, Z)
                if m == 4:
                    turn(t, 1, Z)
                    mm(t, 2, Lo, Z)
                    return mm(t, 3, Z, Lo)
                if m == 5:
                    mm(t, 0, Cm, B)
                    return mm(t, 1, B, Cm)
                if m == 6:
                    mm(t, 2, Cm, B)
                    mm(t, 3, B, Cm)
                    return mm(t, 0, B, Z)
                if m == 7:
                    mm(t, 1, Cm, B)
                    return mm(t, 2, B, Z)
                if m == 8:
                    return mm(t, 3, B, Z)
                return mm(t, 0, A, Z)

            for m in range(1, 10):
                for t in range(NT):
                    if m == 1:
                        pe.wait_ge(s.lower, t + 1)
                    else:
                        pe.wait_ge(s.sub_v, reached(V_STAGES, m - 1, t))
                        pe.wait_ge(s.sub_a, reached(A_STAGES, m - 1, t) if m - 1 in A_STAGES else reached(A_STAGES, m - 2, t))
                    product(m, t).then_inc(s.prod, 1)

            pe.wait_ge(s.sub_a, reached(A_STAGES, 9, 1))
            for h in range(H):
                cols = slice(h * P, (h + 1) * P)
                last = nc.tensor.matmul(k.psum[:, 1, cols], B[:, 0, cols], v[:, 0, cols], start=True, stop=True)
            last.then_inc(s.v0, 1)
            pe.wait_ge(s.extra, 2)
            for h in range(H):
                cols = slice(h * P, (h + 1) * P)
                last = nc.tensor.matmul(k.psum[:, 5, cols], kbg1[:, cols], B[:, 1, cols], start=True, stop=True)
            last.then_inc(s.w1, 1)
            pe.wait_ge(k.s_out_w, 64)
            output_product(nc, k, 0, 0, ATTENTION, begin=True)
            pe.wait_ge(s.vn0, 1)
            for h in range(H):
                cols = slice(h * P, (h + 1) * P)
                last = nc.tensor.matmul(k.psum[:, 2, cols], kg0[:, cols], vn[:, 0, cols], start=True, stop=True)
            last.then_inc(s.st_psum, 1)
            for h in range(H):
                cols = slice(h * P, (h + 1) * P)
                last = nc.tensor.matmul(k.psum[:, 3, cols], AT[:, 0, cols], vn[:, 0, cols], start=True, stop=True)
            last.then_inc(s.o0, 1)
            output_product(nc, k, 0, 1, ATTENTION, begin=True)
            pe.wait_ge(s.st, 1)
            pe.wait_ge(s.nw1, 1)
            for h in range(H):
                cols = slice(h * P, (h + 1) * P)
                nc.tensor.matmul(k.psum[:, 6, cols], B[:, 1, cols], v[:, 1, cols], start=True, stop=False)
                last = nc.tensor.matmul(k.psum[:, 6, cols], nw1[:, cols], st[:, cols], start=False, stop=True)
            last.then_inc(s.vn1_psum, 1)
            output_product(nc, k, 1, 0, ATTENTION, begin=True)
            pe.wait_ge(s.vn1, 1)
            for h in range(H):
                cols = slice(h * P, (h + 1) * P)
                nc.tensor.matmul(k.psum[:, 7, cols], qgT1[:, h, :], st[:, cols], start=True, stop=False)
                last = nc.tensor.matmul(k.psum[:, 7, cols], AT[:, 1, cols], vn[:, 1, cols], start=False, stop=True)
            last.then_inc(s.o1, 1)
            pe.wait_ge(s.o_sb, 1)
            output_product(nc, k, 1, 1, ATTENTION, begin=True)
            for t in range(NT):
                pe.wait_ge(s.on, t + 1)
                for h in range(H):
                    last = nc.tensor.transpose(k.psum[:, 4 + t, h * P:(h + 1) * P], o[:, t, h * P:(h + 1) * P], k.ident[:])
                last.then_inc(s.onT, 1)

        @block.scalar
        def _(act):
            act.wait_ge(k.s_gdn_w, 48)
            nc.scalar.activation(ea[:], e.a_log[:], ACT.Exp).then_inc(s.alog, 1)
            nc.scalar.activation(w.tb, beta, ACT.Exp, scale=-1.0).then_inc(s.beta_exp, 1)
            log1p_exp_scalar(nc, act, s, w)
            for i in range(6):
                act.wait_ge(s.nat_psum, i + 1)
                nc.scalar.copy((q, kk_, v)[i // 2][:, i % 2, :], bank(2 + i)).then_inc(s.nat, 1)
            act.wait_ge(s.nat, 2)
            for t in range(NT):
                for h in range(H):
                    cols = slice(h * P, (h + 1) * P)
                    last = nc.scalar.activation(A[:, t, cols], q[:, t, cols], ACT.Square, accum_out=ssq[:, 0, t, h:h + 1])
            last.then_inc(s.ssq, 1)
            act.wait_ge(s.z_psum, 1)
            nc.scalar.copy(e.z[:, 1, :], bank(1)).then_inc(s.z, 1)
            act.wait_ge(s.ssq, 2)
            nc.scalar.activation(rs[:].rearrange("p a t h -> p (a t h)"), ssq[:].rearrange("p a t h -> p (a t h)"),
                                 ACT.Sqrt, bias=k.eps[:, 0:1]).then_inc(s.root, 1)
            act.wait_ge(s.cum, 1)
            nc.scalar.activation(w.e_cum, w.cum, ACT.Exp).then_inc(s.exps, 1)
            nc.scalar.activation(w.e_left, w.last, ACT.Exp).then_inc(s.exps, 1)
            for t in range(NT):
                act.wait_ge(s.decay_in, t + 1)
                nc.scalar.activation(D_t[:, t, :], D_t[:, t, :], ACT.Exp).then_inc(s.decay, 1)
                nc.scalar.activation(Dn[:, t, :], Dn[:, t, :], ACT.Exp, scale=-1.0).then_inc(s.decay, 1)
            for i in (0, 2):
                for t in range(NT):
                    act.wait_ge(s.T_psum, 2 * i + t + 1)
                    nc.scalar.copy((qT, kT, kbT)[i][:, :, t * P:(t + 1) * P], heads(bank(2 + 2 * i + t))).then_inc(s.T_a, 1)
            for m in A_STAGES:
                for t in range(NT):
                    act.wait_ge(s.prod, NT * (m - 1) + t + 1)
                    moves = {1: [(A, 0)], 2: [(B, 2)], 4: [(A, 1), (B, 3)], 5: [(B, 0)], 6: [(B, 2), (Cm, 3)], 7: [(B, 1)],
                             9: [(B, 0)]}[m]
                    for to, b in moves:
                        last = nc.scalar.copy(to[:, t, :], bank(4 * t + b))
                    last.then_inc(s.sub_a, 1)
            for t in range(NT):
                nc.scalar.activation(e.z[:, t, :], e.z[:, t, :], ACT.Silu).then_inc(s.z, 1)
            act.wait_ge(s.w1, 1)
            nc.scalar.mul(nw1[:], bank(5), -1.0).then_inc(s.nw1, 1)
            act.wait_ge(s.st_psum, 1)
            nc.scalar.copy(st[:], bank(2)).then_inc(s.st, 1)
            for t in range(NT):
                act.wait_ge((s.o0, s.o1)[t], 1)
                nc.scalar.copy(o[:, t, :], bank(3 + 4 * t)).then_inc(s.o_sb, 1)
                act.wait_ge(s.ssq_o, t + 1)
                nc.scalar.activation(rs[:, 0, t, :], ssq[:, 0, t, :], ACT.Sqrt, bias=k.eps[:, 0:1], scale=1.0 / GD).then_inc(s.root_o, 1)
            for t in range(NT):
                act.wait_ge(s.onT, t + 1)
                nc.scalar.copy(k.mixT[:, 4:8, t * P:(t + 1) * P], heads(bank(4 + t))).then_inc(s.mixed, 1)

        @block.gpsimd
        def _(pool):
            pool.wait_ge(s.gates, 1)
            nc.gpsimd.tensor_copy(wide[:].rearrange("p t (h c) -> p (t h) c", h=H),
                                  over(w.g.rearrange("p t h -> p (t h)"), 2, GD)).then_inc(s.wide, 1)
            pool.wait_ge(s.nat, 6)
            pool.wait_ge(s.gates, 1)
            for t in range(NT):
                last = nc.gpsimd.tensor_tensor(heads(v[:, t, :]), heads(v[:, t, :]), per_head(w.beta[:, t, :]), ALU.mult)
            pool.wait_ge(s.scaled, 3)
            pool.wait_ge(s.exps, 2)
            nc.gpsimd.tensor_tensor(heads(qg1[:]), heads(q[:, 1, :]), per_head(w.e_cum[:, 1, :]), ALU.mult).then_inc(s.extra, 1)
            nc.gpsimd.tensor_tensor(heads(kg0[:]), heads(kk_[:, 0, :]), per_head(w.e_left[:, 0, :]), ALU.mult)
            nc.gpsimd.tensor_tensor(heads(kbg1[:]), heads(kb[:, 1, :]), per_head(w.e_cum[:, 1, :]), ALU.mult).then_inc(s.extra, 1)

        @block.vector
        def _(dve):
            step = Chain(dve, s.vec)
            step(nc.vector.tensor_tensor(blk[:], k.block8[:], k.upto[:], ALU.mult))
            step(nc.vector.tensor_tensor(blk[:], blk[:], k.ident[:], ALU.subtract))
            dve.wait_ge(s.beta_exp, 1)
            step(nc.vector.tensor_scalar(w.tb, w.tb, 1.0, None, ALU.add))
            step(nc.vector.reciprocal(w.beta, w.tb))
            dve.wait_ge(k.s_gdn_w, 48)
            step(nc.vector.tensor_tensor(w.x, decay, over(e.dt_bias[:], 1, NT), ALU.add))
            log1p_exp_vector(nc, dve, step, s, w.x, w.lp, w)
            step(nc.vector.scalar_tensor_tensor(w.g, w.x, 0.0, w.lp, ALU.max, ALU.add))
            dve.wait_ge(s.alog, 1)
            for t in range(NT):
                step(nc.vector.scalar_tensor_tensor(w.g[:, t, :], w.g[:, t, :], -1.0, ea[:], ALU.mult, ALU.mult))
            nc.vector.engine_nop().then_inc(s.gates, 1)
            dve.wait_ge(s.nat, 4)
            for t in range(NT):
                step(nc.vector.tensor_tensor(B[:, t, :], kk_[:, t, :], kk_[:, t, :], ALU.mult))
                step(nc.vector.tensor_reduce(ssq[:, 1, t, :], heads(B[:, t, :]), AX.X, ALU.add))
            nc.vector.engine_nop().then_inc(s.ssq, 1)
            dve.wait_ge(s.cum_psum, 1)
            step(nc.vector.tensor_copy(w.cum.rearrange("p t h -> p (t h)"), k.psum[:, 0, 0:NT * H]))
            step(nc.vector.tensor_tensor(w.last.rearrange("p t h -> p (t h)"), k.psum[:, 0, NT * H:2 * NT * H],
                                         w.cum.rearrange("p t h -> p (t h)"), ALU.subtract))
            nc.vector.engine_nop().then_inc(s.cum, 1)
            dve.wait_ge(s.root, 1)
            step(nc.vector.reciprocal(rs[:].rearrange("p a t h -> p (a t h)"), rs[:].rearrange("p a t h -> p (a t h)")))
            for t in range(NT):
                step(nc.vector.scalar_tensor_tensor(heads(q[:, t, :]), heads(q[:, t, :]), float(GD ** -0.5),
                                                    per_head(rs[:, 0, t, :]), ALU.mult, ALU.mult))
            nc.vector.engine_nop().then_inc(s.scaled, 1)
            for t in range(NT):
                step(nc.vector.tensor_tensor(heads(kk_[:, t, :]), heads(kk_[:, t, :]), per_head(rs[:, 1, t, :]), ALU.mult))
            nc.vector.engine_nop().then_inc(s.scaled, 1)
            for t in range(NT):
                step(nc.vector.tensor_tensor(heads(kb[:, t, :]), heads(kk_[:, t, :]), per_head(w.beta[:, t, :]), ALU.mult))
            nc.vector.engine_nop().then_inc(s.scaled, 1)
            for t in range(NT):
                dve.wait_ge(s.cumrow, t + 1)
                for h in range(H):
                    cols = slice(h * P, (h + 1) * P)
                    nc.vector.scalar_tensor_tensor(D_t[:, t, cols], k.psum[:, 1 - t, cols], w.cum[:, t, h:h + 1],
                                                   k.no_later_T[:], ALU.subtract, ALU.add)
                    last = nc.vector.scalar_tensor_tensor(Dn[:, t, cols], k.psum[:, 1 - t, cols], w.cum[:, t, h:h + 1],
                                                          k.off_strict[:], ALU.subtract, ALU.add)
                last.then_inc(s.decay_in, 1)
            for t in range(NT):
                dve.wait_ge(s.T_psum, 2 + t + 1)
                nc.vector.tensor_copy(kT[:, :, t * P:(t + 1) * P], heads(bank(4 + t))).then_inc(s.T_v, 1)
            dve.wait_ge(s.T_psum, 7)
            nc.vector.tensor_copy(qgT1[:], heads(bank(0))).then_inc(s.T_v, 1)
            dve.wait_ge(s.decay, 2 * NT)
            blocks, blocks_t = over(k.block8[:], 1, H), over(blk[:], 1, H)
            one = over(k.ident[:], 1, H)
            for t in range(NT):
                dve.wait_ge(s.pair_psum, t + 1)
                step(nc.vector.tensor_tensor(AT[:, t, :], bank(4 * t + 1), D_t[:, t, :], ALU.mult))
                step(nc.vector.tensor_tensor(B[:, t, :], bank(4 * t + 2), D_t[:, t, :], ALU.mult))
                step(nc.vector.tensor_tensor(heads(B[:, t, :]), heads(B[:, t, :]), blocks_t, ALU.mult))
                step(nc.vector.tensor_tensor(Lo[:, t, :], bank(4 * t + 3), Dn[:, t, :], ALU.mult))
                step(nc.vector.tensor_tensor(heads(A[:, t, :]), heads(Lo[:, t, :]), blocks, ALU.mult))
                step(nc.vector.tensor_tensor(Lo[:, t, :], Lo[:, t, :], A[:, t, :], ALU.subtract))
                step(nc.vector.tensor_tensor(heads(Z[:, t, :]), one, heads(B[:, t, :]), ALU.subtract))
                nc.vector.engine_nop().then_inc(s.lower, 1)
            for m in V_STAGES:
                for t in range(NT):
                    dve.wait_ge(s.prod, NT * (m - 1) + t + 1)
                    if m == 4:
                        step(nc.vector.tensor_copy(Cm[:, t, :], bank(4 * t + 2)))
                        last = nc.vector.tensor_tensor(heads(Z[:, t, :]), one, heads(Cm[:, t, :]), ALU.subtract)
                    elif m in (1, 5):
                        last = nc.vector.tensor_copy((B if m == 1 else Cm)[:, t, :], bank(4 * t + 1))
                    else:
                        b = {2: 3, 3: 0, 6: 0, 7: 2, 8: 3}[m]
                        last = nc.vector.tensor_tensor(Z[:, t, :], Z[:, t, :], bank(4 * t + b), ALU.add)
                    last.then_inc(s.sub_v, 1)
            dve.wait_ge(s.v0, 1)
            nc.vector.tensor_copy(vn[:, 0, :], bank(1)).then_inc(s.vn0, 1)
            dve.wait_ge(s.vn1_psum, 1)
            nc.vector.tensor_copy(vn[:, 1, :], bank(6)).then_inc(s.vn1, 1)
            for t in range(NT):
                dve.wait_ge(s.o_sb, t + 1)
                step(nc.vector.tensor_tensor(wide[:, t, :], o[:, t, :], o[:, t, :], ALU.mult))
                step(nc.vector.tensor_reduce(ssq[:, 0, t, :], heads(wide[:, t, :]), AX.X, ALU.add))
                nc.vector.engine_nop().then_inc(s.ssq_o, 1)
                dve.wait_ge(s.z, 1 + NT)
                dve.wait_ge(s.root_o, t + 1)
                step(nc.vector.reciprocal(rs[:, 0, t, :], rs[:, 0, t, :]))
                step(nc.vector.tensor_tensor(heads(o[:, t, :]), heads(o[:, t, :]), per_head(rs[:, 0, t, :]), ALU.mult))
                step(nc.vector.tensor_tensor(heads(o[:, t, :]), heads(o[:, t, :]), over(e.o_gain[:], 1, H), ALU.mult))
                step(nc.vector.tensor_tensor(o[:, t, :], o[:, t, :], e.z[:, t, :], ALU.mult))
                nc.vector.engine_nop().then_inc(s.on, 1)
    ctx.close()


def output_product(nc, k, t, half, chunks, begin):
    for c in chunks:
        last = nc.tensor.matmul(k.psum[:, 2 * t + half, :], k.mixT[:, c, t * P:(t + 1) * P], columns_of(k, 2 + half)[:, c, :],
                                start=begin and c == chunks[0], stop=True, skip_group_check=True)
    return last


def mixer_output(nc, k, d, layer, x, chunks):
    ctx = ExitStack()
    s = semaphores(ctx, nc, f"out{layer}", "vec mixed variance root rstd centred normed eps")
    ln = named(**layer_norm_tiles(lambda n, sh, dt=F32: ctx.enter_context(nc.sbuf_tensor(f"out{layer}_{n}", sh, dt))))
    with nc.Block(no_gpsimd_drain=True) as block:
        @block.sync
        def _(sp):
            sp.wait_ge(s.mixed, 2 * NT)
            load_up(sp, k, d, layer, 2, 2, x.gu1)

        @block.tensor
        def _(pe):
            for t in range(NT):
                for half in range(2):
                    output_product(nc, k, t, half, chunks, begin=False).then_inc(s.mixed, 1)

        @block.scalar
        def _(act):
            act.wait_ge(s.eps, 1)
            layer_norm_scalar(nc, act, s, ln)

        @block.vector
        def _(dve):
            step = Chain(dve, s.vec)
            nc.vector.memset(ln.ln_eps[:], LN_EPS).then_inc(s.eps, 1)
            layer_norm_vector(nc, dve, step, s, k, ln, s.mixed, together=False)
    ctx.close()


def even_shared(ctx, nc, k):
    def sb(name, shape, dt=F32):
        return ctx.enter_context(nc.sbuf_tensor(f"ev_{name}", shape, dt))

    e = named()
    e.lat = sb("lat", [P, NT, EV_LAT + 2 * GH])
    e.cols = sb("cols", [P, CONV_W * G_CHUNKS + 3])
    e.gT = sb("gT", [P, G_CHUNKS, S])
    e.z = sb("z", [P, NT, GH * GD])
    e.o_gain = sb("o_gain", [P, GD])
    e.a_log = sb("a_log", [P, GH])
    e.dt_bias = sb("dt_bias", [P, GH])
    w = semaphores(ctx, nc, "even", "mla_weights gv_weights z_weights out_weights gdn_small_weights")
    k.s_mla_w, k.s_gv_w, k.s_z_w, k.s_out_w, k.s_gdn_w = w.mla_weights, w.gv_weights, w.z_weights, w.out_weights, w.gdn_small_weights
    return e



OD_K = LH * LK
OD_V = 2 * OD_K
OD_GATES = OD_V + LH * LV
OD_O = OD_GATES + 2 * LH
OD_SQ = OD_O + LH * LV
OD_SK = OD_SQ + WH * WD
OD_END = OD_SK + 2 * WKV * WD
MEMORY, WINDOWED = range(0, 4), range(4, 8)


def odd_shared(ctx, nc, k):
    def sb(name, shape, dt=F32):
        return ctx.enter_context(nc.sbuf_tensor(f"od_{name}", shape, dt))

    e = named()
    e.mqT = sb("mqT", [P, 2, S])
    e.mkT = sb("mkT", [P, LH, S])
    e.v1 = sb("v1", [P, NT, LH, LV + 1])
    e.gate_o = sb("gate_o", [P, NT, LH * LV])
    e.m_gain = sb("m_gain", [P, LH * LV])
    e.rows = {n: sb(n, [LH, S]) for n in ("decay", "rest", "stab")}
    e.sq = sb("sq", [P, NT, WH, WD])
    e.sk = sb("sk", [P, NT, WKV, 2, 2, WD])
    e.sv = sb("sv", [P, NT, WKV, WD])
    e.sinks = sb("sinks", [P, WH])
    e.window = sb("window", [P, 2 * P])
    w = semaphores(ctx, nc, "odd", "v_weights o_weights out_weights small_weights")
    k.s_odd_v_w, k.s_odd_o_w, k.s_odd_out_w, k.s_odd_small = w.v_weights, w.o_weights, w.out_weights, w.small_weights
    return e


def odd_kv_weights(k):
    return k.w_down[0][:].rearrange("p j n -> p (j n)").rearrange("p (k n) -> p k n", k=KD)


def odd_first_loads(sp, k, d, first, s):
    win = d.od_w_in[0].rearrange("(p k) n -> p k n", k=KD)
    sp.dma_start(k.gates_w[:], win[:, :, OD_GATES:OD_O]).then_inc(first.gates_w, 16)
    for i, src in enumerate((d.mlstm_b_i, d.mlstm_b_f)):
        sp.dma_start(k.gate_bias[:, i:i + 1], src.rearrange("o h -> h o")).then_inc(first.gates_w, 16)
    sp.wait_ge(s.up, PAIRS - 1)
    sp.dma_start(columns_of(k, 1), win[:, :, OD_SQ:OD_SK]).then_inc(first.sq_w, 16)
    sp.dma_start(columns_of(k, 0), win[:, :, 0:OD_V]).then_inc(first.qk_w, 16)
    sp.wait_ge(s.down_b, PAIRS - 1)
    sp.dma_start(odd_kv_weights(k), win[:, :, OD_SK:OD_END]).then_inc(first.kv_w, 16)


def natural(nc, k, weights, places, sem):
    for t in range(NT):
        for kk in range(KD):
            last = nc.tensor.matmul(places[t], k.xT[:, kk, t * P:(t + 1) * P], weights[:, kk, :],
                                    start=kk == 0, stop=kk == KD - 1)
        last.then_inc(sem, 1)


def odd_project(nc, k, d, e, first):
    ctx = ExitStack()
    s = semaphores(ctx, nc, "odp", "xT_psum xT vec gates_psum gates_read mq_psum mk_psum mqT mkT "
                                   "skv_psum skv sq_psum sq zeros pool mag exp_mag one_more log_u")

    def sb(name, shape, dt=F32):
        return ctx.enter_context(nc.sbuf_tensor(f"odp_{name}", shape, dt))

    wg, bias = k.gates_w, k.gate_bias
    raw_i, raw_f, lp, run, off = (sb(n, [LH, S]) for n in ("raw_i", "raw_f", "lp", "run", "none"))
    w = named(**{n: sb(n, [LH, S])[:] for n in ("mag", "t", "u", "d", "tiny", "log")})
    sk_raw = sb("sk_raw", [P, NT, WKV, WD])
    tmp = [sb(f"tmp{i}", [P, WH, WD // 2]) for i in range(4)]
    win = d.od_w_in[0].rearrange("(p k) n -> p k n", k=KD)

    with nc.Block(no_gpsimd_drain=True) as block:
        @block.sync
        def _(sp):
            sp.dma_start(columns_of(k, 2), win[:, :, OD_V:OD_GATES]).then_inc(k.s_odd_v_w, 16)
            sp.dma_start(columns_of(k, 3), win[:, :, OD_O:OD_SQ]).then_inc(k.s_odd_o_w, 16)
            sp.dma_start(e.m_gain[:], d.mlstm_norm.to_broadcast([P, LH * LV])).then_inc(k.s_odd_small, 16)
            sp.dma_start(e.sinks[:], d.swa_sinks.to_broadcast([P, WH])).then_inc(k.s_odd_small, 16)
            for i, src in enumerate((d.ln1_g, d.ln1_b)):
                sp.dma_start(k.ln[:, i, :], src[1:2].to_broadcast([P, D])).then_inc(k.s_odd_out_w, 16)

        @block.gpsimd
        def _(pool):
            nc.gpsimd.memset(e.mkT[:], 0.0).then_inc(s.zeros, 1)
            nc.gpsimd.memset(e.sk[:], 0.0).then_inc(s.zeros, 1)
            nc.gpsimd.memset(e.v1[:, :, :, LV:], 1.0).then_inc(s.zeros, 1)
            nc.gpsimd.memset(e.window[:], 0.0).then_inc(s.zeros, 1)
            pool.wait_ge(s.zeros, 4)
            nc.gpsimd.affine_select(out=e.window[:, 0:P], in_=e.window[:, 0:P], pattern=[[1, P]],
                                    compare_op=ALU.is_gt, fill=NEG, base=0, channel_multiplier=-1).then_inc(s.pool, 1)
            nc.gpsimd.affine_select(out=e.window[:, P:], in_=e.window[:, P:], pattern=[[-1, P]],
                                    compare_op=ALU.is_ge, fill=NEG, base=0, channel_multiplier=1).then_inc(s.pool, 1)
            pool.wait_ge(s.pool, 2)

        @block.tensor
        def _(pe):
            transpose_x_tensor(nc, pe, s, k)
            pe.wait_ge(s.xT, KD // 2)
            pe.wait_ge(first.gates_w, 48)
            for i in range(2):
                for kk in range(KD):
                    last = nc.tensor.matmul(k.psum[0:LH, 4, i * S:(i + 1) * S], wg[:, kk, i * LH:(i + 1) * LH], k.xT[:, kk, :],
                                            start=kk == 0, stop=kk == KD - 1)
            last.then_inc(s.gates_psum, 1)
            pe.wait_ge(first.kv_w, 16)
            natural(nc, k, odd_kv_weights(k), (k.psum[:, 7, 0:S], k.psum[:, 7, S:2 * S]), s.skv_psum)
            pe.wait_ge(first.sq_w, 16)
            natural(nc, k, columns_of(k, 1), (k.psum[:, 0, :], k.psum[:, 1, :]), s.sq_psum)
            pe.wait_ge(first.qk_w, 16)
            for i, sem in enumerate((s.mq_psum, s.mk_psum)):
                w0 = columns_of(k, 0)
                for c in range(2):
                    for kk in range(KD):
                        last = nc.tensor.matmul(k.psum[:, 5 + i, c * S:(c + 1) * S],
                                                w0[:, kk, i * OD_K + c * P:i * OD_K + (c + 1) * P], k.xT[:, kk, :],
                                                start=kk == 0, stop=kk == KD - 1)
                last.then_inc(sem, 1)

        @block.scalar
        def _(act):
            transpose_x_scalar(nc, act, s, k)
            log1p_exp_scalar(nc, act, s, w)
            act.wait_ge(s.skv_psum, NT)
            both = k.psum[:, 7, :].rearrange("p (t c) -> p t c", t=NT)
            nc.scalar.copy(sk_raw[:].rearrange("p t g c -> p t (g c)"), both[:, :, 0:WKV * WD]).then_inc(s.skv, 1)
            nc.scalar.copy(e.sv[:].rearrange("p t g c -> p t (g c)"), both[:, :, WKV * WD:]).then_inc(s.skv, 1)
            for t in range(NT):
                act.wait_ge(s.sq_psum, t + 1)
                nc.scalar.copy(e.sq[:, t, :, :].rearrange("p h c -> p (h c)"), k.psum[:, t, :]).then_inc(s.sq, 1)
            act.wait_ge(s.mq_psum, 1)
            nc.scalar.copy(flat(e.mqT[:]), k.psum[:, 5, :]).then_inc(s.mqT, 1)
            act.wait_ge(s.zeros, 4)
            act.wait_ge(s.mk_psum, 1)
            for h in range(LH):
                part = slice((h % 2) * LK, (h % 2 + 1) * LK)
                nc.scalar.mul(e.mkT[part, h, :], k.psum[part, 6, (h // 2) * S:(h // 2 + 1) * S], float(LK ** -0.5)).then_inc(s.mkT, 1)

        @block.vector
        def _(dve):
            step = Chain(dve, s.vec)
            step(nc.vector.memset(off[:], 0.0))
            dve.wait_ge(s.gates_psum, 1)
            dve.wait_ge(first.gates_w, 48)
            step(nc.vector.tensor_scalar(raw_i[:], k.psum[0:LH, 4, 0:S], bias[:, 0:1], None, ALU.add))
            step(nc.vector.tensor_scalar(raw_f[:], k.psum[0:LH, 4, S:2 * S], bias[:, 1:2], None, ALU.add))
            nc.vector.engine_nop().then_inc(s.gates_read, 1)
            log1p_exp_vector(nc, dve, step, s, raw_f[:], lp[:], w)
            step(nc.vector.scalar_tensor_tensor(raw_f[:], raw_f[:], 0.0, lp[:], ALU.min, ALU.subtract))
            step(nc.vector.tensor_tensor_scan(run[:], raw_f[:], off[:], 0.0, ALU.add, ALU.add))
            step(nc.vector.tensor_tensor_scan(e.rows["stab"][:], raw_f[:], raw_i[:], 0.0, ALU.add, ALU.max))
            step(nc.vector.tensor_tensor(e.rows["decay"][:], run[:], e.rows["stab"][:], ALU.subtract))
            step(nc.vector.tensor_tensor(e.rows["rest"][:], raw_i[:], run[:], ALU.subtract))
            half = WD // 2
            own = slice(MLA_R // 2, None)
            dve.wait_ge(s.zeros, 4)
            dve.wait_ge(s.skv, 1)
            for t in range(NT):
                rope(nc, step, tmp, sk_raw[:, t, :, 0:half], sk_raw[:, t, :, half:], e.sk[:, t, :, 0, 0, 0:half],
                     e.sk[:, t, :, 0, 0, half:], k.cos[:, t, own], k.sin[:, t, own])
                step(nc.vector.tensor_copy(e.sk[:, t, :, 1, 1, :], e.sk[:, t, :, 0, 0, :]))
            for t in range(NT):
                dve.wait_ge(s.sq, t + 1)
                q1, q2 = e.sq[:, t, :, 0:half], e.sq[:, t, :, half:]
                rope(nc, step, tmp, q1, q2, q1, q2, k.cos[:, t, own], k.sin[:, t, own])
    ctx.close()


def odd_memory(nc, k, e):
    ctx = ExitStack()
    s = semaphores(ctx, nc, "mem", "vec sel wide_psum cols_psum cols neg_m qk_psum exps_in exps pairs out_psum num "
                                   "ssq root normed turned mixed")

    def sb(name, shape, dt=F32):
        return ctx.enter_context(nc.sbuf_tensor(f"mem_{name}", shape, dt))

    H, C = LH, LH * LV
    sel = sb("head_rows", [H, H, P])
    cols = sb("cols", [P, 2 * NT, H])
    floor = sb("floor", [P, NT, H])
    ex = sb("exps", [P, H, S + P])
    w = sb("weights", [P, H, S + P])
    num = sb("num", [P, NT, H, LV + 1])
    den = sb("den", [P, NT, H])
    rden = sb("rden", [P, NT, H])
    o = sb("out", [P, NT, C])
    sq = sb("squares", [P, NT, C])
    ssq = sb("ssq", [P, NT, H])
    root = sb("root", [P, NT, H])
    heads = lambda ap: ap.rearrange("p (h c) -> p h c", h=H)
    wide = lambda h: k.psum[:, 4 + h // 2, (h % 2) * S:(h % 2 + 1) * S]

    with nc.Block(no_gpsimd_drain=True) as block:
        @block.tensor
        def _(pe):
            for i, r in enumerate(("rest", "stab")):
                for t in range(NT):
                    last = nc.tensor.transpose(k.psum[:, 6, (NT * i + t) * H:(NT * i + t + 1) * H],
                                               e.rows[r][:, t * P:(t + 1) * P], k.ident[0:H, 0:H])
            last.then_inc(s.cols_psum, 1)
            pe.wait_ge(s.sel, 1)
            for h in range(H):
                last = nc.tensor.matmul(wide(h), sel[:, h, :], e.rows["decay"][:], start=True, stop=True)
            last.then_inc(s.wide_psum, 1)
            for h in range(H):
                nc.tensor.matmul(k.psum[:, h, 0:S], e.mkT[:, h, 0:P], e.mqT[:, h // 2, :], start=True, stop=True)
                nc.tensor.matmul(k.psum[:, h, S:S + P], e.mkT[:, h, P:], e.mqT[:, h // 2, P:], start=True,
                                 stop=True).then_inc(s.qk_psum, 1)
            pe.wait_ge(s.pairs, H)
            for t in range(NT):
                for h in range(H):
                    place = k.psum[:, 4 + 2 * t + h // 2, (h % 2) * (LV + 1):(h % 2 + 1) * (LV + 1)]
                    for kt in range(t + 1):
                        first = S if kt else t * P
                        last = nc.tensor.matmul(place, w[:, h, first:first + P], e.v1[:, kt, h, :], start=kt == 0, stop=kt == t)
                last.then_inc(s.out_psum, 1)
            pe.wait_ge(k.s_odd_out_w, 64)
            for t in range(NT):
                for half in range(2):
                    output_product(nc, k, t, half, WINDOWED, begin=True)
            pe.wait_ge(s.num, 4)
            for t in range(NT):
                pe.wait_ge(s.normed, t + 1)
                for h in range(H):
                    last = nc.tensor.transpose(k.psum[:, 6 + t, h * P:(h + 1) * P], o[:, t, h * P:(h + 1) * P], k.ident[:])
                last.then_inc(s.turned, 1)

        @block.scalar
        def _(act):
            act.wait_ge(s.cols, 1)
            nc.scalar.activation(flat(floor[:]), flat(cols[:, NT:, :]), ACT.Exp, scale=-1.0).then_inc(s.neg_m, 1)
            act.wait_ge(s.exps_in, 1)
            for h in range(H):
                nc.scalar.activation(ex[:, h, P:S], wide(h)[:, P:], ACT.Exp, bias=cols[:, 0, h:h + 1]).then_inc(s.exps, 1)
                nc.scalar.activation(ex[:, h, 0:P], ex[:, h, 0:P], ACT.Exp).then_inc(s.exps, 1)
                nc.scalar.activation(ex[:, h, S:], ex[:, h, S:], ACT.Exp).then_inc(s.exps, 1)
            for t in range(NT):
                act.wait_ge(s.out_psum, t + 1)
                for half in range(2):
                    nc.scalar.copy(num[:, t, 2 * half:2 * half + 2, :].rearrange("p h c -> p (h c)"),
                                   k.psum[:, 4 + 2 * t + half, 0:2 * (LV + 1)]).then_inc(s.num, 1)
            act.wait_ge(s.ssq, 1)
            nc.scalar.activation(flat(root[:]), flat(ssq[:]), ACT.Sqrt, bias=k.eps[:, 0:1], scale=1.0 / LV).then_inc(s.root, 1)
            for t in range(NT):
                act.wait_ge(s.turned, t + 1)
                nc.scalar.copy(k.mixT[:, 0:H, t * P:(t + 1) * P], heads(k.psum[:, 6 + t, :])).then_inc(s.mixed, 1)

        @block.vector
        def _(dve):
            step = Chain(dve, s.vec)
            nc.vector.tensor_copy(sel[:], over(k.ident[0:H, 0:H], 2, P)).then_inc(s.sel, 1)
            dve.wait_ge(s.cols_psum, 1)
            nc.vector.tensor_copy(cols[:].rearrange("p i h -> p (i h)"), k.psum[:, 6, 0:2 * NT * H]).then_inc(s.cols, 1)
            dve.wait_ge(s.cols, 1)
            dve.wait_ge(s.wide_psum, 1)
            for h in range(H):
                for t in range(NT):
                    place = slice(S, S + P) if t else slice(0, P)
                    last = nc.vector.scalar_tensor_tensor(ex[:, h, place], wide(h)[:, t * P:(t + 1) * P], cols[:, t, h:h + 1],
                                                          k.no_later_T[:], ALU.add, ALU.add)
            last.then_inc(s.exps_in, 1)
            for h in range(H):
                dve.wait_ge(s.exps, 3 * h + 3)
                dve.wait_ge(s.qk_psum, h + 1)
                nc.vector.tensor_tensor(w[:, h, :], ex[:, h, :], k.psum[:, h, 0:S + P], ALU.mult).then_inc(s.pairs, 1)
            dve.wait_ge(s.neg_m, 1)
            dve.wait_ge(k.s_odd_small, 32)
            for t in range(NT):
                dve.wait_ge(s.num, 2 * t + 2)
                step(nc.vector.scalar_tensor_tensor(den[:, t, :], num[:, t, :, LV], -1.0, num[:, t, :, LV], ALU.mult, ALU.max))
                step(nc.vector.tensor_tensor(den[:, t, :], den[:, t, :], floor[:, t, :], ALU.max))
                step(nc.vector.reciprocal(rden[:, t, :], den[:, t, :]))
                step(nc.vector.tensor_tensor(heads(o[:, t, :]), num[:, t, :, 0:LV], over(rden[:, t, :], 2, LV), ALU.mult))
                step(nc.vector.tensor_tensor(sq[:, t, :], o[:, t, :], o[:, t, :], ALU.mult))
                step(nc.vector.tensor_reduce(ssq[:, t, :], heads(sq[:, t, :]), AX.X, ALU.add))
            nc.vector.engine_nop().then_inc(s.ssq, 1)
            for t in range(NT):
                step(nc.vector.tensor_tensor(e.gate_o[:, t, :], e.gate_o[:, t, :], e.m_gain[:], ALU.mult))
            dve.wait_ge(s.root, 1)
            step(nc.vector.reciprocal(flat(root[:]), flat(root[:])))
            for t in range(NT):
                step(nc.vector.tensor_tensor(heads(o[:, t, :]), heads(o[:, t, :]), over(root[:, t, :], 2, LV), ALU.mult))
                nc.vector.tensor_tensor(o[:, t, :], o[:, t, :], e.gate_o[:, t, :], ALU.mult).then_inc(s.normed, 1)
    ctx.close()


def odd_window(nc, k, d, e, x):
    ctx = ExitStack()
    s = semaphores(ctx, nc, "win", "v_psum v o_psum o vec qT_psum kT_psum qT kT scores masked max sunk sink_exp probs scaled turned pT mixed done")

    def sb(name, shape, dt=F32):
        return ctx.enter_context(nc.sbuf_tensor(f"win_{name}", shape, dt))

    qT = sb("qT", [P, WH // 2, S])
    kT = sb("kT", [P, WKV, 2, S])
    group = WH // WKV
    a = named(pr=sb("pr", [P, WH, S]), pT=sb("pT", [P, 2, 2, WH // 2 * P]), mx=sb("max", [P, WH]),
                        nb=sb("negmax", [P, WH]), den=sb("den", [P, WH]), dinv=sb("dinv", [P, WH]),
                        sunk=sb("sunk", [P, WH]), scale=float(WD ** -0.5), mask=e.window, sinks=e.sinks, chunk=4,
                        qT=lambda h, t: qT[:, h // 2, t * P:(t + 1) * P],
                        kT=lambda h, keys: kT[:, h // group, h % 2, 0:keys],
                        v=lambda h, kt: e.sv[:, kt, h // group, :])

    with nc.Block(no_gpsimd_drain=True) as block:
        @block.sync
        def _(sp):
            load_early_experts(sp, k, d, 1, x, lambda e: None)
            for half, used in enumerate((s.v_psum, s.o_psum)):
                sp.wait_ge(used, NT)
                sp.dma_start(columns_of(k, 2 + half),
                             d.od_w_out[0][:, half * BANK:(half + 1) * BANK].rearrange("(c p) n -> p c n", p=P)
                             ).then_inc(k.s_odd_out_w, 16)

        @block.tensor
        def _(pe):
            for b in range(2):
                for i in range(2):
                    for t in range(NT):
                        last = nc.tensor.transpose(k.psum[:, b, i * S + t * P:i * S + (t + 1) * P],
                                                   e.sq[:, t, 4 * b + 2 * i:4 * b + 2 * i + 2, :].rearrange("p h c -> p (h c)"), k.ident[:])
                last.then_inc(s.qT_psum, 1)
            for g in range(WKV):
                for i in range(2):
                    for t in range(NT):
                        last = nc.tensor.transpose(k.psum[:, 2 + g, i * S + t * P:i * S + (t + 1) * P],
                                                   e.sk[:, t, g, i, :, :].rearrange("p u c -> p (u c)"), k.ident[:])
                last.then_inc(s.kT_psum, 1)

            def projections(t):
                if t == 0:
                    pe.wait_ge(k.s_odd_v_w, 16)
                    pe.wait_ge(s.qT, 4)
                    pe.wait_ge(s.kT, 4)
                    natural(nc, k, columns_of(k, 2), (k.psum[:, 1, :], k.psum[:, 3, :]), s.v_psum)
                else:
                    pe.wait_ge(k.s_odd_o_w, 16)
                    pe.wait_ge(s.masked, 8)
                    natural(nc, k, columns_of(k, 3), (k.psum[:, 4, :], k.psum[:, 5, :]), s.o_psum)
                    pe.wait_ge(s.v, NT)

            attention_tensor(nc, pe, s, k, a, projections)

        @block.scalar
        def _(act):
            for b in range(2):
                act.wait_ge(s.qT_psum, b + 1)
                nc.scalar.copy(flat(qT[:, 2 * b:2 * b + 2, :]), k.psum[:, b, :]).then_inc(s.qT, 2)

            def projections(t):
                for u in range(NT):
                    if t == 0:
                        act.wait_ge(s.v_psum, u + 1)
                        nc.scalar.copy(e.v1[:, u, :, 0:LV], k.psum[:, 1 + 2 * u, :].rearrange("p (h c) -> p h c", h=LH)).then_inc(s.v, 1)
                    else:
                        act.wait_ge(s.o_psum, u + 1)
                        nc.scalar.activation(e.gate_o[:, u, :], k.psum[:, 4 + u, :], ACT.Sigmoid).then_inc(s.o, 1)

            attention_scalar(nc, act, s, k, a, projections)

        @block.vector
        def _(dve):
            step = Chain(dve, s.vec)
            for g in range(WKV):
                dve.wait_ge(s.kT_psum, g + 1)
                nc.vector.tensor_copy(flat(kT[:, g, :, :]), k.psum[:, 2 + g, :]).then_inc(s.kT, 2)
            dve.wait_ge(k.s_odd_small, 32)
            attention_vector(nc, dve, step, s, k, a)
    ctx.close()



def decoder_trunk(nc, d):
    with ExitStack() as ctx:
        k = persistent(ctx, nc)
        odd_first = semaphores(ctx, nc, "odd_first", "gates_w kv_w sq_w qk_w")
        with ExitStack() as layer:
            x = expert_semaphores(layer, nc, 0)
            with ExitStack() as mixer:
                e = even_shared(mixer, nc, k)
                even_first = semaphores(mixer, nc, "even_first", "x w0")
                constants(nc, k, lambda sp: even_first_loads(sp, k, d, even_first))
                even_project(nc, k, d, e, even_first)
                even_latent_attention(nc, k, d, e)
                even_delta_net(nc, k, d, e, x)
                mixer_output(nc, k, d, 0, x, DELTA)
            moe_layer(nc, k, d, 0, x, fetch_next=lambda sp, s: odd_first_loads(sp, k, d, odd_first, s))
        with ExitStack() as layer:
            x = expert_semaphores(layer, nc, 1)
            with ExitStack() as mixer:
                e = odd_shared(mixer, nc, k)
                odd_project(nc, k, d, e, odd_first)
                odd_window(nc, k, d, e, x)
                odd_memory(nc, k, e)
                mixer_output(nc, k, d, 1, x, MEMORY)
            moe_layer(nc, k, d, 1, x, out=d.out[0])


INPUTS = ("x", "positions", "ev_w_in", "mla_q_norm", "mla_w_qb", "mla_kv_norm", "mla_w_kvb", "gdn_conv", "gdn_a_log",
          "gdn_dt_bias", "gdn_norm", "ev_w_out", "od_w_in", "mlstm_b_i", "mlstm_b_f", "mlstm_norm", "swa_sinks", "od_w_out",
          "ln1_g", "ln1_b", "router_w", "router_b", "moe_w_gate", "moe_w_up", "moe_w_down", "shared_w_gate", "shared_w_up",
          "shared_w_down", "ln2_g", "ln2_b")


def kernel(**inputs):
    import concourse.bacc as bacc
    from concourse.bass_utils import run_bass_kernel_spmd

    nc = bacc.Bacc("TRN2", target_bir_lowering=False, num_devices=1)
    arrays = {f"in_{name}": np.ascontiguousarray(inputs[name]) for name in INPUTS}
    d = named(**{name: nc.dram_tensor(f"in_{name}", list(arrays[f"in_{name}"].shape),
                                                mybir.dt.from_np(arrays[f"in_{name}"].dtype), kind="ExternalInput").ap()
                           for name in INPUTS})
    d.out = nc.dram_tensor("out_x", [1, S, D], F32, kind="ExternalOutput").ap()
    decoder_trunk(nc, d)
    result = run_bass_kernel_spmd(nc, [arrays], core_ids=[0])
    return result.results[0]["out_x"]
```
